# Optimizing a Trainium2 kernel written in Bass

```python
import math
import jax
import jax.numpy as jnp
from jax import lax
import numpy as np

D_MODEL = 1024
BATCH = 1
SEQ = 256
DEPTH = 2

N_BIAS_HEADS = 8
N_BUCKETS = 32
MAX_DISTANCE = 128
Q_BLOCK = 128
NEG = -1e30
EPS = 1e-6

N_HEADS_A = 8
HEAD_DIM_A = 64
MOBA_BLOCK = 256
MOBA_TOPK = 3

LRU_WIDTH = D_MODEL // 2
LRU_BLOCKS = 8
LRU_BLOCK = LRU_WIDTH // LRU_BLOCKS
CONV_WIDTH = 4
LRU_C = 8.0

N_HEADS_C = 8
HEAD_DIM_C = D_MODEL // N_HEADS_C
N_KV_GROUPS = 2
HEADS_PER_GROUP = N_HEADS_C // N_KV_GROUPS
CMP_LEN = 32
CMP_STRIDE = 16
CMP_HIDDEN = 256
SEL_BLOCK = 64
SEL_TOPK = 16
WINDOW = 512
SEL_FORCE = 1e4

D_FF = 4 * D_MODEL

N_EVEN = (DEPTH + 1) // 2
N_ODD = DEPTH // 2

AB_IN = 3 * N_HEADS_A * HEAD_DIM_A + 2 * LRU_WIDTH
AB_OUT = N_HEADS_A * HEAD_DIM_A + LRU_WIDTH
C_KV = N_KV_GROUPS * HEAD_DIM_C
C_IN = N_HEADS_C * HEAD_DIM_C + 6 * C_KV + 3 * N_HEADS_C
C_OUT = N_HEADS_C * HEAD_DIM_C

kernel_name = 'hybrid_moba_rglru_nsa_trunk'

def rmsnorm(x, g):
    xf = x.astype(jnp.float32)
    y = xf * lax.rsqrt(jnp.mean(xf * xf, axis=-1, keepdims=True) + EPS)
    return (y * g.astype(jnp.float32)).astype(x.dtype)

def masked_softmax(s, mask):
    s = jnp.where(mask, s.astype(jnp.float32), NEG)
    e = jnp.exp(s - jnp.max(s, axis=-1, keepdims=True)) * mask
    return e / jnp.maximum(jnp.sum(e, axis=-1, keepdims=True), 1e-30)

def rel_bucket(dist):
    n = jnp.maximum(dist, 0)
    exact = N_BUCKETS // 2
    nf = jnp.maximum(n, 1).astype(jnp.float32)
    large = exact + (jnp.log(nf / exact) / math.log(MAX_DISTANCE / exact)
                     * (N_BUCKETS - exact)).astype(jnp.int32)
    large = jnp.minimum(large, N_BUCKETS - 1)
    return jnp.where(n < exact, n, large)

def bias_shared(table, bucket):
    return table.T[:, bucket].astype(jnp.float32)

def bias_per_head(table, bucket):
    return jax.vmap(lambda tb, bk: tb[bk])(table.T, bucket).astype(jnp.float32)

def bias_per_group(table, bucket):
    tg = table.reshape(N_BUCKETS, N_KV_GROUPS, HEADS_PER_GROUP).transpose(1, 2, 0)
    return jax.vmap(lambda tb, bk: tb[:, bk])(tg, bucket).astype(jnp.float32)

def moba_attention(q, k, v, rel_bias):
    T, H, dh = q.shape
    scale = dh ** -0.5
    nb = -(-T // MOBA_BLOCK)
    pad = nb * MOBA_BLOCK - T
    q = q.transpose(1, 0, 2)
    kp = jnp.pad(k.transpose(1, 0, 2), ((0, 0), (0, pad), (0, 0)))
    vp = jnp.pad(v.transpose(1, 0, 2), ((0, 0), (0, pad), (0, 0)))
    kb = kp.reshape(H, nb, MOBA_BLOCK, dh)
    vb = vp.reshape(H, nb, MOBA_BLOCK, dh)
    kmean = jnp.mean(kb.astype(jnp.float32), axis=2)
    n_sel = min(MOBA_TOPK, nb)
    n_g = n_sel * MOBA_BLOCK
    blk = jnp.arange(nb)
    offs = jnp.arange(MOBA_BLOCK)

    def one_block(qi):
        start = qi * Q_BLOCK
        t = start + jnp.arange(Q_BLOCK)
        own = start // MOBA_BLOCK
        qb = lax.dynamic_slice_in_dim(q, start, Q_BLOCK, axis=1)
        route = jnp.einsum('hqd,hnd->hqn', qb.astype(jnp.float32), kmean)
        route = jnp.where((blk < own)[None, None, :], route, NEG)
        rval, idx = lax.top_k(route, n_sel)
        valid = rval > NEG / 2
        kg = jax.vmap(lambda kh, ih: kh[ih])(kb, idx)
        vg = jax.vmap(lambda vh, ih: vh[ih])(vb, idx)
        pos_s = idx[..., None] * MOBA_BLOCK + offs
        s_sel = jnp.einsum('hqd,hqnbd->hqnb', qb, kg,
                           preferred_element_type=jnp.float32) * scale
        s_sel = s_sel + bias_per_head(rel_bias, rel_bucket(t[None, :, None, None] - pos_s))
        m_sel = jnp.broadcast_to(valid[..., None], s_sel.shape)
        k_own = lax.dynamic_slice_in_dim(kp, own * MOBA_BLOCK, MOBA_BLOCK, axis=1)
        v_own = lax.dynamic_slice_in_dim(vp, own * MOBA_BLOCK, MOBA_BLOCK, axis=1)
        d_own = t[:, None] - (own * MOBA_BLOCK + offs)[None, :]
        s_own = jnp.einsum('hqd,hbd->hqb', qb, k_own,
                           preferred_element_type=jnp.float32) * scale
        s_own = s_own + bias_shared(rel_bias, rel_bucket(d_own))
        m_own = jnp.broadcast_to((d_own >= 0)[None], s_own.shape)
        s = jnp.concatenate([s_sel.reshape(H, Q_BLOCK, n_g), s_own], axis=-1)
        m = jnp.concatenate([m_sel.reshape(H, Q_BLOCK, n_g), m_own], axis=-1)
        p = masked_softmax(s, m).astype(v.dtype)
        return (jnp.einsum('hqn,hqnd->hqd', p[..., :n_g], vg.reshape(H, Q_BLOCK, n_g, dh))
                + jnp.einsum('hqb,hbd->hqd', p[..., n_g:], v_own))

    out = lax.map(one_block, jnp.arange(T // Q_BLOCK))
    return out.transpose(0, 2, 1, 3).reshape(T, H * dh)

def rglru(xr, conv_w, conv_b, w_rg, b_rg, w_ig, b_ig, lru_lambda):
    T, W = xr.shape
    xp = jnp.pad(xr, ((CONV_WIDTH - 1, 0), (0, 0)))
    xc = conv_b + sum(xp[j:j + T] * conv_w[j] for j in range(CONV_WIDTH))
    xblk = xc.reshape(T, LRU_BLOCKS, LRU_BLOCK)
    r = jax.nn.sigmoid((jnp.einsum('tbi,bij->tbj', xblk, w_rg).reshape(T, W) + b_rg)
                       .astype(jnp.float32))
    i = jax.nn.sigmoid((jnp.einsum('tbi,bij->tbj', xblk, w_ig).reshape(T, W) + b_ig)
                       .astype(jnp.float32))
    log_a = -LRU_C * r * jax.nn.softplus(-lru_lambda.astype(jnp.float32))
    a = jnp.exp(log_a)
    b = jnp.sqrt(-jnp.expm1(2.0 * log_a)) * i * xc.astype(jnp.float32)

    def combine(c1, c2):
        a1, b1 = c1
        a2, b2 = c2
        return a1 * a2, a2 * b1 + b2

    _, h = lax.associative_scan(combine, (a, b), axis=0)
    return h.astype(xr.dtype)

def compress(kt, pos_emb, w1, w2):
    T, G, dh = kt.shape
    nc = (T - CMP_LEN) // CMP_STRIDE + 1
    idx = jnp.arange(nc)[:, None] * CMP_STRIDE + jnp.arange(CMP_LEN)[None, :]
    blocks = kt[idx] + pos_emb[None, :, None, :]
    flat = blocks.transpose(0, 2, 1, 3).reshape(nc, G, CMP_LEN * dh)
    return jax.nn.gelu(flat @ w1) @ w2

def nsa_attention(q, kc_t, vc_t, ks_t, vs_t, kw_t, vw_t, g_logit,
                  cmp_pos_k, cmp_pos_v, cmp_k_w1, cmp_k_w2, cmp_v_w1, cmp_v_w2, rel_bias):
    T = q.shape[0]
    G, P, dh = N_KV_GROUPS, HEADS_PER_GROUP, HEAD_DIM_C
    scale = dh ** -0.5
    qg = q.reshape(T, G, P, dh).transpose(1, 2, 0, 3)
    kc = compress(kc_t, cmp_pos_k, cmp_k_w1, cmp_k_w2).transpose(1, 0, 2)
    vc = compress(vc_t, cmp_pos_v, cmp_v_w1, cmp_v_w2).transpose(1, 0, 2)
    nc = kc.shape[1]
    cmp_start = jnp.arange(nc) * CMP_STRIDE
    cmp_end = cmp_start + CMP_LEN - 1
    ns = T // SEL_BLOCK
    sblk = jnp.arange(ns)
    sel_start = sblk * SEL_BLOCK
    overlap = ((cmp_start[:, None] < sel_start[None, :] + SEL_BLOCK)
               & (cmp_start[:, None] + CMP_LEN > sel_start[None, :])).astype(jnp.float32)
    ks_b = ks_t.transpose(1, 0, 2).reshape(G, ns, SEL_BLOCK, dh)
    vs_b = vs_t.transpose(1, 0, 2).reshape(G, ns, SEL_BLOCK, dh)
    kw_p = jnp.pad(kw_t.transpose(1, 0, 2), ((0, 0), (WINDOW, 0), (0, 0)))
    vw_p = jnp.pad(vw_t.transpose(1, 0, 2), ((0, 0), (WINDOW, 0), (0, 0)))
    gates = jax.nn.sigmoid(g_logit.astype(jnp.float32)).reshape(T, G, P, 3).transpose(1, 2, 0, 3)
    n_sel = min(SEL_TOPK, ns)
    n_g = n_sel * SEL_BLOCK
    offs_s = jnp.arange(SEL_BLOCK)
    n_w = WINDOW + Q_BLOCK

    def one_block(qi):
        start = qi * Q_BLOCK
        t = start + jnp.arange(Q_BLOCK)
        qb = lax.dynamic_slice_in_dim(qg, start, Q_BLOCK, axis=2)
        d_c = t[:, None] - cmp_end[None, :]
        s_c = jnp.einsum('gpqd,gnd->gpqn', qb, kc, preferred_element_type=jnp.float32) * scale
        s_c = s_c + bias_shared(rel_bias, rel_bucket(d_c)).reshape(G, P, Q_BLOCK, nc)
        p_c = masked_softmax(s_c, d_c >= 0)
        o_c = jnp.einsum('gpqn,gnd->gpqd', p_c.astype(vc.dtype), vc)
        imp = jnp.einsum('gpqn,nj->gqj', p_c, overlap)
        cur = t // SEL_BLOCK
        forced = ((sblk[None, :] == 0) | (sblk[None, :] == cur[:, None])
                  | (sblk[None, :] == cur[:, None] - 1))
        imp = jnp.where(forced[None], imp + SEL_FORCE, imp)
        imp = jnp.where((sblk[None, :] > cur[:, None])[None], NEG, imp)
        sval, idx = lax.top_k(imp, n_sel)
        valid = sval > NEG / 2
        kg = jax.vmap(lambda kb_, ib: kb_[ib])(ks_b, idx)
        vg = jax.vmap(lambda vb_, ib: vb_[ib])(vs_b, idx)
        pos_s = idx[..., None] * SEL_BLOCK + offs_s
        d_s = t[None, :, None, None] - pos_s
        s_s = jnp.einsum('gpqd,gqnbd->gpqnb', qb, kg, preferred_element_type=jnp.float32) * scale
        s_s = s_s + bias_per_group(rel_bias, rel_bucket(d_s))
        m_s = (valid[..., None] & (d_s >= 0))[:, None]
        p_s = masked_softmax(s_s.reshape(G, P, Q_BLOCK, n_g), m_s.reshape(G, 1, Q_BLOCK, n_g))
        o_s = jnp.einsum('gpqn,gqnd->gpqd', p_s.astype(vs_b.dtype),
                         vg.reshape(G, Q_BLOCK, n_g, dh))
        kwb = lax.dynamic_slice_in_dim(kw_p, start, n_w, axis=1)
        vwb = lax.dynamic_slice_in_dim(vw_p, start, n_w, axis=1)
        pos_w = start - WINDOW + jnp.arange(n_w)
        d_w = t[:, None] - pos_w[None, :]
        m_w = (pos_w[None, :] >= 0) & (d_w >= 0) & (d_w < WINDOW)
        s_w = jnp.einsum('gpqd,gkd->gpqk', qb, kwb, preferred_element_type=jnp.float32) * scale
        s_w = s_w + bias_shared(rel_bias, rel_bucket(d_w)).reshape(G, P, Q_BLOCK, n_w)
        p_w = masked_softmax(s_w, m_w)
        o_w = jnp.einsum('gpqk,gkd->gpqd', p_w.astype(vwb.dtype), vwb)
        gb = lax.dynamic_slice_in_dim(gates, start, Q_BLOCK, axis=2)
        return (gb[..., 0:1] * o_c + gb[..., 1:2] * o_s + gb[..., 2:3] * o_w).astype(q.dtype)

    out = lax.map(one_block, jnp.arange(T // Q_BLOCK))
    return out.transpose(0, 3, 1, 2, 4).reshape(T, G * P * dh)

def mixer_ab(h, w_in, conv_w, conv_b, w_rg, b_rg, w_ig, b_ig, lru_lambda, w_out, rel_bias):
    Bt, T, _ = h.shape
    dA = N_HEADS_A * HEAD_DIM_A
    proj = h @ w_in
    q, k, v, xr, gr = jnp.split(proj, [dA, 2 * dA, 3 * dA, 3 * dA + LRU_WIDTH], axis=-1)
    shp = (Bt, T, N_HEADS_A, HEAD_DIM_A)
    o_a = jax.vmap(moba_attention, in_axes=(0, 0, 0, None))(
        q.reshape(shp), k.reshape(shp), v.reshape(shp), rel_bias)
    o_b = jax.vmap(rglru, in_axes=(0, None, None, None, None, None, None, None))(
        xr, conv_w, conv_b, w_rg, b_rg, w_ig, b_ig, lru_lambda)
    o_b = o_b * jax.nn.gelu(gr)
    return jnp.concatenate([o_a, o_b], axis=-1) @ w_out

def mixer_c(h, w_in, cmp_pos_k, cmp_pos_v, cmp_k_w1, cmp_k_w2, cmp_v_w1, cmp_v_w2,
            w_out, rel_bias):
    Bt, T, _ = h.shape
    dq = N_HEADS_C * HEAD_DIM_C
    proj = h @ w_in
    pieces = jnp.split(proj, [dq + j * C_KV for j in range(7)], axis=-1)
    q = pieces[0].reshape(Bt, T, N_HEADS_C, HEAD_DIM_C)
    kv = [p.reshape(Bt, T, N_KV_GROUPS, HEAD_DIM_C) for p in pieces[1:7]]
    gl = pieces[7].reshape(Bt, T, N_HEADS_C, 3)
    o = jax.vmap(nsa_attention, in_axes=(0,) * 8 + (None,) * 7)(
        q, kv[0], kv[1], kv[2], kv[3], kv[4], kv[5], gl,
        cmp_pos_k, cmp_pos_v, cmp_k_w1, cmp_k_w2, cmp_v_w1, cmp_v_w2, rel_bias)
    return o @ w_out

def setup_inputs(seed: int = 0) -> dict:
    key = jax.random.key(seed)
    ks = jax.random.split(key, 26)
    f32 = jnp.float32

    def nrm(k, shape, fan_in):
        return jax.random.normal(k, shape, f32) * fan_in ** -0.5

    def gain(k, shape):
        return 1.0 + 0.05 * jax.random.normal(k, shape, f32)

    u = jax.random.uniform(ks[8], (N_EVEN, LRU_WIDTH), f32, 0.9, 0.999)
    a = u ** (1.0 / LRU_C)
    lam = jnp.log(a) - jnp.log1p(-a)
    return {
        'x': jax.random.normal(ks[0], (BATCH, SEQ, D_MODEL), f32),
        'rel_bias': 0.3 * jax.random.normal(ks[1], (N_BUCKETS, N_BIAS_HEADS), f32),
        'ab_w_in': nrm(ks[2], (N_EVEN, D_MODEL, AB_IN), D_MODEL),
        'ab_conv_w': nrm(ks[3], (N_EVEN, CONV_WIDTH, LRU_WIDTH), CONV_WIDTH),
        'ab_conv_b': 0.02 * jax.random.normal(ks[4], (N_EVEN, LRU_WIDTH), f32),
        'ab_w_rg': nrm(ks[5], (N_EVEN, LRU_BLOCKS, LRU_BLOCK, LRU_BLOCK), LRU_BLOCK),
        'ab_b_rg': 0.1 * jax.random.normal(ks[6], (N_EVEN, LRU_WIDTH), f32),
        'ab_w_ig': nrm(ks[7], (N_EVEN, LRU_BLOCKS, LRU_BLOCK, LRU_BLOCK), LRU_BLOCK),
        'ab_b_ig': 0.1 * jax.random.normal(ks[9], (N_EVEN, LRU_WIDTH), f32),
        'ab_lru_lambda': lam,
        'ab_w_out': nrm(ks[10], (N_EVEN, AB_OUT, D_MODEL), AB_OUT),
        'c_w_in': nrm(ks[11], (N_ODD, D_MODEL, C_IN), D_MODEL),
        'c_cmp_pos_k': 0.1 * jax.random.normal(ks[12], (N_ODD, CMP_LEN, HEAD_DIM_C), f32),
        'c_cmp_pos_v': 0.1 * jax.random.normal(ks[13], (N_ODD, CMP_LEN, HEAD_DIM_C), f32),
        'c_cmp_k_w1': nrm(ks[14], (N_ODD, CMP_LEN * HEAD_DIM_C, CMP_HIDDEN), CMP_LEN * HEAD_DIM_C),
        'c_cmp_k_w2': nrm(ks[15], (N_ODD, CMP_HIDDEN, HEAD_DIM_C), CMP_HIDDEN),
        'c_cmp_v_w1': nrm(ks[16], (N_ODD, CMP_LEN * HEAD_DIM_C, CMP_HIDDEN), CMP_LEN * HEAD_DIM_C),
        'c_cmp_v_w2': nrm(ks[17], (N_ODD, CMP_HIDDEN, HEAD_DIM_C), CMP_HIDDEN),
        'c_w_out': nrm(ks[18], (N_ODD, C_OUT, D_MODEL), C_OUT),
        'norm_mix_pre': gain(ks[19], (DEPTH, D_MODEL)),
        'norm_mix_post': gain(ks[20], (DEPTH, D_MODEL)),
        'norm_mlp_pre': gain(ks[21], (DEPTH, D_MODEL)),
        'norm_mlp_post': gain(ks[22], (DEPTH, D_MODEL)),
        'w_up': nrm(ks[23], (DEPTH, D_MODEL, D_FF), D_MODEL),
        'w_down': nrm(ks[24], (DEPTH, D_FF, D_MODEL), D_FF),
    }

def reference(x, rel_bias,
              ab_w_in, ab_conv_w, ab_conv_b, ab_w_rg, ab_b_rg, ab_w_ig, ab_b_ig,
              ab_lru_lambda, ab_w_out,
              c_w_in, c_cmp_pos_k, c_cmp_pos_v, c_cmp_k_w1, c_cmp_k_w2, c_cmp_v_w1,
              c_cmp_v_w2, c_w_out,
              norm_mix_pre, norm_mix_post, norm_mlp_pre, norm_mlp_post, w_up, w_down):
    for layer in range(DEPTH):
        i = layer // 2
        h = rmsnorm(x, norm_mix_pre[layer])
        if layer % 2 == 0:
            m = mixer_ab(h, ab_w_in[i], ab_conv_w[i], ab_conv_b[i], ab_w_rg[i], ab_b_rg[i],
                         ab_w_ig[i], ab_b_ig[i], ab_lru_lambda[i], ab_w_out[i], rel_bias)
        else:
            m = mixer_c(h, c_w_in[i], c_cmp_pos_k[i], c_cmp_pos_v[i], c_cmp_k_w1[i],
                        c_cmp_k_w2[i], c_cmp_v_w1[i], c_cmp_v_w2[i], c_w_out[i], rel_bias)
        x = x + rmsnorm(m, norm_mix_post[layer])
        h = rmsnorm(x, norm_mlp_pre[layer])
        f = jnp.square(jax.nn.relu(h @ w_up[layer])) @ w_down[layer]
        x = x + rmsnorm(f, norm_mlp_post[layer])
    return x


_drawn_inputs = setup_inputs


def setup_inputs(seed=0):
    import zlib

    import numpy as np

    out = dict(_drawn_inputs(seed))
    spreads = {}
    factors = {'ab_b_rg': 3.705, 'c_cmp_pos_k': 8.0}
    for name, (base, spread) in spreads.items():
        noise = np.random.default_rng([zlib.crc32(name.encode()), seed]).standard_normal(out[name].shape)
        drawn = base * np.exp(spread * noise) if base else spread * noise
        out[name] = jnp.asarray(drawn.astype(out[name].dtype))
    for name, factor in factors.items():
        out[name] = (out[name] * factor).astype(out[name].dtype)
    return out
```

```python
import math
from contextlib import ExitStack

import numpy as np

import concourse.bass as bass
from concourse import mybir

F32 = mybir.dt.float32
F32R = mybir.dt.float32r
ALU = mybir.AluOpType
ACT = mybir.ActivationFunctionType
AX = mybir.AxisListType

P = 128
T = 256
TT = T // P
D = 1024
KT = D // P
FF = 4096
HEADS = 8
EPS = 1e-6
MASKED = 1e30
CHUNK = 2048
RING = 4
LEAD = 2

W = 512
CT = W // P
TAPS = 4
LRU_C = 8.0
DH_A = 64
DH_C = 128
GROUPS = 2
PER_GROUP = HEADS // GROUPS
CMP_LEN = 32
CMP_STRIDE = 16
NC = (T - CMP_LEN) // CMP_STRIDE + 1
CMP_HIDDEN = 256
NPAD = 32
BUCKETS = 32

XR, Q0, K0, V0, GR, OUT0 = 0, 2, 4, 6, 8, 10
MLP0 = 14
MLP_CHUNKS = 32
Q1 = MLP0 + MLP_CHUNKS
KS, VS, KW, VW, KC, VC = range(Q1 + 4, Q1 + 10)
CMPK, CMPV, OUT1 = Q1 + 10, Q1 + 14, Q1 + 18
MLP1 = OUT1 + 4
CHUNKS = MLP1 + MLP_CHUNKS
UNIT_MLP0 = 2 * OUT0
UNIT_Q1 = UNIT_MLP0 + 2 * (MLP_CHUNKS // 2)
UNIT_MLP1 = UNIT_Q1 + 2 * (CMPK - Q1)
JOBS0 = HEADS
JOBS = 3 * HEADS


def unit_of(chunk, half):
    return (2 * chunk if chunk < MLP0 else UNIT_Q1 + 2 * (chunk - Q1)) + half


LAST_OF_BRANCH = {1: MLP0 - 1, 2: Q1 - 1, 3: MLP1 - 1, 4: CHUNKS - 1}


def sq_of(u):
    return u - UNIT_MLP0 if u < UNIT_Q1 else MLP_CHUNKS + u - UNIT_MLP1


def cmp_keys(i):
    return ((i + 1) * P - CMP_LEN) // CMP_STRIDE + 1


FILL0 = {0: [(V0 + 1, 0)], 1: [(V0 + 1, 1)], 3: [(GR, 0)], 5: [(GR, 1)], 7: [(GR + 1, 0)], 8: [(GR + 1, 1)]}


def fill1():
    units = [(c, h) for c in range(KW, OUT1) for h in range(2)]
    steps, at = {}, 0
    n = 2 * HEADS
    for s in range(n):
        upto = min(len(units), math.ceil((s + 1) * len(units) / n))
        steps[s + HEADS] = units[at:upto]
        at = upto
    return steps


FILL1 = fill1()
KCMP_STEP = 1 + next(s for s, units in FILL1.items() if (CMPK + 3, 1) in units)


def trunk(nc, x_in, w_stream, gains, lru_vec, lru_gate, rel_bias, bias_select, ident_in, gate_w,
          cmp_pos, cmp_w2, out):
    with ExitStack() as ctx:
        def sb(name, shape, dt=F32):
            return ctx.enter_context(nc.sbuf_tensor(name, shape, dt))

        def sem(name):
            return ctx.enter_context(nc.semaphore(name))

        raw = sb("raw", [P, RING, CHUNK])
        w_hi = sb("w_hi", [P, RING, CHUNK], F32R)
        w_lo = sb("w_lo", [P, RING, CHUNK], F32R)
        x = sb("x", [P, TT, D])
        tok = sb("tok", [P, TT, D])
        t_hi = sb("t_hi", [P, KT, T], F32R)
        t_lo = sb("t_lo", [P, KT, T], F32R)
        gain = sb("gain", [P, 2, D])
        toep = sb("toep", [P, HEADS, 3 * P])
        qT = sb("qT", [P, HEADS, T])
        kT = sb("kT", [P, 4, T])
        v = sb("v", [P, TT, W])
        lgate = v[:, :, :].rearrange("p w (t n) -> p w t n", t=CT)
        xr = sb("xr", [P, CT, T + TAPS - 1])
        xc = tok[:, :, W:]
        decay = qT[:, CT:, :]

        def xc_tile(t):
            return xc[:, t // 2, (t % 2) * T:(t % 2 + 1) * T]

        def pairs(buf):
            return buf[:, :, :].rearrange("p (a b) t -> p a (b t)", a=2)

        rg = sb("rg", [P, CT, T])
        ig = sb("ig", [P, CT, T])
        mixb = sb("mixb", [P, CT, T])
        relu, square = rg[:, 0:2, :], rg[:, 2:4, :]
        cmp_in = rg
        hidden = xr[:, :, :].rearrange("p a t -> p (a t)")[:, 0:2 * CMP_HIDDEN].rearrange("p (w n) -> p w n", w=2)
        hvT = mixb[:, 0:2, :].rearrange("p t (g j n) -> p t g j n", g=GROUPS, j=PER_GROUP)
        ce = mixb[:, 2:4, :].rearrange("p i (h n) -> p i h n", h=HEADS)
        flat_hi = sb("flat_hi", [P, 2, CMP_LEN * GROUPS * NC], F32R)
        flat_lo = sb("flat_lo", [P, 2, CMP_LEN * GROUPS * NC], F32R)
        h_hi, h_lo = (f[:, :, :].rearrange("p w n -> p (w n)")[:, 0:4 * T].rearrange("p (s t) -> p s t", s=4)
                      for f in (flat_hi, flat_lo))
        sneg = sb("sneg", [P, 2, 3 * P])
        prob = sb("prob", [P, 2, 3 * P])
        pT = sb("pT", [P, 2, 3 * P])
        cpT = sneg[:, :, 0:T].rearrange("p i (g t) -> p i g t", g=GROUPS)
        cs = prob[:, :, 0:HEADS * 16].rearrange("p i (h n) -> p i h n", h=HEADS)
        mneg = sb("mneg", [P, 2 * JOBS])
        sums = sb("sums", [P, 2 * JOBS])
        coef = sb("coef", [P, 2 * JOBS])
        stat = sb("stat", [P, 32])
        lvec = sb("lvec", [P, CT, 8])
        sp = sb("sp", [P, 6, CT])
        ident = sb("ident", [P, P])
        table = sb("table", [BUCKETS + 1, HEADS])
        select = decay[0:BUCKETS + 1, 0:2, :].rearrange("p a t -> p (a t)")[:, 0:3 * P - 1]
        ext = mixb[0:HEADS, 0:2, :].rearrange("p a t -> p (a t)")[:, 0:3 * P - 1]
        xr_flat, ig_flat = (b[:, :, :].rearrange("p a t -> p (a t)") for b in (xr, ig))
        w2 = xr_flat[:, 2 * CMP_HIDDEN:2 * CMP_HIDDEN + 4 * P].rearrange("p (w t n) -> p w t n", w=2, t=2)
        gw = ig_flat[:, 0:KT * 3 * HEADS].rearrange("p (k n) -> p k n", k=KT)
        pos = ig_flat[:, CMP_LEN * GROUPS * NC:CMP_LEN * (GROUPS * NC + 2)].rearrange("p (w l) -> p w l", w=2)
        gw_hi = sb("gw_hi", [P, KT, 3 * HEADS], F32R)
        gw_lo = sb("gw_lo", [P, KT, 3 * HEADS], F32R)
        gates = sb("gates", [P, TT, 3 * HEADS])
        hkT = sb("hkT", [P, 2, GROUPS * NC])
        kcmp = sb("kcmp", [P, GROUPS * NC])
        vcmp = pT[:, 0, 0:GROUPS * P].rearrange("p (g d) -> p g d", g=GROUPS)
        cst = sb("cst", [P, TT, 4, HEADS])
        acc = ctx.enter_context(nc.psum_tensor("acc", [P, 4, 512], F32))
        wk = [ctx.enter_context(nc.psum_tensor(f"wk{i}", [P, 512], F32)) for i in range(4)]
        ext_dram = nc.dram_tensor("bias_rows", [HEADS, P, 3 * P - 1], F32, kind="Internal").ap()

        landed = [sem(f"landed{i}") for i in range(RING)]
        hi_ready, lo_ready = sem("hi_ready"), sem("lo_ready")
        half_done = sem("half_done")
        x_landed = [sem("x_landed0"), sem("x_landed1")]
        gain_landed = [sem("gain_post_landed"), sem("gain_pre_landed")]
        lru_landed, nsa_landed, small_landed, table_landed = (sem("lru_landed"), sem("nsa_landed"), sem("ident_landed"),
                                                              sem("table_landed"))
        ext_stored, toep_landed, out_stored = sem("ext_stored"), sem("toep_landed"), sem("out_stored")
        cleared, table_one = sem("cleared"), sem("table_one")
        ext_done, ext_read = sem("ext_done"), sem("ext_read")
        unit_done, unit_read = sem("unit_done"), sem("unit_read")
        post_sq, post_std, x_ready = sem("post_sq"), sem("post_std"), sem("x_ready")
        pre_sq, pre_std, xn_ready = sem("pre_sq"), sem("pre_std"), sem("xn_ready")
        xT_done, tT_hi, tT_ready = sem("xT_done"), sem("tT_hi"), sem("tT_ready")
        relu_ready, squared, h_ready = sem("relu_ready"), sem("squared"), sem("h_ready")
        sp_ready, xc_ready = sem("sp_ready"), sem("xc_ready")
        lru_gates_done, lru_gates = sem("lru_gates_done"), sem("lru_gates")
        decays, beta2_ready, beta_ready, ob_ready = sem("decays"), sem("beta2_ready"), sem("beta_ready"), sem("ob_ready")
        lru_b = sem("lru_b")
        scores_done, sneg_ready, exp_done = sem("scores_done"), sem("sneg_ready"), sem("exp_done")
        pT_done, pT_ready, pv_done, o_ready = sem("pT_done"), sem("pT_ready"), sem("pv_done"), sem("o_ready")
        gw_ready, gates_done, gates_ready = sem("gw_ready"), sem("gates_done"), sem("gates_ready")
        flat_ready, cmp_gelu = sem("flat_ready"), sem("cmp_gelu")
        hT_done, hT_ready, kv_done, kv_ready = sem("hT_done"), sem("hT_ready"), sem("kv_done"), sem("kv_ready")
        cs_done, cs_ready, ce_exp, ce_ready = sem("cs_done"), sem("cs_ready"), sem("ce_exp"), sem("ce_ready")
        cpT_done, cpT_ready, cpv_done = sem("cpT_done"), sem("cpT_ready"), sem("cpv_done")
        oc_ready = sem("oc_ready")
        oT_done, oT_hi, oT_ready = sem("oT_done"), sem("oT_hi"), sem("oT_ready")
        dve_step = sem("dve_step")

        def job(k):
            if k < JOBS0:
                return k, DH_A, (k % 2) * DH_A, k // 2, k // 2, k * DH_A
            branch, head = divmod(k - JOBS0, HEADS)
            g = head // PER_GROUP
            return head, DH_C, 0, head, GROUPS * branch + g, (GROUPS * branch + g) * DH_C

        block = ctx.enter_context(nc.Block())

        @block.sync
        def _(eng):
            for i in range(TT):
                eng.dma_start(x[:, i, :], x_in[i * P:(i + 1) * P, :]).then_inc(x_landed[i], 16)
            eng.dma_start(ident[:, :], ident_in).then_inc(small_landed, 16)
            for c in range(RING):
                eng.dma_start(raw[:, c, :], w_stream[c]).then_inc(landed[c], 16)
            with eng.Fori(0, CHUNKS // RING - 1) as j:
                for c in range(RING):
                    eng.wait_ge(lo_ready, j * RING + (c + 1))
                    eng.dma_start(raw[:, c, :], w_stream[bass.ds(j * RING + (RING + c), 1)]
                                  .rearrange("o p f -> (o p) f")).then_inc(landed[c], 16)
            for i in range(TT):
                eng.wait_ge(x_ready, 3 * TT + i + 1)
                eng.dma_start(out[i * P:(i + 1) * P, :], x[:, i, :]).then_inc(out_stored, 16)
            eng.wait_ge(out_stored, 16 * TT)

        @block.gpsimd
        def _(eng):
            def load_gain(which, row):
                eng.dma_start(gain[:, which, :], bass.AP(gains.tensor, row * D, [[0, P], [1, D]]))\
                   .then_inc(gain_landed[which], 16)

            load_gain(1, 0)
            eng.memset(table[:, :], 1.0).then_inc(table_one, 1)
            eng.wait_ge(table_one, 1)
            eng.dma_start(table[0:BUCKETS, :], rel_bias).then_inc(table_landed, 16)
            eng.dma_start(select, bias_select).then_inc(table_landed, 16)
            eng.dma_start(lvec[:, :, :], lru_vec).then_inc(lru_landed, 16)
            eng.dma_start(lgate, lru_gate).then_inc(lru_landed, 16)
            eng.memset(xr[:, :, 0:TAPS - 1], 0.0).then_inc(cleared, 1)
            eng.wait_ge(ext_read, 1)
            eng.dma_start(ext_dram, bass.AP(ext.tensor, ext.offset, [list(ext.ap[0]), [0, P], list(ext.ap[1])]))\
               .then_inc(ext_stored, 16)
            eng.wait_ge(ext_stored, 16)
            rows = 3 * P - 1
            for at, m0, n in ((0, P, P), (P, 0, 2 * P)):
                eng.dma_start(toep[:, :, at:at + n],
                              bass.AP(ext_dram.tensor, m0 + P - 1, [[rows - 1, P], [P * rows, HEADS], [1, n]]))\
                   .then_inc(toep_landed, 16)
            load_gain(0, 1)
            eng.wait_ge(ob_ready, 1)
            eng.dma_start(gw, gate_w).then_inc(nsa_landed, 16)
            eng.dma_start(pos, cmp_pos).then_inc(nsa_landed, 16)
            eng.dma_start(w2, cmp_w2).then_inc(nsa_landed, 16)
            for b in range(1, 4):
                eng.wait_ge(xn_ready, TT * b)
                load_gain(1, 2 * b)
                eng.wait_ge(x_ready, TT * b)
                load_gain(0, 2 * b + 1)

        @block.scalar
        def _(eng):
            def hi(c, load, used):
                eng.wait_ge(landed[c], load)
                if used is not None:
                    eng.wait_ge(half_done, used)
                nc.scalar.activation(w_hi[:, c, :], raw[:, c, :], ACT.Copy).then_inc(hi_ready, 1)

            def split(n):
                if n < CHUNKS:
                    hi(n % RING, 16 * (n // RING + 1), 2 * (n - RING + 1) if n >= RING else None)

            def norms(b, post, pre):
                if post:
                    for i in range(TT):
                        k = TT * (b - 1) + i
                        eng.wait_ge(half_done, 2 * LAST_OF_BRANCH[b] + i + 1)
                        nc.scalar.activation(tok[:, i, :], acc[:, 2 * i:2 * i + 2, :], ACT.Square,
                                             accum_out=stat[:, k:k + 1]).then_inc(post_sq, 1)
                        eng.wait_ge(post_sq, k + 1)
                        nc.scalar.activation(stat[:, 8 + k:9 + k], stat[:, k:k + 1], ACT.Sqrt,
                                             scale=1.0 / D, bias=EPS).then_inc(post_std, 1)
                if pre:
                    for i in range(TT):
                        k = TT * b + i
                        if b == 0:
                            eng.wait_ge(x_landed[i], 16)
                        else:
                            eng.wait_ge(x_ready, TT * (b - 1) + i + 1)
                        nc.scalar.activation(tok[:, i, :], x[:, i, :], ACT.Square,
                                             accum_out=stat[:, 16 + k:17 + k]).then_inc(pre_sq, 1)
                        eng.wait_ge(pre_sq, k + 1)
                        nc.scalar.activation(stat[:, 24 + k:25 + k], stat[:, 16 + k:17 + k], ACT.Sqrt,
                                             scale=1.0 / D, bias=EPS).then_inc(pre_std, 1)
                    for i in range(TT):
                        k = TT * b + i
                        for half in range(2):
                            eng.wait_ge(xT_done, 2 * k + half + 1)
                            nc.scalar.activation(
                                t_hi[:, 4 * half:4 * half + 4, i * P:(i + 1) * P],
                                wk[2 * (1 - i) + half][:, :].rearrange("p (k t) -> p k t", k=4),
                                ACT.Copy).then_inc(tT_hi, 1)

            def evacuate(c, half):
                u = unit_of(c, half)
                src = wk[half][:, 0:T]
                func, scale = ACT.Copy, 1.0
                if c < Q0:
                    dst = xr[:, 2 * c + half, TAPS - 1:]
                    if u == 0:
                        eng.wait_ge(cleared, 1)
                elif c < K0:
                    dst, scale = qT[:, 2 * (c - Q0) + half, :], -DH_A ** -0.5
                elif c < V0:
                    dst = kT[:, 2 * (c - K0) + half, :]
                elif c < GR:
                    dst = v[:, half, T * (c - V0):T * (c - V0 + 1)]
                elif c < OUT0:
                    dst, func = mixb[:, 2 * (c - GR) + half, :], ACT.Gelu_apprx_tanh
                elif c < KS:
                    dst, scale = qT[:, 2 * (c - Q1) + half, :], -DH_C ** -0.5
                elif c in (KS, KW):
                    dst = kT[:, c - KS + half, :]
                elif c in (VS, VW):
                    dst = v[:, half, T * ((c - VS) // 2):T * ((c - VS) // 2 + 1)]
                else:
                    dst = cmp_in[:, 2 * (c - KC) + half, :]
                if c == GR and half == 0:
                    eng.wait_ge(lru_b, 1)
                eng.wait_ge(half_done, 2 * c + half + 1)
                nc.scalar.activation(dst, src, func, scale=scale).then_inc(unit_read, 1)

            def exps(k):
                eng.wait_ge(sneg_ready, k + 1)
                if k >= 2:
                    eng.wait_ge(pT_done, k - 1)
                for i, (a, n) in enumerate(((0, P), (P, 2 * P))):
                    e = nc.scalar.activation(prob[:, k % 2, a:a + n], sneg[:, k % 2, a:a + n], ACT.Exp,
                                             scale=-1.0, bias=mneg[:, 2 * k + i:2 * k + i + 1],
                                             accum_out=sums[:, 2 * k + i:2 * k + i + 1])
                e.then_inc(exp_done, 1)

            def mlp(first, unit0):
                def relus(c, u, j4=0):
                    for s in range(2):
                        eng.wait_ge(half_done, j4 * 2 + (2 * c + s + 1))
                        if sq_of(u) >= 2:
                            eng.wait_ge(squared, j4 + (sq_of(u) + s - 1))
                        nc.scalar.activation(relu[:, s, :], wk[s][:, 0:T], ACT.Relu).then_inc(unit_read, 1)

                split(first + LEAD)
                relus(first, unit0)
                with eng.Fori(0, 7) as j:
                    for c in range(4):
                        n = first + 1 + c + LEAD
                        hi(n % RING, j * 16 + 16 * (n // RING + 1), j * 8 + 2 * (n - RING + 1))
                        if c % 2 == 0:
                            relus(first + 1 + c, unit0 + 2 + c, j * 4)
                split(first + 29 + LEAD)
                relus(first + 29, unit0 + 30)
                split(first + 30 + LEAD)
                split(first + 31 + LEAD)

            def o_parts(groups):
                for g, (i, half, bank) in enumerate(groups):
                    n = g + (0 if len(groups) == 2 else 2)
                    eng.wait_ge(oT_done, n + 1)
                    nc.scalar.activation(t_hi[:, 4 * half:4 * half + 4, i * P:(i + 1) * P],
                                         wk[bank][:, :].rearrange("p (k t) -> p k t", k=4),
                                         ACT.Copy).then_inc(oT_hi, 1)

            norms(0, False, True)
            split(0)
            split(1)
            for c in range(XR, V0 + 1):
                split(c + LEAD)
                if c == Q0:
                    eng.wait_ge(sp_ready, 1)
                    nc.scalar.activation(sp[:, 1, :], sp[:, 0, :], ACT.Exp).then_inc(sp_ready, 1)
                if c == K0 + 1:
                    eng.wait_ge(lru_gates_done, 1)
                    for w in range(2):
                        for t in range(CT):
                            s = nc.scalar.activation((rg, ig)[w][:, t, :], acc[:, t, w * T:(w + 1) * T],
                                                     ACT.Sigmoid, bias=lvec[:, t, 5 + w:6 + w])
                            s.then_inc(lru_gates, 1)
                if c == V0:
                    eng.wait_ge(lru_gates, 8)
                    eng.wait_ge(sp_ready, 3)
                    eng.wait_ge(ext_stored, 16)
                    for t in range(CT):
                        nc.scalar.activation(decay[:, t, :], rg[:, t, :], ACT.Exp, scale=sp[:, 4, t:t + 1])\
                          .then_inc(decays, 1)
                    for t in range(CT):
                        nc.scalar.activation(mixb[:, t, :], rg[:, t, :], ACT.Exp, scale=sp[:, 5, t:t + 1])\
                          .then_inc(decays, 1)
                    eng.wait_ge(decays, 2 * CT)
                    for t in range(CT):
                        nc.scalar.activation(rg[:, t, :], rg[:, t, :], ACT.Tanh, scale=sp[:, 3, t:t + 1])\
                          .then_inc(decays, 1)
                for half in range(2):
                    evacuate(c, half)
            eng.wait_ge(beta2_ready, 1)
            nc.scalar.activation(mixb[:, :, :], mixb[:, :, :], ACT.Sqrt).then_inc(beta_ready, 1)
            for k in range(JOBS0 + 2):
                if k < JOBS0:
                    exps(k)
                for c, half in FILL0.get(k, []):
                    if half == 0:
                        split(c + LEAD)
                for c, half in FILL0.get(k, []):
                    evacuate(c, half)
            for c in range(OUT0, OUT0 + 2):
                split(c + LEAD)
            o_parts(((0, 0, 2), (1, 0, 3)))
            for c in range(OUT0 + 2, MLP0):
                split(c + LEAD)
            norms(1, True, True)
            mlp(MLP0, UNIT_MLP0)
            norms(2, True, True)
            for c in range(Q1, KW):
                split(c + LEAD)
                for half in range(2):
                    evacuate(c, half)
            for i in range(TT):
                eng.wait_ge(gates_done, i + 1)
                nc.scalar.activation(gates[:, i, :], wk[2 + i][:, 0:3 * HEADS], ACT.Sigmoid)\
                  .then_inc(gates_ready, 1)
            for k in range(JOBS0, JOBS):
                exps(k)
                for c, half in FILL1.get(k, []):
                    if half == 0:
                        split(c + LEAD)
                for c, half in FILL1.get(k, []):
                    if c < CMPK:
                        evacuate(c, half)
                    elif half == 1 and c in (CMPK + 3, CMPV + 3):
                        which = (c - CMPK) // 4
                        eng.wait_ge(half_done, 2 * c + 2)
                        nc.scalar.activation(hidden[0:GROUPS * NC, which, :], wk[which][0:GROUPS * NC, 0:CMP_HIDDEN],
                                             ACT.Gelu_apprx_tanh).then_inc(cmp_gelu, 1)
            for i in range(TT):
                n = cmp_keys(i)
                eng.wait_ge(cs_ready, i + 1)
                nc.scalar.activation(ce[:, i, :, 0:n], cs[:, i, :, 0:n], ACT.Exp, scale=-1.0).then_inc(ce_exp, 1)
            o_parts([(i, half, 2 * i + half) for i in range(TT) for half in range(2)])
            for c in range(OUT1, MLP1):
                split(c + LEAD)
            norms(3, True, True)
            mlp(MLP1, UNIT_MLP1)
            norms(4, True, False)

        @block.vector
        def _(eng):
            steps = [0]

            def link(ins):
                steps[0] += 1
                ins.then_inc(dve_step, 1)
                eng.wait_ge(dve_step, steps[0])

            def lo(c, n):
                eng.wait_ge(hi_ready, n + 1)
                nc.vector.tensor_tensor(w_lo[:, c, :], raw[:, c, :], w_hi[:, c, :].bitcast(F32),
                                        ALU.subtract).then_inc(lo_ready, 1)

            def split(n):
                if n < CHUNKS:
                    lo(n % RING, n)

            def scaled(i, k0, src, which):
                link(nc.vector.reciprocal(stat[:, k0:k0 + 1], stat[:, k0:k0 + 1]))
                return nc.vector.scalar_tensor_tensor(out=tok[:, i, :], in0=src, scalar=stat[:, k0:k0 + 1],
                                                      in1=gain[:, which, :], op0=ALU.mult, op1=ALU.mult)

            def norms(b, post, pre):
                if post:
                    eng.wait_ge(gain_landed[0], 16 * b)
                    for i in range(TT):
                        k = TT * (b - 1) + i
                        eng.wait_ge(post_std, k + 1)
                        link(scaled(i, 8 + k, acc[:, 2 * i:2 * i + 2, :].rearrange("p a n -> p (a n)"), 0))
                        nc.vector.tensor_tensor(x[:, i, :], x[:, i, :], tok[:, i, :], ALU.add)\
                          .then_inc(x_ready, 1)
                if pre:
                    eng.wait_ge(gain_landed[1], 16 * (b + 1))
                    for i in range(TT):
                        k = TT * b + i
                        eng.wait_ge(pre_std, k + 1)
                        scaled(i, 24 + k, x[:, i, :], 1).then_inc(xn_ready, 1)
                    for i in range(TT):
                        k = TT * b + i
                        for half in range(2):
                            eng.wait_ge(tT_hi, 2 * k + half + 1)
                            dst = slice(4 * half, 4 * half + 4), slice(i * P, (i + 1) * P)
                            nc.vector.tensor_tensor(
                                t_lo[:, dst[0], dst[1]],
                                wk[2 * (1 - i) + half][:, :].rearrange("p (k t) -> p k t", k=4),
                                t_hi[:, dst[0], dst[1]].bitcast(F32), ALU.subtract).then_inc(tT_ready, 1)

            def scores(k):
                head = job(k)[0]
                eng.wait_ge(scores_done, k + 1)
                if k >= 2:
                    eng.wait_ge(exp_done, k - 1)
                for i, (a, n) in enumerate(((0, P), (P, 2 * P))):
                    s = nc.vector.tensor_tensor_reduce(
                        out=sneg[:, k % 2, a:a + n], in0=wk[2 + k % 2][:, a:a + n],
                        in1=toep[:, head, a:a + n], scale=1.0, scalar=3.0e38, op0=ALU.add, op1=ALU.min,
                        accum_out=mneg[:, 2 * k + i:2 * k + i + 1])
                s.then_inc(sneg_ready, 1)

            def probs_out(k):
                eng.wait_ge(pT_done, k + 1)
                if k >= 2:
                    eng.wait_ge(pv_done, k - 1)
                nc.vector.tensor_copy(pT[:, k % 2, :], acc[:, k % 2, 0:3 * P]).then_inc(pT_ready, 1)

            def head_out(k):
                head, d = job(k)[0:2]
                c2 = coef[:, 2 * k:2 * k + 2]
                eng.wait_ge(exp_done, k + 1)
                link(nc.vector.tensor_scalar(c2, sums[:, 2 * k:2 * k + 2], 1e-30, None, ALU.max))
                link(nc.vector.reciprocal(c2, c2))
                if k >= JOBS0:
                    branch = 1 + (k - JOBS0) // HEADS
                    eng.wait_ge(gates_ready, TT)
                    link(nc.vector.tensor_tensor(c2, c2, gates[:, :, 3 * head + branch], ALU.mult))
                eng.wait_ge(pv_done, k + 1)
                for i in range(TT):
                    dst = tok[:, i, head * d:(head + 1) * d]
                    src = acc[:, 2 + k % 2, i * T:i * T + d]
                    if k < 2 * HEADS:
                        o = nc.vector.tensor_scalar(dst, src, coef[:, 2 * k + i:2 * k + i + 1], None, ALU.mult)
                    else:
                        if i == 0:
                            eng.wait_ge(o_ready, k - HEADS + 1)
                        o = nc.vector.scalar_tensor_tensor(out=dst, in0=src, scalar=coef[:, 2 * k + i:2 * k + i + 1],
                                                           in1=dst, op0=ALU.mult, op1=ALU.add)
                o.then_inc(o_ready, 1)

            def pipeline(first, last, fill, extra):
                for s in range(first, last + 2):
                    if s < last:
                        scores(s)
                    if first <= s - 1 < last:
                        probs_out(s - 1)
                    if first <= s - 2 < last:
                        head_out(s - 2)
                    for c, half in fill.get(s, []):
                        if half == 0:
                            split(c + LEAD)
                    extra(s)

            def squares(slot, s, read, sq):
                eng.wait_ge(unit_read, read)
                if not isinstance(sq, int) or sq >= 2:
                    eng.wait_ge(h_ready, sq - 1)
                nc.vector.tensor_tensor(h_hi[:, slot, :], relu[:, s, :], relu[:, s, :], ALU.mult)
                nc.vector.tensor_tensor(square[:, s, :], relu[:, s, :], relu[:, s, :], ALU.mult)\
                  .then_inc(squared, 1)
                eng.wait_ge(squared, sq + 1)
                nc.vector.tensor_tensor(h_lo[:, slot, :], square[:, s, :], h_hi[:, slot, :].bitcast(F32),
                                        ALU.subtract).then_inc(h_ready, 1)

            def mlp(first, unit0):
                split(first + LEAD)
                for s in range(2):
                    squares(s, s, unit0 + s + 1, sq_of(unit0 + s))
                with eng.Fori(0, 7) as j:
                    for c in range(4):
                        n = first + 1 + c + LEAD
                        lo(n % RING, j * 4 + n)
                        if c % 2 == 0:
                            for s in range(2):
                                u = unit0 + 2 + c + s
                                squares((2 + c + s) % 4, s, j * 4 + (u + 1), j * 4 + sq_of(u))
                split(first + 29 + LEAD)
                for s in range(2):
                    u = unit0 + 30 + s
                    squares(2 + s, s, u + 1, sq_of(u))
                split(first + 30 + LEAD)
                split(first + 31 + LEAD)

            def o_parts(groups):
                for g, (i, half, bank) in enumerate(groups):
                    n = g + (0 if len(groups) == 2 else 2)
                    eng.wait_ge(oT_hi, n + 1)
                    dst = slice(4 * half, 4 * half + 4), slice(i * P, (i + 1) * P)
                    nc.vector.tensor_tensor(t_lo[:, dst[0], dst[1]],
                                            wk[bank][:, :].rearrange("p (k t) -> p k t", k=4),
                                            t_hi[:, dst[0], dst[1]].bitcast(F32), ALU.subtract)\
                      .then_inc(oT_ready, 1)

            norms(0, False, True)
            split(0)
            split(1)
            for c in range(XR, V0 + 1):
                split(c + LEAD)
                if c == XR:
                    eng.wait_ge(ext_done, 1)
                    nc.vector.tensor_copy(ext, acc[0:HEADS, 0, 0:3 * P - 1]).then_inc(ext_read, 1)
                if c == XR + 1:
                    lam = lvec[:, :, 7]
                    eng.wait_ge(lru_landed, 32)
                    nc.vector.scalar_tensor_tensor(out=sp[:, 0, :], in0=lam, scalar=-1.0, in1=lam, op0=ALU.mult,
                                                   op1=ALU.min).then_inc(sp_ready, 1)
                if c == K0:
                    eng.wait_ge(sp_ready, 2)
                    link(nc.vector.tensor_scalar(sp[:, 2, :], sp[:, 1, :], 2.0, None, ALU.add))
                    link(nc.vector.reciprocal(sp[:, 2, :], sp[:, 2, :]))
                    link(nc.vector.tensor_tensor(sp[:, 1, :], sp[:, 1, :], sp[:, 2, :], ALU.mult))
                    link(nc.vector.tensor_tensor(sp[:, 2, :], sp[:, 1, :], sp[:, 1, :], ALU.mult))
                    link(nc.vector.memset(sp[:, 3, :], 1.0 / 17))
                    for odd in range(15, 0, -2):
                        link(nc.vector.tensor_tensor(sp[:, 3, :], sp[:, 3, :], sp[:, 2, :], ALU.mult))
                        link(nc.vector.tensor_scalar(sp[:, 3, :], sp[:, 3, :], 1.0 / odd, None, ALU.add))
                    link(nc.vector.tensor_tensor(sp[:, 3, :], sp[:, 3, :], sp[:, 1, :], ALU.mult))
                    link(nc.vector.tensor_scalar(sp[:, 3, :], sp[:, 3, :], 2.0 * LRU_C, None, ALU.mult))
                    link(nc.vector.tensor_scalar(sp[:, 2, :], lam, -LRU_C, 0.0, ALU.mult, ALU.max))
                    link(nc.vector.tensor_tensor(sp[:, 3, :], sp[:, 3, :], sp[:, 2, :], ALU.add))
                    nc.vector.tensor_scalar(sp[:, 4, :], sp[:, 3, :], -1.0, None, ALU.mult)
                    nc.vector.tensor_scalar(sp[:, 5, :], sp[:, 3, :], -2.0, None, ALU.mult).then_inc(sp_ready, 1)
                if c == Q0:
                    eng.wait_ge(unit_read, 2 * CT // 2)
                    for t in range(CT):
                        link(nc.vector.tensor_scalar(xc_tile(t), xr[:, t, 0:T], lvec[:, t, 0:1],
                                                     lvec[:, t, 4:5], ALU.mult, ALU.add))
                        for tap in range(1, TAPS):
                            o = nc.vector.scalar_tensor_tensor(out=xc_tile(t), in0=xr[:, t, tap:tap + T],
                                                               scalar=lvec[:, t, tap:tap + 1], in1=xc_tile(t),
                                                               op0=ALU.mult, op1=ALU.add)
                            if tap < TAPS - 1:
                                link(o)
                        o.then_inc(xc_ready, 1)
                if c == K0 + 1:
                    eng.wait_ge(lru_gates, 8)
                    link(nc.vector.tensor_tensor(pairs(ig), pairs(ig), xc, ALU.mult))
                if c == V0:
                    eng.wait_ge(decays, 3 * CT)
                    nc.vector.scalar_tensor_tensor(out=mixb[:, :, :], in0=mixb[:, :, :], scalar=1.0,
                                                   in1=rg[:, :, :], op0=ALU.add, op1=ALU.mult)\
                      .then_inc(beta2_ready, 1)

            def recurrence(s):
                if s == 0:
                    eng.wait_ge(beta_ready, 1)
                    nc.vector.tensor_tensor(ig[:, :, :], ig[:, :, :], mixb[:, :, :], ALU.mult).then_inc(lru_b, 1)
                    eng.wait_ge(lru_b, 1)
                elif s <= CT:
                    link(nc.vector.tensor_tensor_scan(xc_tile(s - 1), decay[:, s - 1, :], ig[:, s - 1, :], 0.0,
                                                      ALU.mult, ALU.add))

            eng.wait_ge(toep_landed, 32)
            pipeline(0, JOBS0, FILL0, recurrence)
            eng.wait_ge(unit_read, 2 * OUT0)
            link(nc.vector.tensor_tensor(pairs(rg), xc, pairs(mixb), ALU.mult))
            link(nc.vector.tensor_copy(t_hi[:, CT:, :], rg[:, :, :]))
            nc.vector.tensor_tensor(t_lo[:, CT:, :], rg[:, :, :], t_hi[:, CT:, :].bitcast(F32), ALU.subtract)\
              .then_inc(ob_ready, 1)
            for c in range(OUT0, OUT0 + 2):
                split(c + LEAD)
            o_parts(((0, 0, 2), (1, 0, 3)))
            for c in range(OUT0 + 2, MLP0):
                split(c + LEAD)
            norms(1, True, True)
            mlp(MLP0, UNIT_MLP0)
            norms(2, True, True)
            eng.wait_ge(nsa_landed, 48)
            link(nc.vector.tensor_copy(gw_hi[:, :, :], gw))
            nc.vector.tensor_tensor(gw_lo[:, :, :], gw, gw_hi[:, :, :].bitcast(F32), ALU.subtract)\
              .then_inc(gw_ready, 1)
            for c in range(Q1, KW):
                split(c + LEAD)

            def flatten(which):
                src = cmp_in[:, 2 * which:2 * which + 2, :]
                flat = ig[:, :, :].rearrange("p a t -> p (a t)")[:, 0:CMP_LEN * GROUPS * NC]\
                    .rearrange("p (l g n) -> p l g n", l=CMP_LEN, g=GROUPS)
                eng.wait_ge(unit_read, unit_of(KC + which, 1) + 1)
                if which == 1:
                    eng.wait_ge(flat_ready, 1)
                for g in range(GROUPS):
                    s = src[:, g, :]
                    blocks = bass.AP(s.tensor, s.offset, [list(s.ap[0]), [1, CMP_LEN], [CMP_STRIDE, NC]])
                    p = pos[:, which, :]
                    emb = bass.AP(p.tensor, p.offset, [list(p.ap[0]), [1, CMP_LEN], [0, NC]])
                    o = nc.vector.tensor_tensor(flat[:, :, g, :], blocks, emb, ALU.add)
                link(o)
                flat1 = flat.rearrange("p l g n -> p (l g n)")
                link(nc.vector.tensor_copy(flat_hi[:, which, :], flat1))
                nc.vector.tensor_tensor(flat_lo[:, which, :], flat1, flat_hi[:, which, :].bitcast(F32),
                                        ALU.subtract).then_inc(flat_ready, 1)

            def cmp_hidden(which):
                eng.wait_ge(hT_done, which + 1)
                for t in range(2):
                    src = wk[which][:, t * NPAD:t * NPAD + GROUPS * NC]
                    if which == 0:
                        o = nc.vector.tensor_copy(hkT[:, t, :], src)
                    else:
                        s4 = bass.AP(src.tensor, src.offset,
                                     [list(src.ap[0]), [NC, GROUPS], [0, PER_GROUP], [1, NC]])
                        o = nc.vector.tensor_copy(hvT[:, t, :, :, 0:NC], s4)
                o.then_inc(hT_ready, 1)

            def cmp_kv(which):
                eng.wait_ge(kv_done, which + 1)
                if which == 0:
                    nc.vector.tensor_copy(kcmp[:, :], wk[0][:, P:P + GROUPS * NC]).then_inc(kv_ready, 1)
                else:
                    nc.vector.tensor_copy(vcmp, wk[1][:, T:2 * T].rearrange("p (g d) -> p g d", g=GROUPS))\
                      .then_inc(kv_ready, 1)

            def extra(s):
                units = FILL1.get(s, [])
                for which in range(2):
                    if (KC + which, 1) in units:
                        flatten(which)
                if s == KCMP_STEP:
                    cmp_hidden(0)
                if s == KCMP_STEP + 1:
                    cmp_kv(0)

            link(nc.vector.memset(mixb[:, :, :], 0.0))
            pipeline(JOBS0, JOBS, FILL1, extra)
            cmp_hidden(1)
            cmp_kv(1)
            bias = [toep[:, :, CMP_LEN - 1:P:CMP_STRIDE], toep[:, :, P + CMP_LEN - 1::CMP_STRIDE]]
            for i in range(TT):
                n = cmp_keys(i)
                s_i = cs[:, i, :, 0:n]
                eng.wait_ge(cs_done, i + 1)
                link(nc.vector.tensor_tensor(s_i, wk[2 + i][:, 0:HEADS * 16].rearrange("p (h n) -> p h n", n=16)[:, :, 0:n],
                                             bias[i], ALU.add))
                link(nc.vector.tensor_reduce(cst[:, i, 0, :], s_i, AX.X, ALU.min))
                m = cst[:, i, 0, :]
                nc.vector.tensor_tensor(s_i, s_i, bass.AP(m.tensor, m.offset, [list(m.ap[0]), [1, HEADS], [0, n]]),
                                        ALU.subtract).then_inc(cs_ready, 1)
            for i in range(TT):
                n = cmp_keys(i)
                e_i = ce[:, i, :, 0:n]
                eng.wait_ge(ce_exp, i + 1)
                nc.vector.scalar_tensor_tensor(out=e_i, in0=bias[i], scalar=MASKED / 10, in1=e_i,
                                               op0=ALU.is_lt, op1=ALU.mult).then_inc(ce_ready, 1)
                eng.wait_ge(ce_ready, i + 1)
                link(nc.vector.tensor_reduce(cst[:, i, 1, :], e_i, AX.X, ALU.add))
                link(nc.vector.tensor_scalar(cst[:, i, 1, :], cst[:, i, 1, :], 1e-30, None, ALU.max))
                link(nc.vector.reciprocal(cst[:, i, 2, :], cst[:, i, 1, :]))
                link(nc.vector.tensor_tensor(cst[:, i, 3, :], cst[:, i, 2, :], gates[:, i, 0::3], ALU.mult))
            for i in range(TT):
                eng.wait_ge(cpT_done, i + 1)
                nc.vector.tensor_copy(cpT[:, i], acc[:, i, 0:T].rearrange("p (g t) -> p g t", g=GROUPS))\
                  .then_inc(cpT_ready, 1)
            for i in range(TT):
                eng.wait_ge(cpv_done, TT)
                for h in range(HEADS):
                    g, j = divmod(h, PER_GROUP)
                    dst = tok[:, i, h * P:(h + 1) * P]
                    at = (i * GROUPS + g) * P
                    src = (acc[:, 2, at:at + P], acc[:, 3, at:at + P], wk[2][:, at:at + P], wk[3][:, at:at + P])[j]
                    if h == 0 and i == 0:
                        eng.wait_ge(o_ready, JOBS)
                    o = nc.vector.scalar_tensor_tensor(out=dst, in0=src, scalar=cst[:, i, 3, h:h + 1], in1=dst,
                                                       op0=ALU.mult, op1=ALU.add)
                o.then_inc(oc_ready, 1)
            o_parts([(i, half, 2 * i + half) for i in range(TT) for half in range(2)])
            for c in range(OUT1, MLP1):
                split(c + LEAD)
            norms(3, True, True)
            mlp(MLP1, UNIT_MLP1)
            norms(4, True, False)

        @block.tensor
        def _(eng):
            PASSES = ((0, 0), (1, 0), (0, 1))
            t_part, w_part, h_part = (t_hi, t_lo), (w_hi, w_lo), (h_hi, h_lo)

            def group(psum, lhsT, rhs, n):
                for k in range(n):
                    for a, w in PASSES:
                        m = nc.tensor.matmul(psum, lhsT(k, a, w), rhs(k, a, w), start=k == 0 and (a, w) == (0, 0),
                                             stop=k == n - 1 and (a, w) == PASSES[-1])
                return m

            def weights(c, part):
                return w_part[part][:, c, :].rearrange("p (k n) -> p k n", k=KT)

            def up_unit(slot, half, bank):
                return group(wk[bank][:, 0:T],
                             lambda k, a, w: weights(slot, w)[:, k, half * P:(half + 1) * P],
                             lambda k, a, w: t_part[a][:, k, :], KT)

            def token_unit(slot, i, bank):
                return group(wk[bank][:, 0:T],
                             lambda k, a, w: t_part[a][:, k, i * P:(i + 1) * P],
                             lambda k, a, w: weights(slot, w)[:, k, :], KT)

            def unit(c, half):
                u = unit_of(c, half)
                if half == 0:
                    eng.wait_ge(lo_ready, c + 1)
                if u >= 2:
                    eng.wait_ge(unit_read, u - 1)
                f = token_unit if c in (V0, V0 + 1, VS, VW) else up_unit
                f(c % RING, half, half).then_inc(half_done, 1)

            def chunk(c):
                for half in range(2):
                    unit(c, half)

            def down(slot, r0, part, first, last, before_tile_1=lambda: None):
                for i in range(TT):
                    if i == 1:
                        before_tile_1()
                    for half in range(2):
                        for r in range(2):
                            for a, w in PASSES:
                                m = nc.tensor.matmul(
                                    acc[:, 2 * i + half, :],
                                    part[a][:, r0 + r, i * P:(i + 1) * P],
                                    w_part[w][:, slot, r * D + half * 512:r * D + half * 512 + 512],
                                    start=first and r == 0 and (a, w) == (0, 0),
                                    stop=last and r == 1 and (a, w) == PASSES[-1])
                    m.then_inc(half_done, 1)

            def out_chunk(c, r0, first, last, before_tile_1=lambda: None):
                eng.wait_ge(lo_ready, c + 1)
                down(c % RING, r0, t_part, first, last, before_tile_1)

            def transposed_x(b):
                for i in range(TT):
                    eng.wait_ge(xn_ready, TT * b + i + 1)
                    for half in range(2):
                        for q in range(4):
                            k = 4 * half + q
                            m = nc.tensor.transpose(wk[2 * (1 - i) + half][:, q * P:(q + 1) * P],
                                                    tok[:, i, k * P:(k + 1) * P], ident[:, :])
                        m.then_inc(xT_done, 1)
                eng.wait_ge(tT_ready, 2 * TT * (b + 1))

            def transposed_o(groups, ready, base):
                for i, half, bank in groups:
                    ready(i)
                    for q in range(4):
                        k = 4 * half + q
                        m = nc.tensor.transpose(wk[bank][:, q * P:(q + 1) * P], tok[:, i, k * P:(k + 1) * P],
                                                ident[:, :])
                    m.then_inc(oT_done, 1)

            def scores(k):
                head, d, p0, qs, ks, v0 = job(k)
                if k == 0:
                    eng.wait_ge(unit_read, unit_of(K0 + 1, 1) + 1)
                if k >= 2:
                    eng.wait_ge(sneg_ready, k - 1)
                bank = wk[2 + k % 2]
                q, kk = qT[p0:p0 + d, qs, :], kT[p0:p0 + d, ks, :]
                nc.tensor.matmul(bank[:, 0:P], q[:, 0:P], kk[:, 0:P], start=True, stop=True)
                nc.tensor.matmul(bank[:, P:3 * P], q[:, P:T], kk, start=True, stop=True).then_inc(scores_done, 1)

            def turn(k):
                eng.wait_ge(exp_done, k + 1)
                if k >= 2:
                    eng.wait_ge(pT_ready, k - 1)
                for n in range(3):
                    m = nc.tensor.transpose(acc[:, k % 2, n * P:(n + 1) * P], prob[:, k % 2, n * P:(n + 1) * P],
                                            ident[:, :])
                m.then_inc(pT_done, 1)

            def values(k):
                head, d, p0, qs, ks, v0 = job(k)
                eng.wait_ge(pT_ready, k + 1)
                if k < JOBS0:
                    eng.wait_ge(unit_read, unit_of(V0 + k // 4, 1) + 1)
                if k >= 2:
                    eng.wait_ge(o_ready, k - 1)
                bank = acc[:, 2 + k % 2, :]
                pt = pT[:, k % 2, :]
                nc.tensor.matmul(bank[:, 0:d], pt[:, 0:P], v[:, 0, v0:v0 + d], start=True, stop=True)
                nc.tensor.matmul(bank[:, T:T + d], pt[:, P:2 * P], v[:, 0, v0:v0 + d], start=True, stop=False)
                nc.tensor.matmul(bank[:, T:T + d], pt[:, 2 * P:3 * P], v[:, 1, v0:v0 + d], start=False, stop=True)\
                  .then_inc(pv_done, 1)

            def pipeline(first, last, fill, filler, extra):
                for s in range(first, last + 2):
                    if s < last:
                        scores(s)
                    if first <= s - 1 < last:
                        turn(s - 1)
                    if first <= s - 2 < last:
                        values(s - 2)
                    for c, half in fill.get(s, []):
                        filler(c, half)
                    extra(s)

            def cmp_unit(c, half):
                if c < CMPK:
                    return unit(c, half)
                which, at = divmod(c - CMPK, 4)
                if half == 0:
                    eng.wait_ge(lo_ready, c + 1)
                if at == 0 and half == 0:
                    eng.wait_ge(flat_ready, which + 1)
                    eng.wait_ge(unit_read, unit_of(VC, 1) + 1)
                for q in range(4):
                    place = 8 * at + 4 * half + q
                    for a, w in PASSES:
                        m = nc.tensor.matmul(wk[which][0:GROUPS * NC, 0:CMP_HIDDEN],
                                             (flat_hi, flat_lo)[a][:, which, place * GROUPS * NC:(place + 1) * GROUPS * NC],
                                             weights(c % RING, w)[:, 4 * half + q, :],
                                             start=place == 0 and (a, w) == (0, 0),
                                             stop=place == CMP_LEN - 1 and (a, w) == PASSES[-1])
                m.then_inc(half_done, 1)

            def hidden_turned(which):
                eng.wait_ge(cmp_gelu, which + 1)
                for t in range(2):
                    m = nc.tensor.transpose(wk[which][:, t * NPAD:t * NPAD + GROUPS * NC],
                                            hidden[0:GROUPS * NC, which, t * P:(t + 1) * P],
                                            ident[0:GROUPS * NC, 0:GROUPS * NC])
                m.then_inc(hT_done, 1)

            def compressed(which):
                eng.wait_ge(hT_ready, which + 1)
                if which == 0:
                    for t in range(2):
                        m = nc.tensor.matmul(wk[0][:, P:P + GROUPS * NC], w2[:, 0, t, :], hkT[:, t, :],
                                             start=t == 0, stop=t == 1)
                else:
                    for g in range(GROUPS):
                        for t in range(2):
                            m = nc.tensor.matmul(wk[1][:, T + g * P:T + (g + 1) * P],
                                                 hvT[:, t, g, :, :].rearrange("p j n -> p (j n)"),
                                                 w2[:, 1, t, :], start=t == 0, stop=t == 1)
                m.then_inc(kv_done, 1)

            def mlp(first, unit0):
                def up(c, u, slot):
                    eng.wait_ge(lo_ready, c + 1)
                    for s in range(2):
                        eng.wait_ge(unit_read, u + (s - 1))
                        up_unit(slot, s, s).then_inc(half_done, 1)

                def dn(c, slot, h0, ready, first_sum, last_sum):
                    eng.wait_ge(lo_ready, c + 1)
                    eng.wait_ge(h_ready, ready)
                    down(slot, h0, h_part, first_sum, last_sum)

                def body(j4, first_sum):
                    for c in range(0, 4, 2):
                        n = first + 1 + c
                        up(j4 + n, j4 + (unit0 + 2 + c), n % RING)
                        dn(j4 + (n + 1), (n + 1) % RING, c, j4 + (sq_of(unit0) + c + 2),
                           first_sum and c == 0, False)

                up(first, unit0, first % RING)
                body(0, True)
                with eng.Fori(1, 7) as j:
                    body(j * 4, False)
                n = first + 29
                up(n, unit0 + 30, n % RING)
                dn(n + 1, (n + 1) % RING, 0, sq_of(unit0) + 30, False, False)
                dn(n + 2, (n + 2) % RING, 2, sq_of(unit0) + 32, False, True)

            eng.wait_ge(small_landed, 16)
            transposed_x(0)
            chunk(XR)
            eng.wait_ge(table_landed, 32)
            nc.tensor.matmul(acc[0:HEADS, 0, 0:3 * P - 1], table[:, :], select, start=True, stop=True)\
              .then_inc(ext_done, 1)
            for c in range(XR + 1, K0 + 1):
                chunk(c)
            eng.wait_ge(xc_ready, CT)
            eng.wait_ge(lru_landed, 32)
            eng.wait_ge(ext_read, 1)
            for t in range(CT):
                for w in range(2):
                    m = nc.tensor.matmul(acc[:, t, w * T:(w + 1) * T], lgate[:, w, t, :], xc_tile(t),
                                         start=True, stop=True)
            m.then_inc(lru_gates_done, 1)
            for c in range(K0 + 1, V0 + 1):
                chunk(c)
            eng.wait_ge(lru_gates, 8)
            pipeline(0, JOBS0, FILL0, unit, lambda s: None)
            eng.wait_ge(ob_ready, 1)
            eng.wait_ge(pT_ready, JOBS0)
            out_chunk(OUT0, CT, True, False, lambda: eng.wait_ge(o_ready, JOBS0))
            transposed_o(((0, 0, 2), (1, 0, 3)), lambda i: None, 0)
            out_chunk(OUT0 + 1, CT + 2, False, False)
            eng.wait_ge(oT_ready, 2)
            out_chunk(OUT0 + 2, 0, False, False)
            out_chunk(OUT0 + 3, 2, False, True)
            transposed_x(1)
            mlp(MLP0, UNIT_MLP0)
            transposed_x(2)
            for c in range(Q1, KW):
                chunk(c)
            eng.wait_ge(gw_ready, 1)
            for i in range(TT):
                group(wk[2 + i][:, 0:3 * HEADS], lambda k, a, w: t_part[a][:, k, i * P:(i + 1) * P],
                      lambda k, a, w: (gw_hi, gw_lo)[w][:, k, :], KT).then_inc(gates_done, 1)
            eng.wait_ge(unit_read, unit_of(VS, 1) + 1)
            eng.wait_ge(gates_ready, TT)

            def extra(s):
                if s == KCMP_STEP:
                    hidden_turned(0)
                if s == KCMP_STEP + 1:
                    compressed(0)

            def filler(c, half):
                cmp_unit(c, half)

            pipeline(JOBS0, JOBS, FILL1, filler, extra)
            hidden_turned(1)
            eng.wait_ge(kv_ready, 1)
            eng.wait_ge(sneg_ready, JOBS)
            for i in range(TT):
                for h in range(HEADS):
                    g = h // PER_GROUP
                    m = nc.tensor.matmul(wk[2 + i][:, h * 16:h * 16 + NC], qT[:, h, i * P:(i + 1) * P],
                                         kcmp[:, g * NC:(g + 1) * NC], start=True, stop=True)
                m.then_inc(cs_done, 1)
            compressed(1)
            for i in range(TT):
                eng.wait_ge(ce_ready, i + 1)
                eng.wait_ge(pT_ready, JOBS)
                for g in range(GROUPS):
                    m = nc.tensor.transpose(acc[:, i, g * P:(g + 1) * P],
                                            ce[:, i, g * PER_GROUP:(g + 1) * PER_GROUP, :].rearrange("p h n -> p (h n)"),
                                            ident[:, :])
                m.then_inc(cpT_done, 1)
            eng.wait_ge(kv_ready, 2)
            eng.wait_ge(o_ready, JOBS)
            eng.wait_ge(cs_ready, TT)
            for i in range(TT):
                eng.wait_ge(cpT_ready, i + 1)
                for g in range(GROUPS):
                    at = (i * GROUPS + g) * P
                    for j in range(PER_GROUP):
                        dst = (acc[:, 2, at:at + P], acc[:, 3, at:at + P], wk[2][:, at:at + P], wk[3][:, at:at + P])[j]
                        rows = slice(j * NPAD, (j + 1) * NPAD)
                        m = nc.tensor.matmul(dst, cpT[rows, i, g, :], vcmp[rows, g, :], start=True, stop=True)
                m.then_inc(cpv_done, 1)
            transposed_o([(i, half, 2 * i + half) for i in range(TT) for half in range(2)],
                         lambda i: eng.wait_ge(oc_ready, i + 1), 2)
            eng.wait_ge(oT_ready, 6)
            for c in range(4):
                out_chunk(OUT1 + c, 2 * c, c == 0, c == 3)
            transposed_x(3)
            mlp(MLP1, UNIT_MLP1)


def bucket_rows():
    exact = BUCKETS // 2
    rows = np.zeros((BUCKETS + 1, 3 * P - 1), np.float32)
    for j in range(3 * P - 1):
        n = T - 1 - j
        if n < 0:
            rows[BUCKETS, j] = MASKED
        elif n < exact:
            rows[n, j] = -1.0
        else:
            large = exact + int(math.log(n / exact) / math.log(128 / exact) * (BUCKETS - exact))
            rows[min(large, BUCKETS - 1), j] = -1.0
    return rows


def columns(w):
    k, n = w.shape
    return w.reshape(k // P, P, n // 256, 256).transpose(2, 1, 0, 3).reshape(n // 256, P, -1)


def rows(w):
    return w.reshape(-1, 2, P, D).transpose(0, 2, 1, 3).reshape(-1, P, 2 * D)


def places(w):
    return w.reshape(-1, 8, P, CMP_HIDDEN).transpose(0, 2, 1, 3).reshape(-1, P, CHUNK)


def kernel(**inputs):
    import concourse.bacc as bacc
    from concourse.bass_utils import run_bass_kernel_spmd

    a = {k: np.asarray(v) for k, v in inputs.items()}
    dq = HEADS * DH_A
    w_in, c_in, w_o = a["ab_w_in"][0], a["c_w_in"][0], a["ab_w_out"][0]
    part = lambda lo, n: columns(w_in[:, lo:lo + n])

    def mlp_stream(layer):
        up, down = columns(a["w_up"][layer]), rows(a["w_down"][layer])
        order = [up[0]]
        for c in range(15):
            order += [up[c + 1], down[c]]
        return np.stack(order + [down[15]])

    def c_part(j):
        lo = HEADS * DH_C + j * GROUPS * DH_C
        return columns(c_in[:, lo:lo + GROUPS * DH_C])

    stream = np.concatenate([
        part(3 * dq, W), part(0, dq), part(dq, dq), part(2 * dq, dq), part(3 * dq + W, W),
        rows(w_o[dq:]), rows(w_o[:dq]), mlp_stream(0),
        columns(c_in[:, :HEADS * DH_C]), c_part(2), c_part(3), c_part(4), c_part(5), c_part(0), c_part(1),
        places(a["c_cmp_k_w1"][0]), places(a["c_cmp_v_w1"][0]), rows(a["c_w_out"][0]), mlp_stream(1)])
    assert stream.shape == (CHUNKS, P, CHUNK)
    gains = np.stack([a[n][layer] for layer in range(2)
                      for n in ("norm_mix_pre", "norm_mix_post", "norm_mlp_pre", "norm_mlp_post")])
    lru_vec = np.stack([*a["ab_conv_w"][0], a["ab_conv_b"][0], a["ab_b_rg"][0], a["ab_b_ig"][0],
                        a["ab_lru_lambda"][0]], axis=1).reshape(CT, P, 8).transpose(1, 0, 2)
    lru_gate = np.zeros((P, 2, CT, P), np.float32)
    for w, name in enumerate(("ab_w_rg", "ab_w_ig")):
        for b in range(8):
            r = (b % 2) * 64
            lru_gate[r:r + 64, w, b // 2, r:r + 64] = a[name][0, b]
    fed = {
        "x_in": a["x"][0], "w_stream": stream, "gains": gains, "lru_vec": lru_vec, "lru_gate": lru_gate,
        "rel_bias": a["rel_bias"], "bias_select": bucket_rows(), "ident_in": np.eye(P, dtype=np.float32),
        "gate_w": c_in[:, -3 * HEADS:].reshape(KT, P, 3 * HEADS).transpose(1, 0, 2),
        "cmp_pos": np.stack([a["c_cmp_pos_k"][0].T, a["c_cmp_pos_v"][0].T], axis=1),
        "cmp_w2": np.stack([a[n][0].reshape(2, P, P).transpose(1, 0, 2) for n in ("c_cmp_k_w2", "c_cmp_v_w2")],
                           axis=1),
    }
    nc = bacc.Bacc("TRN2", target_bir_lowering=False, num_devices=1)
    arrays, args = {}, []
    for name, value in fed.items():
        value = np.ascontiguousarray(value)
        arrays[name] = value
        args.append(nc.dram_tensor(name, value.shape, mybir.dt.from_np(value.dtype), kind="ExternalInput").ap())
    out = nc.dram_tensor("out", [T, D], F32, kind="ExternalOutput").ap()
    trunk(nc, *args, out)
    r = run_bass_kernel_spmd(nc, [arrays], core_ids=[0])
    return r.results[0]["out"].reshape(1, T, D)
```

```python
import math
from contextlib import ExitStack

import numpy as np

import concourse.bass as bass
from concourse import mybir

F32 = mybir.dt.float32
F32R = mybir.dt.float32r
ALU = mybir.AluOpType
ACT = mybir.ActivationFunctionType
AX = mybir.AxisListType

P = 128
T = 256
TT = T // P
D = 1024
KT = D // P
FF = 4096
HEADS = 8
EPS = 1e-6
MASKED = 1e30
CHUNK = 2048
RING = 4
LEAD = 2

W = 512
CT = W // P
TAPS = 4
LRU_C = 8.0
DH_A = 64
DH_C = 128
GROUPS = 2
PER_GROUP = HEADS // GROUPS
CMP_LEN = 32
CMP_STRIDE = 16
NC = (T - CMP_LEN) // CMP_STRIDE + 1
CMP_HIDDEN = 256
NPAD = 32
BUCKETS = 32

V0, XR, QA, KA, QB, KB, GR, OUT0 = 0, 2, 4, 5, 6, 7, 8, 10
MLP0 = 14
MLP_CHUNKS = 32
Q1 = MLP0 + MLP_CHUNKS
VS, VW, QS_A, KS, QS_B, KC, QS_C, VC, QS_D, KW = range(Q1, Q1 + 10)
QS = (QS_A, QS_B, QS_C, QS_D)
CMPK, CMPV, OUT1 = Q1 + 10, Q1 + 14, Q1 + 18
MLP1 = OUT1 + 4
CHUNKS = MLP1 + MLP_CHUNKS
UNIT_MLP0 = 2 * OUT0
UNIT_Q1 = UNIT_MLP0 + 2 * (MLP_CHUNKS // 2)
UNIT_MLP1 = UNIT_Q1 + 2 * (CMPK - Q1)
JOBS0 = HEADS
JOBS = 3 * HEADS


def unit_of(chunk, half):
    return (2 * chunk if chunk < MLP0 else UNIT_Q1 + 2 * (chunk - Q1)) + half


OPENS = {0: V0, 2: VS}
LAST_OF_BRANCH = {1: MLP0 - 1, 2: Q1 - 1, 3: MLP1 - 1, 4: CHUNKS - 1}


def last_chunk(k):
    if k < HEADS:
        return KA if k < HEADS // 2 else KB
    head = k - HEADS
    return max(KS, QS[head // 2]) if head < HEADS else KW


def sq_of(u):
    return u - UNIT_MLP0 if u < UNIT_Q1 else MLP_CHUNKS + u - UNIT_MLP1


def cmp_keys(i):
    return ((i + 1) * P - CMP_LEN) // CMP_STRIDE + 1


def spread(units, first, steps):
    cuts = [math.ceil(n * len(units) / steps) for n in range(steps + 1)]
    return {first + n: units[cuts[n]:cuts[n + 1]] for n in range(steps)}


def both_halves(chunks):
    return [(c, half) for c in chunks for half in range(2)]


FILL0 = spread(both_halves(range(QB, OUT0)), 0, 7)
FILL1 = spread(both_halves(range(QS_B, OUT1)), HEADS, 2 * HEADS - 2)
KCMP_STEP, VCMP_STEP = (1 + next(s for s, units in FILL1.items() if (c, 1) in units) for c in (CMPK + 3, CMPV + 3))


def trunk(nc, x_in, w_stream, gains, lru_vec, lru_gate, rel_bias, bias_select, ident_in, gate_w,
          cmp_pos, cmp_w2, out):
    with ExitStack() as ctx:
        def sb(name, shape, dt=F32):
            return ctx.enter_context(nc.sbuf_tensor(name, shape, dt))

        def sem(name):
            return ctx.enter_context(nc.semaphore(name))

        raw = sb("raw", [P, RING, CHUNK])
        w_hi = sb("w_hi", [P, RING, CHUNK], F32R)
        w_lo = sb("w_lo", [P, RING, CHUNK], F32R)
        x = sb("x", [P, TT, D])
        tok = sb("tok", [P, TT, D])
        t_hi = sb("t_hi", [P, KT, T], F32R)
        t_lo = sb("t_lo", [P, KT, T], F32R)
        gain = sb("gain", [P, 2, D])
        toep = sb("toep", [P, HEADS, 3 * P])
        qT = sb("qT", [P, HEADS, T])
        kT = sb("kT", [P, 4, T])
        v = sb("v", [P, TT, W])
        xr = sb("xr", [P, CT, T + TAPS - 1])
        xc = tok[:, :, W:]
        decay = qT[:, CT:, :]

        def xc_tile(t):
            return xc[:, t // 2, (t % 2) * T:(t % 2 + 1) * T]

        def pairs(buf):
            return buf[:, :, :].rearrange("p (a b) t -> p a (b t)", a=2)

        rg = sb("rg", [P, CT, T])
        ig = sb("ig", [P, CT, T])
        lgate = ig[:, :, :].rearrange("p a t -> p (a t)").rearrange("p (w t n) -> p w t n", w=2, t=CT)
        mixb = sb("mixb", [P, CT, T])
        relu, square = rg[:, 0:2, :], rg[:, 2:4, :]
        cmp_in = rg
        hidden = xr[:, :, :].rearrange("p a t -> p (a t)")[:, 0:2 * CMP_HIDDEN].rearrange("p (w n) -> p w n", w=2)
        hvT = mixb[:, 0:2, :].rearrange("p t (g j n) -> p t g j n", g=GROUPS, j=PER_GROUP)
        ce = mixb[:, 2:4, :].rearrange("p i (h n) -> p i h n", h=HEADS)
        flat = sb("flat", [P, 2, CMP_LEN, 2, GROUPS * NC], F32R)
        h_flat = flat[:, :, :, :, :].rearrange("p w l a n -> p (w l a n)")[:, 0:8 * T]
        h_hi, h_lo = (h_flat[:, n * 4 * T:(n + 1) * 4 * T].rearrange("p (s t) -> p s t", s=4) for n in range(2))
        sneg = sb("sneg", [P, 2, 3 * P])
        prob = sb("prob", [P, 2, 3 * P])
        diag = prob[:, :, 0:P]
        junk = sneg[:, :, :].rearrange("p a n -> p (a n)").bitcast(mybir.dt.bfloat16)[:, 0:D]
        pT = sb("pT", [P, 2, 3 * P])
        rg_flat = rg[:, :, :].rearrange("p a t -> p (a t)")
        cs = rg_flat[:, 0:T].rearrange("p (i h n) -> p i h n", i=TT, h=HEADS)
        halves_sum = rg_flat[0:2 * GROUPS * NC, 3 * T:3 * T + GROUPS * NC]
        cpT = rg_flat[:, T:3 * T].rearrange("p (i g t) -> p i g t", i=TT, g=GROUPS)
        mneg = sb("mneg", [P, 2 * JOBS])
        sums = sb("sums", [P, 2 * JOBS])
        coef = sb("coef", [P, 2 * JOBS])
        stat = sb("stat", [P, 2, 4, 4 * TT])
        lvec = sb("lvec", [P, CT, 8])
        sp = sb("sp", [P, 6, CT])
        ident = sb("ident", [P, P])
        one_root = sb("one_root", [P, 1])
        table = sb("table", [BUCKETS + 1, HEADS])
        select = decay[0:BUCKETS + 1, 0:2, :].rearrange("p a t -> p (a t)")[:, 0:3 * P - 1]
        ext = mixb[0:HEADS, 0:2, :].rearrange("p a t -> p (a t)")[:, 0:3 * P - 1]
        xr_flat, ig_flat = (b[:, :, :].rearrange("p a t -> p (a t)") for b in (xr, ig))
        w2 = xr_flat[:, 2 * CMP_HIDDEN:2 * CMP_HIDDEN + 4 * P].rearrange("p (w t n) -> p w t n", w=2, t=2)
        gw = ig_flat[:, 0:KT * 3 * HEADS].rearrange("p (k n) -> p k n", k=KT)
        pos = ig_flat[:, CMP_LEN * GROUPS * NC:CMP_LEN * (GROUPS * NC + 2)].rearrange("p (w l) -> p w l", w=2)
        gw_hi = sb("gw_hi", [P, KT, 3 * HEADS], F32R)
        gw_lo = sb("gw_lo", [P, KT, 3 * HEADS], F32R)
        gates = sb("gates", [P, TT, 3 * HEADS])
        hkT = sb("hkT", [P, 2, GROUPS * NC])
        kcmp = lvec[:, :, :].rearrange("p t v -> p (t v)")[:, 0:GROUPS * NC]
        vcmp = ig_flat.rearrange("p (g n) -> p g n", g=GROUPS)
        cst = sb("cst", [P, TT, 4, HEADS])
        acc = ctx.enter_context(nc.psum_tensor("acc", [P, 4, 512], F32))
        wk = [ctx.enter_context(nc.psum_tensor(f"wk{i}", [P, 512], F32)) for i in range(4)]
        ext_dram = nc.dram_tensor("bias_rows", [HEADS, P, 3 * P - 1], F32, kind="Internal").ap()

        landed = [sem(f"landed{i}") for i in range(RING)]
        hi_ready, lo_ready = sem("hi_ready"), sem("lo_ready")
        half_done = sem("half_done")
        x_landed = [sem("x_landed0"), sem("x_landed1")]
        gain_landed = [sem("gain_post_landed"), sem("gain_pre_landed")]
        lru_landed, nsa_landed, small_landed, table_landed = (sem("lru_landed"), sem("nsa_landed"), sem("ident_landed"),
                                                              sem("table_landed"))
        ext_stored, toep_landed, out_stored = sem("ext_stored"), sem("toep_landed"), sem("out_stored")
        cleared, table_one, zeros = sem("cleared"), sem("table_one"), sem("zeros")
        ext_done, ext_read = sem("ext_done"), sem("ext_read")
        unit_done, unit_read = sem("unit_done"), sem("unit_read")
        post_sq, post_mul, post_std, x_ready = sem("post_sq"), sem("post_mul"), sem("post_std"), sem("x_ready")
        pre_std, xn_ready = sem("pre_std"), sem("xn_ready")
        xT_done, tT_hi, tT_ready = sem("xT_done"), sem("tT_hi"), sem("tT_ready")
        relu_ready, squared, h_ready = sem("relu_ready"), sem("squared"), sem("h_ready")
        sp_ready, xc_ready = sem("sp_ready"), sem("xc_ready")
        lru_gates_done, lru_gates = sem("lru_gates_done"), sem("lru_gates")
        decays, beta2_ready, beta_ready, ob_ready = sem("decays"), sem("beta2_ready"), sem("beta_ready"), sem("ob_ready")
        lru_b = sem("lru_b")
        scores_done, sneg_ready, exp_done = sem("scores_done"), sem("sneg_ready"), sem("exp_done")
        pT_done, pT_ready, pv_done, o_ready = sem("pT_done"), sem("pT_ready"), sem("pv_done"), sem("o_ready")
        gw_ready, gates_done, gates_ready = sem("gw_ready"), sem("gates_done"), sem("gates_ready")
        flat_ready, cmp_product = sem("flat_ready"), sem("cmp_product")
        hT_done, hT_ready, kv_done, kv_ready = sem("hT_done"), sem("hT_ready"), sem("kv_done"), sem("kv_ready")
        cs_done, cs_ready, ce_exp, ce_ready = sem("cs_done"), sem("cs_ready"), sem("ce_exp"), sem("ce_ready")
        cpT_done, cpT_ready, cpv_done = sem("cpT_done"), sem("cpT_ready"), sem("cpv_done")
        oc_ready = sem("oc_ready")
        oT_done, oT_hi, oT_ready = sem("oT_done"), sem("oT_hi"), sem("oT_ready")
        gelu_ready = sem("gelu_ready")
        act_step, dve_step = sem("act_step"), sem("dve_step")

        def unit_bank(c, half):
            return acc[:, half, :] if c - 1 in OPENS.values() else wk[half]

        def job(k):
            if k < JOBS0:
                return k, DH_A, (k % 2) * DH_A, k // 2, k // 2, k * DH_A
            branch, head = divmod(k - JOBS0, HEADS)
            g = head // PER_GROUP
            return head, DH_C, 0, head, GROUPS * branch + g, (GROUPS * branch + g) * DH_C

        block = ctx.enter_context(nc.Block())

        @block.sync
        def _(eng):
            def load_x(i):
                eng.dma_start(x[:, i, :], x_in[i * P:(i + 1) * P, :]).then_inc(x_landed[i], 16)

            def load_chunk(c):
                eng.dma_start(raw[:, c, :], w_stream[c]).then_inc(landed[c], 16)

            load_x(0)
            eng.dma_start(ident[:, :], ident_in).then_inc(small_landed, 16)
            load_chunk(0)
            load_x(1)
            for c in range(1, RING):
                load_chunk(c)
            with eng.Fori(0, CHUNKS // RING - 1) as j:
                for c in range(RING):
                    eng.wait_ge(lo_ready, j * RING + (c + 1))
                    eng.dma_start(raw[:, c, :], w_stream[bass.ds(j * RING + (RING + c), 1)]
                                  .rearrange("o p f -> (o p) f")).then_inc(landed[c], 16)
            for i in range(TT):
                for half in range(2):
                    cols = slice(half * 512, (half + 1) * 512)
                    eng.wait_ge(x_ready, 2 * (3 * TT + i) + half + 1)
                    eng.dma_start(out[i * P:(i + 1) * P, cols], x[:, i, cols]).then_inc(out_stored, 16)
            eng.wait_ge(out_stored, 32 * TT)

        @block.gpsimd
        def _(eng):
            def load_gain(which, row):
                eng.dma_start(gain[:, which, :], bass.AP(gains.tensor, row * D, [[0, P], [1, D]]))\
                   .then_inc(gain_landed[which], 16)

            load_gain(1, 0)
            eng.memset(table[:, :], 1.0).then_inc(table_one, 1)
            eng.wait_ge(table_one, 1)
            eng.dma_start(table[0:BUCKETS, :], rel_bias).then_inc(table_landed, 16)
            eng.dma_start(select, bias_select).then_inc(table_landed, 16)
            eng.dma_start(lvec[:, :, :], lru_vec).then_inc(lru_landed, 16)
            eng.dma_start(lgate, lru_gate).then_inc(lru_landed, 16)
            eng.memset(xr[:, :, 0:TAPS - 1], 0.0).then_inc(cleared, 1)
            eng.wait_ge(ext_read, 1)
            eng.dma_start(ext_dram, bass.AP(ext.tensor, ext.offset, [list(ext.ap[0]), [0, P], list(ext.ap[1])]))\
               .then_inc(ext_stored, 16)
            eng.wait_ge(ext_stored, 16)
            rows = 3 * P - 1
            for at, m0, n in ((0, P, P), (P, 0, 2 * P)):
                eng.dma_start(toep[:, :, at:at + n],
                              bass.AP(ext_dram.tensor, m0 + P - 1, [[rows - 1, P], [P * rows, HEADS], [1, n]]))\
                   .then_inc(toep_landed, 16)
            load_gain(0, 1)
            eng.wait_ge(ob_ready, 2)
            eng.dma_start(gw, gate_w).then_inc(nsa_landed, 16)
            eng.dma_start(pos, cmp_pos).then_inc(nsa_landed, 16)
            eng.dma_start(w2, cmp_w2).then_inc(nsa_landed, 16)
            for b in range(1, 4):
                eng.wait_ge(xn_ready, TT * b)
                load_gain(1, 2 * b)
                eng.wait_ge(x_ready, 2 * TT * b)
                load_gain(0, 2 * b + 1)

        @block.scalar
        def _(eng):
            def hi(c, load, used):
                eng.wait_ge(landed[c], load)
                if used is not None:
                    eng.wait_ge(half_done, used)
                nc.scalar.activation(w_hi[:, c, :], raw[:, c, :], ACT.Copy).then_inc(hi_ready, 1)

            def split(n):
                if n < CHUNKS:
                    hi(n % RING, 16 * (n // RING + 1), 2 * (n - RING + 1) if n >= RING else None)

            steps = [0]

            def link(ins):
                steps[0] += 1
                ins.then_inc(act_step, 1)
                eng.wait_ge(act_step, steps[0])

            def post(b, i):
                k, last = TT * (b - 1) + i, LAST_OF_BRANCH[b]
                first, second, share, std = (stat[:, 0, q, k:k + 1] for q in range(4))
                eng.wait_ge(half_done, 2 * last - 1 if i == 0 else 2 * last + 2)
                nc.scalar.activation(junk[:, 0:512], acc[:, 2 * i, :], ACT.Square, accum_out=first)\
                  .then_inc(post_sq, 1)
                eng.wait_ge(post_sq, k + 1)
                link(nc.scalar.activation(share, first, ACT.Copy, scale=1.0 / D, bias=EPS))
                eng.wait_ge(post_mul, k + 1)
                link(nc.scalar.activation(junk[:, 512:], acc[:, 2 * i + 1, :], ACT.Square, accum_out=second))
                nc.scalar.activation(std, second, ACT.Sqrt, scale=1.0 / D, bias=share).then_inc(post_std, 1)

            def pre(b, i):
                k = TT * b + i
                first, second, share, std = (stat[:, 1, q, k:k + 1] for q in range(4))
                for half in range(2):
                    cols = slice(half * 512, (half + 1) * 512)
                    if b == 0:
                        eng.wait_ge(x_landed[i], 16)
                    else:
                        eng.wait_ge(x_ready, 2 * (TT * (b - 1) + i) + half + 1)
                    link(nc.scalar.activation(junk[:, cols], x[:, i, cols], ACT.Square,
                                              accum_out=(first, second)[half]))
                    if half == 0:
                        link(nc.scalar.activation(share, first, ACT.Copy, scale=1.0 / D, bias=EPS))
                nc.scalar.activation(std, second, ACT.Sqrt, scale=1.0 / D, bias=share).then_inc(pre_std, 1)

            def turned(b, i):
                for half in range(2):
                    eng.wait_ge(xT_done, 2 * (TT * b + i) + half + 1)
                    nc.scalar.activation(t_hi[:, 4 * half:4 * half + 4, i * P:(i + 1) * P],
                                         wk[2 + half][:, :].rearrange("p (k t) -> p k t", k=4),
                                         ACT.Copy).then_inc(tT_hi, 1)

            def boundary(b):
                post(b, 0)
                pre(b, 0)
                post(b, 1)
                turned(b, 0)
                pre(b, 1)
                turned(b, 1)

            def evacuate(c, half):
                u = unit_of(c, half)
                src = unit_bank(c, half)[:, 0:T]
                func, scale = ACT.Copy, 1.0
                if c in (V0, V0 + 1):
                    dst = v[:, half, T * (c - V0):T * (c - V0 + 1)]
                elif c in (XR, XR + 1):
                    dst = xr[:, 2 * (c - XR) + half, TAPS - 1:]
                    if c == XR and half == 0:
                        eng.wait_ge(cleared, 1)
                elif c in (QA, QB):
                    dst, scale = qT[:, c - QA + half, :], -DH_A ** -0.5
                elif c in (KA, KB):
                    dst = kT[:, c - KA + half, :]
                elif c in (GR, GR + 1):
                    dst = xr[:, 2 * (c - GR) + half, 0:T]
                elif c in QS:
                    dst, scale = qT[:, 2 * QS.index(c) + half, :], -DH_C ** -0.5
                elif c in (KS, KW):
                    dst = kT[:, (0 if c == KS else GROUPS) + half, :]
                elif c in (VS, VW):
                    dst = v[:, half, T * (c - VS):T * (c - VS + 1)]
                else:
                    dst = cmp_in[:, (0 if c == KC else 2) + half, :]
                eng.wait_ge(half_done, 2 * c + half + 1)
                nc.scalar.activation(dst, src, func, scale=scale).then_inc(unit_read, 1)

            def exps(k):
                eng.wait_ge(sneg_ready, k + 1)
                if k >= 2:
                    eng.wait_ge(pT_done, k - 1)
                for i, (a, n) in enumerate(((0, P), (P, 2 * P))):
                    e = nc.scalar.activation(prob[:, k % 2, a:a + n], sneg[:, k % 2, a:a + n], ACT.Exp,
                                             scale=-1.0, bias=mneg[:, 2 * k + i:2 * k + i + 1],
                                             accum_out=sums[:, 2 * k + i:2 * k + i + 1])
                e.then_inc(exp_done, 1)

            def mlp(first, unit0):
                def relus(c, u, j4=0):
                    for s in range(2):
                        eng.wait_ge(half_done, j4 * 2 + (2 * c + s + 1))
                        if sq_of(u) >= 2:
                            eng.wait_ge(squared, j4 + (sq_of(u) + s - 1))
                        nc.scalar.activation(relu[:, s, :], wk[s][:, 0:T], ACT.Relu).then_inc(unit_read, 1)

                split(first + LEAD)
                relus(first, unit0)
                with eng.Fori(0, 7) as j:
                    for c in range(4):
                        n = first + 1 + c + LEAD
                        hi(n % RING, j * 16 + 16 * (n // RING + 1), j * 8 + 2 * (n - RING + 1))
                        if c % 2 == 0:
                            relus(first + 1 + c, unit0 + 2 + c, j * 4)
                split(first + 29 + LEAD)
                relus(first + 29, unit0 + 30)
                split(first + 30 + LEAD)
                split(first + 31 + LEAD)

            def o_parts(before, groups):
                for n, (i, half, bank) in enumerate(groups, before):
                    eng.wait_ge(oT_done, n + 1)
                    nc.scalar.activation(t_hi[:, 4 * half:4 * half + 4, i * P:(i + 1) * P],
                                         wk[bank][:, :].rearrange("p (k t) -> p k t", k=4),
                                         ACT.Copy).then_inc(oT_hi, 1)

            def load_sqrt():
                link(nc.scalar.activation(one_root[BUCKETS:BUCKETS + 1, :], table[BUCKETS:BUCKETS + 1, 0:1], ACT.Sqrt))

            eng.wait_ge(table_one, 1)
            load_sqrt()
            pre(0, 0)
            split(0)
            turned(0, 0)
            pre(0, 1)
            split(1)
            turned(0, 1)
            for c in range(V0, QB):
                split(c + LEAD)
                if c == V0 + 1:
                    eng.wait_ge(sp_ready, 1)
                    nc.scalar.activation(sp[:, 1, :], sp[:, 0, :], ACT.Exp).then_inc(sp_ready, 1)
                for half in range(2):
                    evacuate(c, half)

            def lru(s):
                if s == 0:
                    eng.wait_ge(lru_gates_done, 1)
                    for w in range(2):
                        for t in range(CT):
                            nc.scalar.activation((rg, ig)[w][:, t, :], acc[:, t, w * T:(w + 1) * T],
                                                 ACT.Sigmoid, bias=lvec[:, t, 5 + w:6 + w]).then_inc(lru_gates, 1)
                if s in (1, 2):
                    if s == 1:
                        eng.wait_ge(lru_gates, 8)
                        eng.wait_ge(sp_ready, 3)
                        eng.wait_ge(ext_stored, 16)
                    for t in range(CT):
                        nc.scalar.activation((decay, mixb)[s - 1][:, t, :], rg[:, t, :], ACT.Exp,
                                             scale=sp[:, 3 + s, t:t + 1]).then_inc(decays, 1)
                if s == 3:
                    eng.wait_ge(decays, 2 * CT)
                    for t in range(CT):
                        nc.scalar.activation(rg[:, t, :], rg[:, t, :], ACT.Tanh, scale=sp[:, 3, t:t + 1])\
                          .then_inc(decays, 1)
                if s == 4:
                    eng.wait_ge(beta2_ready, 1)
                    nc.scalar.activation(mixb[:, :, :], mixb[:, :, :], ACT.Sqrt).then_inc(beta_ready, 1)

            lru(0)
            for k in range(JOBS0):
                for c, half in FILL0.get(k, []):
                    if half == 0:
                        split(c + LEAD)
                exps(k)
                for c, half in FILL0.get(k, []):
                    evacuate(c, half)
                lru(k + 1)
            eng.wait_ge(unit_read, unit_of(GR + 1, 1) + 1)
            for a in range(2):
                gated = xr[:, 2 * a:2 * a + 2, 0:T]
                nc.scalar.activation(gated, gated, ACT.Gelu_apprx_tanh).then_inc(gelu_ready, 1)
            load_sqrt()
            o_parts(0, ((0, 0, 2), (1, 0, 3)))
            for c in range(OUT0, MLP0):
                split(c + LEAD)
            boundary(1)
            mlp(MLP0, UNIT_MLP0)
            boundary(2)
            for c in range(Q1, QS_B):
                split(c + LEAD)
                for half in range(2):
                    evacuate(c, half)
            for i in range(TT):
                eng.wait_ge(gates_done, i + 1)
                nc.scalar.activation(gates[:, i, :], wk[2 + i][:, 0:3 * HEADS], ACT.Sigmoid)\
                  .then_inc(gates_ready, 1)

            def cmp_hidden(which):
                eng.wait_ge(hT_done, which + 1)
                for t in range(2):
                    src = wk[which][:, t * NPAD:t * NPAD + GROUPS * NC]
                    if which == 0:
                        o = nc.scalar.activation(hkT[:, t, :], src, ACT.Gelu_apprx_tanh)
                    else:
                        s4 = bass.AP(src.tensor, src.offset,
                                     [list(src.ap[0]), [NC, GROUPS], [0, PER_GROUP], [1, NC]])
                        o = nc.scalar.activation(hvT[:, t, :, :, 0:NC], s4, ACT.Gelu_apprx_tanh)
                o.then_inc(hT_ready, 1)

            for k in range(JOBS0, JOBS):
                if k == KCMP_STEP + 3:
                    for i in range(TT):
                        n = cmp_keys(i)
                        eng.wait_ge(cs_ready, i + 1)
                        nc.scalar.activation(ce[:, i, :, 0:n], cs[:, i, :, 0:n], ACT.Exp, scale=-1.0)\
                          .then_inc(ce_exp, 1)
                for c, half in FILL1.get(k, []):
                    if half == 0:
                        split(c + LEAD)
                exps(k)
                for c, half in FILL1.get(k, []):
                    if c < CMPK:
                        evacuate(c, half)
                    elif half == 1 and c in (CMPK + 3, CMPV + 3):
                        which = (c - CMPK) // 4
                        eng.wait_ge(half_done, 2 * c + 2)
                        nc.scalar.activation(hidden[0:2 * GROUPS * NC, which, :],
                                             wk[which][0:2 * GROUPS * NC, 0:CMP_HIDDEN], ACT.Copy)\
                          .then_inc(cmp_product, 1)
                if k == KCMP_STEP:
                    cmp_hidden(0)
            cmp_hidden(1)
            eng.wait_ge(kv_done, 2)
            for j in range(PER_GROUP):
                rows = slice(j * NPAD, (j + 1) * NPAD)
                nc.scalar.activation(vcmp[rows, :, j * P:(j + 1) * P],
                                     wk[1][rows, T:2 * T].rearrange("p (g d) -> p g d", g=GROUPS), ACT.Copy)\
                  .then_inc(kv_ready, 1)
            load_sqrt()
            o_parts(2, [(i, half, 2 * i + half) for i in range(TT) for half in range(2)])
            for c in range(OUT1, MLP1):
                split(c + LEAD)
            boundary(3)
            mlp(MLP1, UNIT_MLP1)
            for i in range(TT):
                post(4, i)

        @block.vector
        def _(eng):
            steps = [0]

            def link(ins):
                steps[0] += 1
                ins.then_inc(dve_step, 1)
                eng.wait_ge(dve_step, steps[0])

            def lo(c, n):
                eng.wait_ge(hi_ready, n + 1)
                nc.vector.tensor_tensor(w_lo[:, c, :], raw[:, c, :], w_hi[:, c, :].bitcast(F32),
                                        ALU.subtract).then_inc(lo_ready, 1)

            def split(n):
                if n < CHUNKS:
                    lo(n % RING, n)

            def post(b, i):
                k, last = TT * (b - 1) + i, LAST_OF_BRANCH[b]
                std = stat[:, 0, 3, k:k + 1]
                if i == 0:
                    eng.wait_ge(gain_landed[0], 16 * b)
                eng.wait_ge(half_done, 2 * last - 1 if i == 0 else 2 * last + 2)
                nc.vector.tensor_tensor(tok[:, i, 512:], acc[:, 2 * i + 1, :], gain[:, 0, 512:], ALU.mult)\
                  .then_inc(post_mul, 1)
                eng.wait_ge(post_sq, k + 1)
                link(nc.vector.tensor_tensor(tok[:, i, 0:512], acc[:, 2 * i, :], gain[:, 0, 0:512], ALU.mult))
                eng.wait_ge(post_std, k + 1)
                link(nc.vector.reciprocal(std, std))
                for half in range(2):
                    cols = slice(half * 512, (half + 1) * 512)
                    nc.vector.scalar_tensor_tensor(out=x[:, i, cols], in0=tok[:, i, cols], scalar=std,
                                                   in1=x[:, i, cols], op0=ALU.mult, op1=ALU.add).then_inc(x_ready, 1)

            def pre(b, i):
                k = TT * b + i
                std = stat[:, 1, 3, k:k + 1]
                if b == 0:
                    eng.wait_ge(x_landed[i], 16)
                else:
                    eng.wait_ge(x_ready, 2 * (TT * (b - 1) + i + 1))
                if i == 0:
                    eng.wait_ge(gain_landed[1], 16 * (b + 1))
                link(nc.vector.tensor_tensor(tok[:, i, :], x[:, i, :], gain[:, 1, :], ALU.mult))
                eng.wait_ge(pre_std, k + 1)
                link(nc.vector.reciprocal(std, std))
                nc.vector.tensor_scalar(diag[:, i, :], ident[:, :], std, None, ALU.mult).then_inc(xn_ready, 1)

            def turned(b, i):
                for half in range(2):
                    eng.wait_ge(tT_hi, 2 * (TT * b + i) + half + 1)
                    dst = slice(4 * half, 4 * half + 4), slice(i * P, (i + 1) * P)
                    nc.vector.tensor_tensor(t_lo[:, dst[0], dst[1]],
                                            wk[2 + half][:, :].rearrange("p (k t) -> p k t", k=4),
                                            t_hi[:, dst[0], dst[1]].bitcast(F32), ALU.subtract)\
                      .then_inc(tT_ready, 1)

            def boundary(b):
                post(b, 0)
                pre(b, 0)
                post(b, 1)
                turned(b, 0)
                pre(b, 1)
                turned(b, 1)

            def scores(k):
                head = job(k)[0]
                eng.wait_ge(scores_done, k + 1)
                if k >= 2:
                    eng.wait_ge(exp_done, k - 1)
                for i, (a, n) in enumerate(((0, P), (P, 2 * P))):
                    s = nc.vector.tensor_tensor_reduce(
                        out=sneg[:, k % 2, a:a + n], in0=wk[2 + k % 2][:, a:a + n],
                        in1=toep[:, head, a:a + n], scale=1.0, scalar=3.0e38, op0=ALU.add, op1=ALU.min,
                        accum_out=mneg[:, 2 * k + i:2 * k + i + 1])
                s.then_inc(sneg_ready, 1)

            def probs_out(k):
                eng.wait_ge(pT_done, k + 1)
                if k >= 2:
                    eng.wait_ge(pv_done, k - 1)
                nc.vector.tensor_copy(pT[:, k % 2, :], acc[:, k % 2, 0:3 * P]).then_inc(pT_ready, 1)

            def head_out(k):
                head, d = job(k)[0:2]
                c2 = coef[:, 2 * k:2 * k + 2]
                eng.wait_ge(exp_done, k + 1)
                link(nc.vector.tensor_scalar(c2, sums[:, 2 * k:2 * k + 2], 1e-30, None, ALU.max))
                link(nc.vector.reciprocal(c2, c2))
                if k >= JOBS0:
                    branch = 1 + (k - JOBS0) // HEADS
                    eng.wait_ge(gates_ready, TT)
                    link(nc.vector.tensor_tensor(c2, c2, gates[:, :, 3 * head + branch], ALU.mult))
                eng.wait_ge(pv_done, k + 1)
                for i in range(TT):
                    dst = tok[:, i, head * d:(head + 1) * d]
                    src = acc[:, 2 + k % 2, i * T:i * T + d]
                    if k < 2 * HEADS:
                        o = nc.vector.tensor_scalar(dst, src, coef[:, 2 * k + i:2 * k + i + 1], None, ALU.mult)
                    else:
                        if i == 0:
                            eng.wait_ge(o_ready, k - HEADS + 1)
                        o = nc.vector.scalar_tensor_tensor(out=dst, in0=src, scalar=coef[:, 2 * k + i:2 * k + i + 1],
                                                           in1=dst, op0=ALU.mult, op1=ALU.add)
                o.then_inc(o_ready, 1)

            def pipeline(first, last, fill, extra):
                for s in range(first, last + 2):
                    if s < last:
                        scores(s)
                    if first <= s - 1 < last:
                        probs_out(s - 1)
                    if first <= s - 2 < last:
                        head_out(s - 2)
                    for c, half in fill.get(s, []):
                        if half == 0:
                            split(c + LEAD)
                    extra(s)

            def squares(slot, s, read, sq):
                eng.wait_ge(unit_read, read)
                if not isinstance(sq, int) or sq >= 2:
                    eng.wait_ge(h_ready, sq - 1)
                nc.vector.tensor_tensor(h_hi[:, slot, :], relu[:, s, :], relu[:, s, :], ALU.mult)
                nc.vector.tensor_tensor(square[:, s, :], relu[:, s, :], relu[:, s, :], ALU.mult)\
                  .then_inc(squared, 1)
                eng.wait_ge(squared, sq + 1)
                nc.vector.tensor_tensor(h_lo[:, slot, :], square[:, s, :], h_hi[:, slot, :].bitcast(F32),
                                        ALU.subtract).then_inc(h_ready, 1)

            def mlp(first, unit0):
                split(first + LEAD)
                for s in range(2):
                    squares(s, s, unit0 + s + 1, sq_of(unit0 + s))
                with eng.Fori(0, 7) as j:
                    for c in range(4):
                        n = first + 1 + c + LEAD
                        lo(n % RING, j * 4 + n)
                        if c % 2 == 0:
                            for s in range(2):
                                u = unit0 + 2 + c + s
                                squares((2 + c + s) % 4, s, j * 4 + (u + 1), j * 4 + sq_of(u))
                split(first + 29 + LEAD)
                for s in range(2):
                    u = unit0 + 30 + s
                    squares(2 + s, s, u + 1, sq_of(u))
                split(first + 30 + LEAD)
                split(first + 31 + LEAD)

            def o_parts(before, groups):
                for n, (i, half, bank) in enumerate(groups, before):
                    eng.wait_ge(oT_hi, n + 1)
                    dst = slice(4 * half, 4 * half + 4), slice(i * P, (i + 1) * P)
                    nc.vector.tensor_tensor(t_lo[:, dst[0], dst[1]],
                                            wk[bank][:, :].rearrange("p (k t) -> p k t", k=4),
                                            t_hi[:, dst[0], dst[1]].bitcast(F32), ALU.subtract)\
                      .then_inc(oT_ready, 1)

            nc.vector.memset(pT[:, 0, 0:P], 0.0).then_inc(zeros, 1)
            eng.wait_ge(small_landed, 16)
            pre(0, 0)
            split(0)
            turned(0, 0)
            pre(0, 1)
            split(1)
            turned(0, 1)
            for c in range(V0, QB):
                split(c + LEAD)
                if c == V0:
                    lam = lvec[:, :, 7]
                    eng.wait_ge(lru_landed, 32)
                    nc.vector.scalar_tensor_tensor(out=sp[:, 0, :], in0=lam, scalar=-1.0, in1=lam, op0=ALU.mult,
                                                   op1=ALU.min).then_inc(sp_ready, 1)
                if c == V0 + 1:
                    eng.wait_ge(ext_done, 1)
                    nc.vector.tensor_copy(ext, acc[0:HEADS, 3, 0:3 * P - 1]).then_inc(ext_read, 1)
                if c == XR:
                    eng.wait_ge(sp_ready, 2)
                    link(nc.vector.tensor_scalar(sp[:, 2, :], sp[:, 1, :], 2.0, None, ALU.add))
                    link(nc.vector.reciprocal(sp[:, 2, :], sp[:, 2, :]))
                    link(nc.vector.tensor_tensor(sp[:, 1, :], sp[:, 1, :], sp[:, 2, :], ALU.mult))
                    link(nc.vector.tensor_tensor(sp[:, 2, :], sp[:, 1, :], sp[:, 1, :], ALU.mult))
                    link(nc.vector.memset(sp[:, 3, :], 1.0 / 17))
                    for odd in range(15, 0, -2):
                        link(nc.vector.tensor_tensor(sp[:, 3, :], sp[:, 3, :], sp[:, 2, :], ALU.mult))
                        link(nc.vector.tensor_scalar(sp[:, 3, :], sp[:, 3, :], 1.0 / odd, None, ALU.add))
                    link(nc.vector.tensor_tensor(sp[:, 3, :], sp[:, 3, :], sp[:, 1, :], ALU.mult))
                    link(nc.vector.tensor_scalar(sp[:, 3, :], sp[:, 3, :], 2.0 * LRU_C, None, ALU.mult))
                    link(nc.vector.tensor_scalar(sp[:, 2, :], lam, -LRU_C, 0.0, ALU.mult, ALU.max))
                    link(nc.vector.tensor_tensor(sp[:, 3, :], sp[:, 3, :], sp[:, 2, :], ALU.add))
                    nc.vector.tensor_scalar(sp[:, 4, :], sp[:, 3, :], -1.0, None, ALU.mult)
                    nc.vector.tensor_scalar(sp[:, 5, :], sp[:, 3, :], -2.0, None, ALU.mult).then_inc(sp_ready, 1)
                if c == QA:
                    eng.wait_ge(unit_read, unit_of(XR + 1, 1) + 1)
                    for tap in range(TAPS):
                        for t in range(CT):
                            if tap == 0:
                                o = nc.vector.tensor_scalar(xc_tile(t), xr[:, t, 0:T], lvec[:, t, 0:1],
                                                            lvec[:, t, 4:5], ALU.mult, ALU.add)
                            else:
                                o = nc.vector.scalar_tensor_tensor(out=xc_tile(t), in0=xr[:, t, tap:tap + T],
                                                                   scalar=lvec[:, t, tap:tap + 1], in1=xc_tile(t),
                                                                   op0=ALU.mult, op1=ALU.add)
                        if tap < TAPS - 1:
                            link(o)
                    o.then_inc(xc_ready, 1)

            def recurrence(s):
                if s == 1:
                    eng.wait_ge(lru_gates, 8)
                    link(nc.vector.tensor_tensor(pairs(ig), pairs(ig), xc, ALU.mult))
                elif s == 3:
                    eng.wait_ge(decays, 3 * CT)
                    nc.vector.scalar_tensor_tensor(out=mixb[:, :, :], in0=mixb[:, :, :], scalar=1.0,
                                                   in1=rg[:, :, :], op0=ALU.add, op1=ALU.mult)\
                      .then_inc(beta2_ready, 1)
                elif s == 4:
                    eng.wait_ge(beta_ready, 1)
                    link(nc.vector.tensor_tensor(ig[:, :, :], ig[:, :, :], mixb[:, :, :], ALU.mult))
                elif 5 <= s < 5 + CT // 2:
                    for t in (2 * (s - 5), 2 * (s - 5) + 1):
                        o = nc.vector.tensor_tensor_scan(xc_tile(t), decay[:, t, :], ig[:, t, :], 0.0,
                                                         ALU.mult, ALU.add)
                    link(o)

            eng.wait_ge(toep_landed, 32)
            pipeline(0, JOBS0, FILL0, recurrence)
            for a in range(2):
                tiles, feats = slice(2 * a, 2 * a + 2), slice(CT + 2 * a, CT + 2 * a + 2)
                eng.wait_ge(gelu_ready, a + 1)
                link(nc.vector.tensor_tensor(rg[:, tiles, :], xc[:, a, :].rearrange("p (b t) -> p b t", b=2),
                                             xr[:, tiles, 0:T], ALU.mult))
                link(nc.vector.tensor_copy(t_hi[:, feats, :], rg[:, tiles, :]))
                nc.vector.tensor_tensor(t_lo[:, feats, :], rg[:, tiles, :], t_hi[:, feats, :].bitcast(F32),
                                        ALU.subtract).then_inc(ob_ready, 1)
            o_parts(0, ((0, 0, 2), (1, 0, 3)))
            for c in range(OUT0, MLP0):
                split(c + LEAD)
            boundary(1)
            mlp(MLP0, UNIT_MLP0)
            boundary(2)
            eng.wait_ge(nsa_landed, 48)
            link(nc.vector.tensor_copy(gw_hi[:, :, :], gw))
            nc.vector.tensor_tensor(gw_lo[:, :, :], gw, gw_hi[:, :, :].bitcast(F32), ALU.subtract)\
              .then_inc(gw_ready, 1)
            for c in range(Q1, QS_B):
                split(c + LEAD)

            def flatten(which):
                src = cmp_in[:, 2 * which:2 * which + 2, :]
                blocks_f32 = ig[:, :, :].rearrange("p a t -> p (a t)")[:, 0:CMP_LEN * GROUPS * NC]\
                    .rearrange("p (l g n) -> p l g n", l=CMP_LEN, g=GROUPS)
                eng.wait_ge(unit_read, unit_of((KC, VC)[which], 1) + 1)
                if which == 1:
                    eng.wait_ge(flat_ready, 1)
                for g in range(GROUPS):
                    s = src[:, g, :]
                    blocks = bass.AP(s.tensor, s.offset, [list(s.ap[0]), [1, CMP_LEN], [CMP_STRIDE, NC]])
                    p = pos[:, which, :]
                    emb = bass.AP(p.tensor, p.offset, [list(p.ap[0]), [1, CMP_LEN], [0, NC]])
                    o = nc.vector.tensor_tensor(blocks_f32[:, :, g, :], blocks, emb, ALU.add)
                link(o)
                flat1 = blocks_f32.rearrange("p l g n -> p l (g n)")
                link(nc.vector.tensor_copy(flat[:, which, :, 0, :], flat1))
                nc.vector.tensor_tensor(flat[:, which, :, 1, :], flat1, flat[:, which, :, 0, :].bitcast(F32),
                                        ALU.subtract).then_inc(flat_ready, 1)

            def cmp_scores(i):
                n = cmp_keys(i)
                s_i = cs[:, i, :, 0:n]
                if i == 0:
                    eng.wait_ge(cs_done, 1)
                link(nc.vector.tensor_tensor(s_i, cmp_scored[:, i, :, 0:n], cmp_bias[i], ALU.add))
                link(nc.vector.tensor_reduce(cst[:, i, 0, :], s_i, AX.X, ALU.min))
                m = cst[:, i, 0, :]
                nc.vector.tensor_tensor(s_i, s_i, bass.AP(m.tensor, m.offset, [list(m.ap[0]), [1, HEADS], [0, n]]),
                                        ALU.subtract).then_inc(cs_ready, 1)

            def cmp_probs(i):
                e_i = ce[:, i, :, 0:cmp_keys(i)]
                eng.wait_ge(ce_exp, i + 1)
                nc.vector.scalar_tensor_tensor(out=e_i, in0=cmp_bias[i], scalar=MASKED / 10, in1=e_i,
                                               op0=ALU.is_lt, op1=ALU.mult).then_inc(ce_ready, 1)
                eng.wait_ge(ce_ready, i + 1)
                link(nc.vector.tensor_reduce(cst[:, i, 1, :], e_i, AX.X, ALU.add))
                link(nc.vector.tensor_scalar(cst[:, i, 1, :], cst[:, i, 1, :], 1e-30, None, ALU.max))
                link(nc.vector.reciprocal(cst[:, i, 2, :], cst[:, i, 1, :]))
                link(nc.vector.tensor_tensor(cst[:, i, 3, :], cst[:, i, 2, :], gates[:, i, 0::3], ALU.mult))

            def cmp_out(i):
                eng.wait_ge(cpv_done, i + 1)
                eng.wait_ge(o_ready, JOBS)
                for h in range(HEADS):
                    g, j = divmod(h, PER_GROUP)
                    dst = tok[:, i, h * P:(h + 1) * P]
                    o = nc.vector.scalar_tensor_tensor(out=dst, in0=wk[2 * i + g][:, j * P:(j + 1) * P],
                                                       scalar=cst[:, i, 3, h:h + 1], in1=dst,
                                                       op0=ALU.mult, op1=ALU.add)
                o.then_inc(oc_ready, 1)

            cmp_scored = wk[0][:, 0:T].rearrange("p (i h n) -> p i h n", i=TT, h=HEADS)
            cmp_bias = [toep[:, :, CMP_LEN - 1:P:CMP_STRIDE], toep[:, :, P + CMP_LEN - 1::CMP_STRIDE]]
            flattened = next(s for s, units in FILL1.items() if (VC, 1) in units)

            def extra(s):
                units = FILL1.get(s, [])
                for which in range(2):
                    if ((KC, VC)[which], 1) in units:
                        flatten(which)
                if s == flattened + 1:
                    n = GROUPS * NC
                    nc.vector.tensor_tensor(halves_sum, ident[0:2 * n, 0:n], ident[0:2 * n, n:2 * n], ALU.add)
                    link(nc.vector.memset(ig[:, :, :], 0.0))
                if s == KCMP_STEP + 1:
                    eng.wait_ge(kv_done, 1)
                    nc.vector.tensor_copy(kcmp[:, :], wk[0][:, P:P + GROUPS * NC]).then_inc(kv_ready, 1)
                if s == KCMP_STEP + 2:
                    for i in range(TT):
                        cmp_scores(i)
                if s == KCMP_STEP + 3:
                    for i in range(TT):
                        cmp_probs(i)
                if s == KCMP_STEP + 4:
                    eng.wait_ge(cpT_done, 1)
                    nc.vector.tensor_copy(cpT, wk[0][:, :].rearrange("p (i g t) -> p i g t", i=TT, g=GROUPS))\
                      .then_inc(cpT_ready, 1)

            link(nc.vector.memset(mixb[:, :, :], 0.0))
            pipeline(JOBS0, JOBS, FILL1, extra)
            for i in range(TT):
                cmp_out(i)
            o_parts(2, [(i, half, 2 * i + half) for i in range(TT) for half in range(2)])
            for c in range(OUT1, MLP1):
                split(c + LEAD)
            boundary(3)
            mlp(MLP1, UNIT_MLP1)
            for i in range(TT):
                post(4, i)

        @block.tensor
        def _(eng):
            PASSES = ((0, 0), (1, 0), (0, 1))
            t_part, w_part, h_part = (t_hi, t_lo), (w_hi, w_lo), (h_hi, h_lo)

            def group(psum, lhsT, rhs, n, before=lambda k: None):
                for k in range(n):
                    before(k)
                    for a, w in PASSES:
                        m = nc.tensor.matmul(psum, lhsT(k, a, w), rhs(k, a, w), start=k == 0 and (a, w) == (0, 0),
                                             stop=k == n - 1 and (a, w) == PASSES[-1])
                return m

            def weights(c, part):
                return w_part[part][:, c, :].rearrange("p (k n) -> p k n", k=KT)

            def up_unit(slot, half, bank, before=lambda k: None):
                return group(wk[bank][:, 0:T],
                             lambda k, a, w: weights(slot, w)[:, k, half * P:(half + 1) * P],
                             lambda k, a, w: t_part[a][:, k, :], KT, before)

            def unit(c, half):
                u = unit_of(c, half)
                if half == 0:
                    eng.wait_ge(lo_ready, c + 1)
                if u >= 2:
                    eng.wait_ge(unit_read, u - 1)
                up_unit(c % RING, half, half).then_inc(half_done, 1)

            def chunk(c):
                for half in range(2):
                    unit(c, half)

            def products(i, slot, r0, part, first=False, last=False):
                for half in range(2):
                    for r in range(2):
                        for a, w in PASSES:
                            m = nc.tensor.matmul(
                                acc[:, 2 * i + half, :],
                                part[a][:, r0 + r, i * P:(i + 1) * P],
                                w_part[w][:, slot, r * D + half * 512:r * D + half * 512 + 512],
                                start=first and r == 0 and (a, w) == (0, 0),
                                stop=last and r == 1 and (a, w) == PASSES[-1])
                return m

            def down(slot, r0, part, first):
                for i in range(TT):
                    products(i, slot, r0, part, first).then_inc(half_done, 1)

            def closing(c, r0, part, ready=lambda n: None):
                for i in range(TT):
                    for n in range(2):
                        if i == 0:
                            eng.wait_ge(lo_ready, c + n + 1)
                            ready(n)
                        m = products(i, (c + n) % RING, r0[n], part, last=n == 1)
                        if (i, n) != (0, 0):
                            m.then_inc(half_done, 1 if (i, n) != (1, 1) else 2)

            def out_chunk(c, r0, first):
                eng.wait_ge(lo_ready, c + 1)
                down(c % RING, r0, t_part, first)

            def keep_clock(n, operand):
                for _ in range(n):
                    nc.tensor.matmul(acc[:, 0, 0:P], operand, operand, start=True, stop=True)

            def turned(b, i):
                eng.wait_ge(xn_ready, TT * b + i + 1)
                for half in range(2):
                    if i == 1:
                        eng.wait_ge(tT_ready, 2 * TT * b + half + 1)
                    for q in range(4):
                        k = 4 * half + q
                        m = nc.tensor.matmul(wk[2 + half][:, q * P:(q + 1) * P], tok[:, i, k * P:(k + 1) * P],
                                             diag[:, i, :], start=True, stop=True)
                    m.then_inc(xT_done, 1)

            def tile_in(b, i):
                def before(k):
                    if k % 4 == 0:
                        eng.wait_ge(tT_ready, 2 * (TT * b + i) + k // 4 + 1)
                return before

            def opening(b):
                c0 = OPENS[b]
                turned(b, 0)
                for i in range(TT):
                    for c in (c0, c0 + 1):
                        if (c, i) == ((c0 + 1, 0) if b == 0 else (c0, 1)):
                            turned(b, 1)
                        eng.wait_ge(lo_ready, c + 1)
                        m = group(unit_bank(c, i)[:, 0:T],
                                  lambda k, a, w: t_part[a][:, k, i * P:(i + 1) * P],
                                  lambda k, a, w: weights(c % RING, w)[:, k, :], KT, tile_in(b, i))
                        if (c, i) != (c0 + 1, 0):
                            m.then_inc(half_done, 1 if (c, i) != (c0 + 1, 1) else 2)

            def transposed_o(groups, ready):
                for i, half, bank in groups:
                    ready(i)
                    for q in range(4):
                        k = 4 * half + q
                        m = nc.tensor.transpose(wk[bank][:, q * P:(q + 1) * P], tok[:, i, k * P:(k + 1) * P],
                                                ident[:, :])
                    m.then_inc(oT_done, 1)

            def scores(k):
                head, d, p0, qs, ks, v0 = job(k)
                eng.wait_ge(unit_read, unit_of(last_chunk(k), 1) + 1)
                if k >= 2:
                    eng.wait_ge(sneg_ready, k - 1)
                bank = wk[2 + k % 2]
                q, kk = qT[p0:p0 + d, qs, :], kT[p0:p0 + d, ks, :]
                nc.tensor.matmul(bank[:, 0:P], q[:, 0:P], kk[:, 0:P], start=True, stop=True)
                nc.tensor.matmul(bank[:, P:3 * P], q[:, P:T], kk, start=True, stop=True).then_inc(scores_done, 1)

            def turn(k):
                eng.wait_ge(exp_done, k + 1)
                if k >= 2:
                    eng.wait_ge(pT_ready, k - 1)
                for n in range(3):
                    m = nc.tensor.transpose(acc[:, k % 2, n * P:(n + 1) * P], prob[:, k % 2, n * P:(n + 1) * P],
                                            ident[:, :])
                m.then_inc(pT_done, 1)

            def values(k):
                head, d, p0, qs, ks, v0 = job(k)
                eng.wait_ge(pT_ready, k + 1)
                if k >= 2:
                    eng.wait_ge(o_ready, k - 1)
                bank = acc[:, 2 + k % 2, :]
                pt = pT[:, k % 2, :]
                nc.tensor.matmul(bank[:, 0:d], pt[:, 0:P], v[:, 0, v0:v0 + d], start=True, stop=True)
                nc.tensor.matmul(bank[:, T:T + d], pt[:, P:2 * P], v[:, 0, v0:v0 + d], start=True, stop=False)
                nc.tensor.matmul(bank[:, T:T + d], pt[:, 2 * P:3 * P], v[:, 1, v0:v0 + d], start=False, stop=True)\
                  .then_inc(pv_done, 1)

            def pipeline(first, last, fill, filler, extra):
                for s in range(first, last + 2):
                    if s < last:
                        scores(s)
                    if first <= s - 1 < last:
                        turn(s - 1)
                    if first <= s - 2 < last:
                        values(s - 2)
                    for c, half in fill.get(s, []):
                        filler(c, half)
                    extra(s)

            def cmp_unit(c, half):
                if c < CMPK:
                    return unit(c, half)
                which, at = divmod(c - CMPK, 4)
                if half == 0:
                    eng.wait_ge(lo_ready, c + 1)
                if at == 0 and half == 0:
                    eng.wait_ge(flat_ready, which + 1)
                    eng.wait_ge(unit_read, unit_of(KW, 1) + 1)
                for q in range(4):
                    place = 8 * at + 4 * half + q
                    for w in range(2):
                        m = nc.tensor.matmul(wk[which][0:2 * GROUPS * NC, 0:CMP_HIDDEN],
                                             flat[:, which, place, :, :].rearrange("p a n -> p (a n)"),
                                             weights(c % RING, w)[:, 4 * half + q, :],
                                             start=(place, w) == (0, 0), stop=(place, w) == (CMP_LEN - 1, 1))
                m.then_inc(half_done, 1)

            def hidden_turned(which):
                eng.wait_ge(cmp_product, which + 1)
                for t in range(2):
                    m = nc.tensor.matmul(wk[which][:, t * NPAD:t * NPAD + GROUPS * NC],
                                         hidden[0:2 * GROUPS * NC, which, t * P:(t + 1) * P], halves_sum,
                                         start=True, stop=True)
                m.then_inc(hT_done, 1)

            def compressed(which):
                eng.wait_ge(hT_ready, which + 1)
                if which == 0:
                    for t in range(2):
                        m = nc.tensor.matmul(wk[0][:, P:P + GROUPS * NC], w2[:, 0, t, :], hkT[:, t, :],
                                             start=t == 0, stop=t == 1)
                else:
                    for g in range(GROUPS):
                        for t in range(2):
                            m = nc.tensor.matmul(wk[1][:, T + g * P:T + (g + 1) * P],
                                                 hvT[:, t, g, :, :].rearrange("p j n -> p (j n)"),
                                                 w2[:, 1, t, :], start=t == 0, stop=t == 1)
                m.then_inc(kv_done, 1)

            def mlp(b, first, unit0):
                def up(c, u, slot, before=lambda k: None):
                    eng.wait_ge(lo_ready, c + 1)
                    for s in range(2):
                        eng.wait_ge(unit_read, u + (s - 1))
                        up_unit(slot, s, s, before).then_inc(half_done, 1)

                def dn(c, slot, h0, ready, first_sum):
                    eng.wait_ge(lo_ready, c + 1)
                    eng.wait_ge(h_ready, ready)
                    down(slot, h0, h_part, first_sum)

                def body(j4, first_sum):
                    for c in range(0, 4, 2):
                        n = first + 1 + c
                        up(j4 + n, j4 + (unit0 + 2 + c), n % RING)
                        dn(j4 + (n + 1), (n + 1) % RING, c, j4 + (sq_of(unit0) + c + 2), first_sum and c == 0)

                up(first, unit0, first % RING, tile_in(b, 1))
                body(0, True)
                with eng.Fori(1, 7) as j:
                    body(j * 4, False)
                up(first + 29, unit0 + 30, (first + 29) % RING)
                closing(first + 30, (0, 2), h_part, lambda n: eng.wait_ge(h_ready, sq_of(unit0) + 30 + 2 * n))

            eng.wait_ge(zeros, 1)
            keep_clock(22, pT[:, 0, 0:P])
            eng.wait_ge(small_landed, 16)
            opening(0)
            eng.wait_ge(table_landed, 32)
            nc.tensor.matmul(acc[0:HEADS, 3, 0:3 * P - 1], table[:, :], select, start=True, stop=True)\
              .then_inc(ext_done, 1)
            for c in range(XR, QB):
                chunk(c)
            eng.wait_ge(xc_ready, 1)
            eng.wait_ge(lru_landed, 32)
            for t in range(CT):
                for w in range(2):
                    m = nc.tensor.matmul(acc[:, t, w * T:(w + 1) * T], lgate[:, w, t, :], xc_tile(t),
                                         start=True, stop=True)
            m.then_inc(lru_gates_done, 1)

            def extra0(s):
                if s == 0:
                    eng.wait_ge(lru_gates, 8)

            pipeline(0, JOBS0, FILL0, unit, extra0)
            transposed_o(((0, 0, 2), (1, 0, 3)), lambda i: eng.wait_ge(o_ready, JOBS0))
            eng.wait_ge(ob_ready, 1)
            out_chunk(OUT0, CT, True)
            eng.wait_ge(ob_ready, 2)
            out_chunk(OUT0 + 1, CT + 2, False)
            eng.wait_ge(oT_ready, 2)
            closing(OUT0 + 2, (0, 2), t_part)
            turned(1, 0)
            keep_clock(12, ident[:, :])
            turned(1, 1)
            mlp(1, MLP0, UNIT_MLP0)
            opening(2)
            for c in range(QS_A, QS_B):
                chunk(c)
            eng.wait_ge(gw_ready, 1)
            for i in range(TT):
                group(wk[2 + i][:, 0:3 * HEADS], lambda k, a, w: t_part[a][:, k, i * P:(i + 1) * P],
                      lambda k, a, w: (gw_hi, gw_lo)[w][:, k, :], KT).then_inc(gates_done, 1)
            eng.wait_ge(gates_ready, TT)

            def extra(s):
                if s == KCMP_STEP:
                    hidden_turned(0)
                if s == KCMP_STEP + 1:
                    compressed(0)
                if s == KCMP_STEP + 2:
                    eng.wait_ge(kv_ready, 1)
                    for i in range(TT):
                        for h in range(HEADS):
                            g, at = h // PER_GROUP, (i * HEADS + h) * 16
                            m = nc.tensor.matmul(wk[0][:, at:at + NC], qT[:, h, i * P:(i + 1) * P],
                                                 kcmp[:, g * NC:(g + 1) * NC], start=True, stop=True)
                    m.then_inc(cs_done, 1)
                if s == KCMP_STEP + 4:
                    eng.wait_ge(ce_ready, TT)
                    for i in range(TT):
                        for g in range(GROUPS):
                            at = (i * GROUPS + g) * P
                            m = nc.tensor.transpose(wk[0][:, at:at + P], ce[:, i, g * PER_GROUP:(g + 1) * PER_GROUP, :]
                                                    .rearrange("p h n -> p (h n)"), ident[:, :])
                    m.then_inc(cpT_done, 1)
                if s == VCMP_STEP:
                    hidden_turned(1)
                if s == JOBS:
                    compressed(1)

            pipeline(JOBS0, JOBS, FILL1, cmp_unit, extra)
            eng.wait_ge(kv_ready, 1 + PER_GROUP)
            eng.wait_ge(cpT_ready, 1)
            eng.wait_ge(sneg_ready, JOBS)
            for i in range(TT):
                for g in range(GROUPS):
                    m = nc.tensor.matmul(wk[2 * i + g][:, :], cpT[:, i, g, :], vcmp[:, g, :], start=True, stop=True)
                m.then_inc(cpv_done, 1)
            transposed_o([(i, half, 2 * i + half) for i in range(TT) for half in range(2)],
                         lambda i: eng.wait_ge(oc_ready, i + 1))
            eng.wait_ge(oT_ready, 4)
            eng.wait_ge(lo_ready, OUT1 + 1)
            products(0, OUT1 % RING, 0, t_part, True).then_inc(half_done, 1)
            eng.wait_ge(oT_ready, 6)
            products(1, OUT1 % RING, 0, t_part, True).then_inc(half_done, 1)
            out_chunk(OUT1 + 1, 2, False)
            closing(OUT1 + 2, (4, 6), t_part)
            turned(3, 0)
            keep_clock(12, ident[:, :])
            turned(3, 1)
            mlp(3, MLP1, UNIT_MLP1)


def bucket_rows():
    exact = BUCKETS // 2
    rows = np.zeros((BUCKETS + 1, 3 * P - 1), np.float32)
    for j in range(3 * P - 1):
        n = T - 1 - j
        if n < 0:
            rows[BUCKETS, j] = MASKED
        elif n < exact:
            rows[n, j] = -1.0
        else:
            large = exact + int(math.log(n / exact) / math.log(128 / exact) * (BUCKETS - exact))
            rows[min(large, BUCKETS - 1), j] = -1.0
    return rows


def columns(w):
    k, n = w.shape
    return w.reshape(k // P, P, n // 256, 256).transpose(2, 1, 0, 3).reshape(n // 256, P, -1)


def rows(w):
    return w.reshape(-1, 2, P, D).transpose(0, 2, 1, 3).reshape(-1, P, 2 * D)


def places(w):
    return w.reshape(-1, 8, P, CMP_HIDDEN).transpose(0, 2, 1, 3).reshape(-1, P, CHUNK)


def kernel(**inputs):
    import concourse.bacc as bacc
    from concourse.bass_utils import run_bass_kernel_spmd

    a = {k: np.asarray(v) for k, v in inputs.items()}
    dq = HEADS * DH_A
    w_in, c_in, w_o = a["ab_w_in"][0], a["c_w_in"][0], a["ab_w_out"][0]
    part = lambda lo, n: columns(w_in[:, lo:lo + n])

    def mlp_stream(layer):
        up, down = columns(a["w_up"][layer]), rows(a["w_down"][layer])
        order = [up[0]]
        for c in range(15):
            order += [up[c + 1], down[c]]
        return np.stack(order + [down[15]])

    def q_part(j):
        return columns(c_in[:, j * GROUPS * DH_C:(j + 1) * GROUPS * DH_C])

    def c_part(j):
        lo = HEADS * DH_C + j * GROUPS * DH_C
        return columns(c_in[:, lo:lo + GROUPS * DH_C])

    stream = np.concatenate([
        part(2 * dq, dq), part(3 * dq, W), part(0, T), part(dq, T), part(T, T), part(dq + T, T), part(3 * dq + W, W),
        rows(w_o[dq:]), rows(w_o[:dq]), mlp_stream(0),
        c_part(3), c_part(5), q_part(0), c_part(2), q_part(1), c_part(0), q_part(2), c_part(1), q_part(3), c_part(4),
        places(a["c_cmp_k_w1"][0]), places(a["c_cmp_v_w1"][0]), rows(a["c_w_out"][0]), mlp_stream(1)])
    assert stream.shape == (CHUNKS, P, CHUNK)
    gains = np.stack([a[n][layer] for layer in range(2)
                      for n in ("norm_mix_pre", "norm_mix_post", "norm_mlp_pre", "norm_mlp_post")])
    lru_vec = np.stack([*a["ab_conv_w"][0], a["ab_conv_b"][0], a["ab_b_rg"][0], a["ab_b_ig"][0],
                        a["ab_lru_lambda"][0]], axis=1).reshape(CT, P, 8).transpose(1, 0, 2)
    lru_gate = np.zeros((P, 2, CT, P), np.float32)
    for w, name in enumerate(("ab_w_rg", "ab_w_ig")):
        for b in range(8):
            r = (b % 2) * 64
            lru_gate[r:r + 64, w, b // 2, r:r + 64] = a[name][0, b]
    fed = {
        "x_in": a["x"][0], "w_stream": stream, "gains": gains, "lru_vec": lru_vec, "lru_gate": lru_gate,
        "rel_bias": a["rel_bias"], "bias_select": bucket_rows(), "ident_in": np.eye(P, dtype=np.float32),
        "gate_w": c_in[:, -3 * HEADS:].reshape(KT, P, 3 * HEADS).transpose(1, 0, 2),
        "cmp_pos": np.stack([a["c_cmp_pos_k"][0].T, a["c_cmp_pos_v"][0].T], axis=1),
        "cmp_w2": np.stack([a[n][0].reshape(2, P, P).transpose(1, 0, 2) for n in ("c_cmp_k_w2", "c_cmp_v_w2")],
                           axis=1),
    }
    nc = bacc.Bacc("TRN2", target_bir_lowering=False, num_devices=1)
    arrays, args = {}, []
    for name, value in fed.items():
        value = np.ascontiguousarray(value)
        arrays[name] = value
        args.append(nc.dram_tensor(name, value.shape, mybir.dt.from_np(value.dtype), kind="ExternalInput").ap())
    out = nc.dram_tensor("out", [T, D], F32, kind="ExternalOutput").ap()
    trunk(nc, *args, out)
    r = run_bass_kernel_spmd(nc, [arrays], core_ids=[0])
    return r.results[0]["out"].reshape(1, T, D)
```

```python
import math
from contextlib import ExitStack

import numpy as np

import concourse.bass as bass
from concourse import mybir

F32 = mybir.dt.float32
F32R = mybir.dt.float32r
ALU = mybir.AluOpType
ACT = mybir.ActivationFunctionType
AX = mybir.AxisListType

P = 128
T = 256
TT = T // P
D = 1024
KT = D // P
HEADS = 8
EPS = 1e-6
MASKED = 1e30
CHUNK = 2048
RING = 4
LEAD = 2

W = 512
CT = W // P
TAPS = 4
LRU_C = 8.0
DH_A = 64
DH_C = 128
GROUPS = 2
PER_GROUP = HEADS // GROUPS
CMP_LEN = 32
CMP_STRIDE = 16
NC = (T - CMP_LEN) // CMP_STRIDE + 1
CMP_HIDDEN = 256
NPAD = 32
BUCKETS = 32

V0, XR, QA, KA, QB, KB, GR, OUT0 = 0, 2, 4, 5, 6, 7, 8, 10
MLP0 = 14
MLP_CHUNKS = 32
Q1 = MLP0 + MLP_CHUNKS
VS, VW, QS_A, KS, QS_B, KC, QS_C, VC, QS_D, KW = range(Q1, Q1 + 10)
QS = (QS_A, QS_B, QS_C, QS_D)
CMPK, CMPV, OUT1 = Q1 + 10, Q1 + 14, Q1 + 18
MLP1 = OUT1 + 4
CHUNKS = MLP1 + MLP_CHUNKS
UNIT_MLP0 = 2 * OUT0
UNIT_Q1 = UNIT_MLP0 + 2 * (MLP_CHUNKS // 2)
UNIT_MLP1 = UNIT_Q1 + 2 * (CMPK - Q1)
PROBS_TO_ACT = 4
JOBS0 = HEADS
JOBS = 3 * HEADS


def unit_of(chunk, half):
    return (2 * chunk if chunk < MLP0 else UNIT_Q1 + 2 * (chunk - Q1)) + half


OPENS = {0: V0, 2: VS}
LAST_OF_BRANCH = {1: MLP0 - 1, 2: Q1 - 1, 3: MLP1 - 1, 4: CHUNKS - 1}


def split_at(c):
    if c in OPENS.values():
        return c + LEAD, c + LEAD + 1
    return () if c - 1 in OPENS.values() else (c + LEAD,)


def last_chunk(k):
    if k < HEADS:
        return KA if k < HEADS // 2 else KB
    head = k - HEADS
    return max(KS, QS[head // 2]) if head < HEADS else KW


def sq_of(u):
    return u - UNIT_MLP0 if u < UNIT_Q1 else MLP_CHUNKS + u - UNIT_MLP1


def cmp_keys(i):
    return ((i + 1) * P - CMP_LEN) // CMP_STRIDE + 1


def spread(units, first, steps):
    cuts = [math.ceil(n * len(units) / steps) for n in range(steps + 1)]
    return {first + n: units[cuts[n]:cuts[n + 1]] for n in range(steps)}


def both_halves(chunks):
    return [(c, half) for c in chunks for half in range(2)]


FILL0 = spread(both_halves(range(QB, OUT0)), 0, 7)
FILL1 = spread(both_halves(range(QS_B, OUT1)), HEADS, 2 * HEADS - 2)
KCMP_STEP, VCMP_STEP = (1 + next(s for s, units in FILL1.items() if (c, 1) in units) for c in (CMPK + 3, CMPV + 3))


def trunk(nc, x_in, w_stream, gains, lru_vec, lru_gate, rel_bias, bias_select, ident_in, gate_w,
          cmp_pos, cmp_w2, out):
    with ExitStack() as ctx:
        def sb(name, shape, dt=F32):
            return ctx.enter_context(nc.sbuf_tensor(name, shape, dt))

        def sem(name):
            return ctx.enter_context(nc.semaphore(name))

        raw = sb("raw", [P, RING, CHUNK])
        w_hi = sb("w_hi", [P, RING, CHUNK], F32R)
        w_lo = sb("w_lo", [P, RING, CHUNK], F32R)
        x = sb("x", [P, TT, D])
        tok = sb("tok", [P, TT, D])
        t_hi = sb("t_hi", [P, KT, T], F32R)
        t_lo = sb("t_lo", [P, KT, T], F32R)
        gain = sb("gain", [P, 2, D])
        toep = sb("toep", [P, HEADS, 3 * P])
        qT = sb("qT", [P, HEADS, T])
        kT = sb("kT", [P, 4, T])
        v = sb("v", [P, TT, W])
        xr = sb("xr", [P, CT, T + TAPS - 1])
        xc = tok[:, :, W:]
        decay = qT[:, CT:, :]

        def xc_tile(t):
            return xc[:, t // 2, (t % 2) * T:(t % 2 + 1) * T]

        def pairs(buf):
            return buf[:, :, :].rearrange("p (a b) t -> p a (b t)", a=2)

        rg = sb("rg", [P, CT, T])
        ig = sb("ig", [P, CT, T])
        lgate = ig[:, :, :].rearrange("p a t -> p (a t)").rearrange("p (w t n) -> p w t n", w=2, t=CT)
        mixb = sb("mixb", [P, CT, T])
        relu, square = rg[:, 0:2, :], rg[:, 2:4, :]
        cmp_in = rg
        hidden = xr[:, :, :].rearrange("p a t -> p (a t)")[:, 0:2 * CMP_HIDDEN].rearrange("p (w n) -> p w n", w=2)
        hvT = mixb[:, 0:2, :].rearrange("p t (g j n) -> p t g j n", g=GROUPS, j=PER_GROUP)
        ce = mixb[:, 2:4, :].rearrange("p i (h n) -> p i h n", h=HEADS)
        flat = sb("flat", [P, 2, CMP_LEN, 2, GROUPS * NC], F32R)
        h_flat = flat[:, :, :, :, :].rearrange("p w l a n -> p (w l a n)")[:, 0:8 * T]
        h_hi, h_lo = (h_flat[:, n * 4 * T:(n + 1) * 4 * T].rearrange("p (s t) -> p s t", s=4) for n in range(2))
        sneg = sb("sneg", [P, 2, 3 * P])
        prob = sb("prob", [P, 2, 3 * P])
        diag = prob[:, :, 0:P]
        junk = sneg[:, :, :].rearrange("p a n -> p (a n)").bitcast(mybir.dt.bfloat16)[:, 0:D]
        pT = sb("pT", [P, 2, 3 * P])
        rg_flat = rg[:, :, :].rearrange("p a t -> p (a t)")
        cs = rg_flat[:, 0:T].rearrange("p (i h n) -> p i h n", i=TT, h=HEADS)
        gelu_x, gelu_y = (rg_flat[:, 3 * T + (1 + n) * 2 * NPAD:3 * T + (2 + n) * 2 * NPAD]
                          .rearrange("p (t n) -> p t n", t=2)[:, :, 0:GROUPS * NC] for n in range(2))
        halves_sum = rg_flat[0:2 * GROUPS * NC, 3 * T:3 * T + GROUPS * NC]
        cpT = rg_flat[:, T:3 * T].rearrange("p (i g t) -> p i g t", i=TT, g=GROUPS)
        mneg = sb("mneg", [P, 2 * JOBS])
        sums = sb("sums", [P, 2 * JOBS])
        coef = sb("coef", [P, 2 * JOBS])
        stat = sb("stat", [P, 2, 4, 4 * TT])
        lvec = sb("lvec", [P, CT, 8])
        sp = sb("sp", [P, 6, CT])
        ident = sb("ident", [P, P])
        one_root = sb("one_root", [P, 1])
        table = sb("table", [BUCKETS + 1, HEADS])
        select = decay[0:BUCKETS + 1, 0:2, :].rearrange("p a t -> p (a t)")[:, 0:3 * P - 1]
        ext = mixb[0:HEADS, 0:2, :].rearrange("p a t -> p (a t)")[:, 0:3 * P - 1]
        xr_flat, ig_flat = (b[:, :, :].rearrange("p a t -> p (a t)") for b in (xr, ig))
        w2 = xr_flat[:, 2 * CMP_HIDDEN:2 * CMP_HIDDEN + 4 * P].rearrange("p (w t n) -> p w t n", w=2, t=2)
        gw = ig_flat[:, 0:KT * 3 * HEADS].rearrange("p (k n) -> p k n", k=KT)
        pos = ig_flat[:, CMP_LEN * GROUPS * NC:CMP_LEN * (GROUPS * NC + 2)].rearrange("p (w l) -> p w l", w=2)
        gw_parts = sb("gw_parts", [P, KT, 2, 3 * HEADS], F32R)
        gates_T = hidden[0:6 * HEADS, 0, :]
        gates_sum = hidden[0:6 * HEADS, 1, 0:3 * HEADS]
        gates = sb("gates", [P, TT, 3 * HEADS])
        hkT = sb("hkT", [P, 2, GROUPS * NC])
        kcmp = lvec[:, :, :].rearrange("p t v -> p (t v)")[:, 0:GROUPS * NC]
        vcmp = ig_flat.rearrange("p (g n) -> p g n", g=GROUPS)
        cst = sb("cst", [P, TT, 2, HEADS])
        acc = ctx.enter_context(nc.psum_tensor("acc", [P, 4, 512], F32))
        wk = [ctx.enter_context(nc.psum_tensor(f"wk{i}", [P, 512], F32)) for i in range(4)]
        ext_dram = nc.dram_tensor("bias_rows", [HEADS, P, 3 * P - 1], F32, kind="Internal").ap()

        landed = [sem(f"landed{i}") for i in range(RING)]
        hi_ready, lo_ready = sem("hi_ready"), sem("lo_ready")
        first_landed, first_hi = [sem("first_landed0"), sem("first_landed1")], sem("first_hi")
        half_done = sem("half_done")
        x_landed = [sem("x_landed0"), sem("x_landed1")]
        gain_landed = [sem("gain_post_landed"), sem("gain_pre_landed")]
        lru_landed, nsa_landed, small_landed, table_landed = (sem("lru_landed"), sem("nsa_landed"), sem("ident_landed"),
                                                              sem("table_landed"))
        ext_stored, toep_landed, out_stored = sem("ext_stored"), sem("toep_landed"), sem("out_stored")
        cleared, table_one, zeros = sem("cleared"), sem("table_one"), sem("zeros")
        ext_done, ext_read = sem("ext_done"), sem("ext_read")
        unit_read = sem("unit_read")
        sums_done = sem("sums_done")
        post_sq, post_std, x_ready = sem("post_sq"), sem("post_std"), sem("x_ready")
        pre_std, xn_ready = sem("pre_std"), sem("xn_ready")
        xT_done, tT_hi, tT_ready = sem("xT_done"), sem("tT_hi"), sem("tT_ready")
        squared, h_ready = sem("squared"), sem("h_ready")
        sp_ready, xc_ready = sem("sp_ready"), sem("xc_ready")
        lru_gates_done, lru_gates = sem("lru_gates_done"), sem("lru_gates")
        decays, beta2_ready, beta_ready, ob_ready = sem("decays"), sem("beta2_ready"), sem("beta_ready"), sem("ob_ready")
        scores_done, sneg_ready, exp_done = sem("scores_done"), sem("sneg_ready"), sem("exp_done")
        pT_done, pT_ready, pv_done, o_ready = sem("pT_done"), sem("pT_ready"), sem("pv_done"), sem("o_ready")
        gw_ready, gates_done = sem("gw_ready"), sem("gates_done")
        gates_read, gates_ready = sem("gates_read"), sem("gates_ready")
        flat_ready, cmp_product = sem("flat_ready"), sem("cmp_product")
        gelu_cubic, gelu_tanh = sem("gelu_cubic"), sem("gelu_tanh")
        hT_done, hT_ready, kv_done, kv_ready = sem("hT_done"), sem("hT_ready"), sem("kv_done"), sem("kv_ready")
        cs_done, cs_ready, ce_exp, ce_ready = sem("cs_done"), sem("cs_ready"), sem("ce_exp"), sem("ce_ready")
        cpT_done, cpT_ready, cpv_done = sem("cpT_done"), sem("cpT_ready"), sem("cpv_done")
        oc_ready = sem("oc_ready")
        oT_done, oT_hi, oT_ready = sem("oT_done"), sem("oT_hi"), sem("oT_ready")
        gelu_ready = sem("gelu_ready")
        coef_part = sem("coef_part")
        act_step, dve_step = sem("act_step"), sem("dve_step")

        def unit_bank(c, half):
            return acc[:, half, :] if c - 1 in OPENS.values() else wk[half]

        def turned_bank(b, i, half):
            return wk[half] if b in (1, 3) and i == 1 else wk[2 + half]

        def wait_sums(eng, b, i, half):
            if (i, half) == (1, 1):
                eng.wait_ge(half_done, 2 * LAST_OF_BRANCH[b] + 2)
            else:
                eng.wait_ge(sums_done, 3 * (b - 1) + 2 * i + half + 1)

        def job(k):
            if k < JOBS0:
                return k, DH_A, (k % 2) * DH_A, k // 2, k // 2, k * DH_A
            branch, head = divmod(k - JOBS0, HEADS)
            g = head // PER_GROUP
            return head, DH_C, 0, head, GROUPS * branch + g, (GROUPS * branch + g) * DH_C

        block = ctx.enter_context(nc.Block())

        @block.sync
        def _(eng):
            def load_x(i):
                eng.dma_start(x[:, i, :], x_in[i * P:(i + 1) * P, :]).then_inc(x_landed[i], 16)

            def load_chunk(c):
                eng.dma_start(raw[:, c, :], w_stream[c]).then_inc(landed[c], 16)

            load_x(0)
            eng.dma_start(ident[:, :], ident_in).then_inc(small_landed, 16)
            for c in range(2):
                eng.dma_start(raw[:, c, 0:CHUNK // 2], w_stream[c, :, 0:CHUNK // 2]).then_inc(first_landed[c], 16)
                eng.dma_start(raw[:, c, CHUNK // 2:], w_stream[c, :, CHUNK // 2:]).then_inc(landed[c], 16)
                if c == 0:
                    load_x(1)
            for c in range(2, RING):
                load_chunk(c)
            with eng.Fori(0, CHUNKS // RING - 1) as j:
                for c in range(RING):
                    eng.wait_ge(lo_ready, j * RING + (c + 1))
                    eng.dma_start(raw[:, c, :], w_stream[bass.ds(j * RING + (RING + c), 1)]
                                  .rearrange("o p f -> (o p) f")).then_inc(landed[c], 16)
            for i in range(TT):
                for half in range(2):
                    cols = slice(half * 512, (half + 1) * 512)
                    eng.wait_ge(x_ready, 2 * (3 * TT + i) + half + 1)
                    eng.dma_start(out[i * P:(i + 1) * P, cols], x[:, i, cols]).then_inc(out_stored, 16)
            eng.wait_ge(out_stored, 32 * TT)

        @block.gpsimd
        def _(eng):
            def load_gain(which, row):
                eng.dma_start(gain[:, which, :], bass.AP(gains.tensor, row * D, [[0, P], [1, D]]))\
                   .then_inc(gain_landed[which], 16)

            load_gain(1, 0)
            eng.memset(table[:, :], 1.0).then_inc(table_one, 1)
            eng.wait_ge(table_one, 1)
            eng.dma_start(table[0:BUCKETS, :], rel_bias).then_inc(table_landed, 16)
            eng.dma_start(select, bias_select).then_inc(table_landed, 16)
            eng.dma_start(lvec[:, :, :], lru_vec).then_inc(lru_landed, 16)
            eng.dma_start(lgate, lru_gate).then_inc(lru_landed, 16)
            eng.memset(xr[:, :, 0:TAPS - 1], 0.0).then_inc(cleared, 1)
            eng.wait_ge(ext_read, 1)
            eng.dma_start(ext_dram, bass.AP(ext.tensor, ext.offset, [list(ext.ap[0]), [0, P], list(ext.ap[1])]))\
               .then_inc(ext_stored, 16)
            eng.wait_ge(ext_stored, 16)
            rows = 3 * P - 1
            for at, m0, n in ((0, P, P), (P, 0, 2 * P)):
                eng.dma_start(toep[:, :, at:at + n],
                              bass.AP(ext_dram.tensor, m0 + P - 1, [[rows - 1, P], [P * rows, HEADS], [1, n]]))\
                   .then_inc(toep_landed, 16)
            load_gain(0, 1)
            eng.wait_ge(ob_ready, 2)
            eng.dma_start(gw, gate_w).then_inc(nsa_landed, 16)
            eng.dma_start(pos, cmp_pos).then_inc(nsa_landed, 16)
            eng.dma_start(w2, cmp_w2).then_inc(nsa_landed, 16)
            for b in range(1, 4):
                eng.wait_ge(xn_ready, TT * b)
                load_gain(1, 2 * b)
                eng.wait_ge(x_ready, 2 * TT * b)
                load_gain(0, 2 * b + 1)

        @block.scalar
        def _(eng):
            def hi(c, load, used):
                eng.wait_ge(landed[c], load)
                if used is not None:
                    eng.wait_ge(half_done, used)
                nc.scalar.activation(w_hi[:, c, :], raw[:, c, :], ACT.Copy).then_inc(hi_ready, 1)

            def split(n):
                if n < CHUNKS:
                    hi(n % RING, 16 * (n // RING + 1), 2 * (n - RING + 1) if n >= RING else None)

            steps = [0]

            def link(ins):
                steps[0] += 1
                ins.then_inc(act_step, 1)
                eng.wait_ge(act_step, steps[0])

            def post(b, i):
                k = TT * (b - 1) + i
                first, second, share, std = (stat[:, 0, q, k:k + 1] for q in range(4))
                wait_sums(eng, b, i, 0)
                nc.scalar.activation(junk[:, 0:512], acc[:, 2 * i, :], ACT.Square, accum_out=first)\
                  .then_inc(post_sq, 1)
                eng.wait_ge(post_sq, 2 * k + 1)
                link(nc.scalar.activation(share, first, ACT.Copy, scale=1.0 / D, bias=EPS))
                wait_sums(eng, b, i, 1)
                nc.scalar.activation(junk[:, 512:], acc[:, 2 * i + 1, :], ACT.Square, accum_out=second)\
                  .then_inc(post_sq, 1)
                eng.wait_ge(post_sq, 2 * k + 2)
                nc.scalar.activation(std, second, ACT.Sqrt, scale=1.0 / D, bias=share).then_inc(post_std, 1)

            def pre(b, i):
                k = TT * b + i
                first, second, share, std = (stat[:, 1, q, k:k + 1] for q in range(4))
                for half in range(2):
                    cols = slice(half * 512, (half + 1) * 512)
                    if b == 0:
                        eng.wait_ge(x_landed[i], 16)
                    else:
                        eng.wait_ge(x_ready, 2 * (TT * (b - 1) + i) + half + 1)
                    link(nc.scalar.activation(junk[:, cols], x[:, i, cols], ACT.Square,
                                              accum_out=(first, second)[half]))
                    if half == 0:
                        link(nc.scalar.activation(share, first, ACT.Copy, scale=1.0 / D, bias=EPS))
                nc.scalar.activation(std, second, ACT.Sqrt, scale=1.0 / D, bias=share).then_inc(pre_std, 1)

            def turned(b, i):
                for half in range(2):
                    eng.wait_ge(xT_done, 2 * (TT * b + i) + half + 1)
                    nc.scalar.activation(t_hi[:, 4 * half:4 * half + 4, i * P:(i + 1) * P],
                                         turned_bank(b, i, half)[:, :].rearrange("p (k t) -> p k t", k=4),
                                         ACT.Copy).then_inc(tT_hi, 1)

            def boundary(b):
                post(b, 0)
                pre(b, 0)
                post(b, 1)
                turned(b, 0)
                pre(b, 1)
                turned(b, 1)

            def evacuate(c, half):
                u = unit_of(c, half)
                src = unit_bank(c, half)[:, 0:T]
                func, scale = ACT.Copy, 1.0
                if c in (V0, V0 + 1):
                    dst = v[:, half, T * (c - V0):T * (c - V0 + 1)]
                elif c in (XR, XR + 1):
                    dst = xr[:, 2 * (c - XR) + half, TAPS - 1:]
                    if c == XR and half == 0:
                        eng.wait_ge(cleared, 1)
                elif c in (QA, QB):
                    dst, scale = qT[:, c - QA + half, :], -DH_A ** -0.5
                elif c in (KA, KB):
                    dst = kT[:, c - KA + half, :]
                elif c in (GR, GR + 1):
                    dst = xr[:, 2 * (c - GR) + half, 0:T]
                elif c in QS:
                    dst, scale = qT[:, 2 * QS.index(c) + half, :], -DH_C ** -0.5
                elif c in (KS, KW):
                    dst = kT[:, (0 if c == KS else GROUPS) + half, :]
                elif c in (VS, VW):
                    dst = v[:, half, T * (c - VS):T * (c - VS + 1)]
                else:
                    dst = cmp_in[:, (0 if c == KC else 2) + half, :]
                eng.wait_ge(half_done, 2 * c + half + 1)
                nc.scalar.activation(dst, src, func, scale=scale).then_inc(unit_read, 1)

            def exps(k):
                eng.wait_ge(sneg_ready, k + 1)
                if k >= 2:
                    eng.wait_ge(pT_done, k - 1)
                for i, (a, n) in enumerate(((0, P), (P, 2 * P))):
                    e = nc.scalar.activation(prob[:, k % 2, a:a + n], sneg[:, k % 2, a:a + n], ACT.Exp,
                                             scale=-1.0, bias=mneg[:, 2 * k + i:2 * k + i + 1],
                                             accum_out=sums[:, 2 * k + i:2 * k + i + 1])
                e.then_inc(exp_done, 1)

            def probs_out(k):
                eng.wait_ge(pT_done, k + 1)
                if k == PROBS_TO_ACT:
                    eng.wait_ge(pT_ready, k)
                eng.wait_ge(pv_done, k - 1)
                nc.scalar.activation(pT[:, k % 2, :], acc[:, k % 2, 0:3 * P], ACT.Copy).then_inc(pT_ready, 1)

            def mlp(first, unit0):
                def relus(c, u, j4=0):
                    for s in range(2):
                        eng.wait_ge(half_done, j4 * 2 + (2 * c + s + 1))
                        if sq_of(u) >= 2:
                            eng.wait_ge(squared, j4 + (sq_of(u) + s - 1))
                        nc.scalar.activation(relu[:, s, :], wk[s][:, 0:T], ACT.Relu).then_inc(unit_read, 1)

                split(first + LEAD)
                relus(first, unit0)
                with eng.Fori(0, 7) as j:
                    for c in range(4):
                        n = first + 1 + c + LEAD
                        hi(n % RING, j * 16 + 16 * (n // RING + 1), j * 8 + 2 * (n - RING + 1))
                        if c % 2 == 0:
                            relus(first + 1 + c, unit0 + 2 + c, j * 4)
                split(first + 29 + LEAD)
                relus(first + 29, unit0 + 30)
                split(first + 30 + LEAD)
                split(first + 31 + LEAD)

            def o_parts(before, groups):
                for n, (i, half, bank) in enumerate(groups, before):
                    eng.wait_ge(oT_done, n + 1)
                    nc.scalar.activation(t_hi[:, 4 * half:4 * half + 4, i * P:(i + 1) * P],
                                         wk[bank][:, :].rearrange("p (k t) -> p k t", k=4),
                                         ACT.Copy).then_inc(oT_hi, 1)

            def load_sqrt():
                link(nc.scalar.activation(one_root[BUCKETS:BUCKETS + 1, :], table[BUCKETS:BUCKETS + 1, 0:1], ACT.Sqrt))

            def split_halves(c):
                half_0, half_1 = slice(0, CHUNK // 2), slice(CHUNK // 2, CHUNK)
                eng.wait_ge(first_landed[c], 16)
                nc.scalar.activation(w_hi[:, c, half_0], raw[:, c, half_0], ACT.Copy).then_inc(first_hi, 1)
                eng.wait_ge(landed[c], 16)
                nc.scalar.activation(w_hi[:, c, half_1], raw[:, c, half_1], ACT.Copy).then_inc(hi_ready, 1)

            eng.wait_ge(table_one, 1)
            load_sqrt()
            pre(0, 0)
            split_halves(0)
            turned(0, 0)
            pre(0, 1)
            split_halves(1)
            turned(0, 1)
            for c in range(V0, QB):
                for n in split_at(c):
                    split(n)
                if c == V0 + 1:
                    eng.wait_ge(sp_ready, 1)
                    nc.scalar.activation(sp[:, 1, :], sp[:, 0, :], ACT.Exp).then_inc(sp_ready, 1)
                for half in range(2):
                    evacuate(c, half)

            def lru(s):
                if s == 0:
                    eng.wait_ge(lru_gates_done, 1)
                    for w in range(2):
                        for t in range(CT):
                            nc.scalar.activation((rg, ig)[w][:, t, :], acc[:, t, w * T:(w + 1) * T],
                                                 ACT.Sigmoid, bias=lvec[:, t, 5 + w:6 + w]).then_inc(lru_gates, 1)
                if s in (1, 2):
                    if s == 1:
                        eng.wait_ge(lru_gates, 8)
                        eng.wait_ge(sp_ready, 3)
                        eng.wait_ge(ext_stored, 16)
                    for t in range(CT):
                        nc.scalar.activation((decay, mixb)[s - 1][:, t, :], rg[:, t, :], ACT.Exp,
                                             scale=sp[:, 3 + s, t:t + 1]).then_inc(decays, 1)
                if s == 3:
                    eng.wait_ge(decays, 2 * CT)
                    for t in range(CT):
                        nc.scalar.activation(rg[:, t, :], rg[:, t, :], ACT.Tanh, scale=sp[:, 3, t:t + 1])\
                          .then_inc(decays, 1)
                if s == 4:
                    eng.wait_ge(beta2_ready, 1)
                    nc.scalar.activation(mixb[:, :, :], mixb[:, :, :], ACT.Sqrt).then_inc(beta_ready, 1)

            lru(0)
            for k in range(JOBS0):
                for c, half in FILL0.get(k, []):
                    if half == 0:
                        split(c + LEAD)
                exps(k)
                if k > PROBS_TO_ACT:
                    probs_out(k - 1)
                for c, half in FILL0.get(k, []):
                    evacuate(c, half)
                lru(k + 1)
            probs_out(JOBS0 - 1)
            eng.wait_ge(unit_read, unit_of(GR + 1, 1) + 1)
            for a in range(2):
                gated = xr[:, 2 * a:2 * a + 2, 0:T]
                nc.scalar.activation(gated, gated, ACT.Gelu_apprx_tanh).then_inc(gelu_ready, 1)
            load_sqrt()
            o_parts(0, ((0, 0, 2), (1, 0, 3)))
            for c in range(OUT0, MLP0):
                split(c + LEAD)
            boundary(1)
            mlp(MLP0, UNIT_MLP0)
            boundary(2)
            for c in range(Q1, QS_B):
                for n in split_at(c):
                    split(n)
                for half in range(2):
                    evacuate(c, half)
                if c == QS_A:
                    eng.wait_ge(gates_done, 1)
                    nc.scalar.activation(gates_T, acc[0:6 * HEADS, 3, 0:T], ACT.Copy).then_inc(gates_read, 1)
            eng.wait_ge(gates_done, 2)
            nc.scalar.activation(gates[:, :, :], acc[:, 3, 0:TT * 3 * HEADS].rearrange("p (i n) -> p i n", i=TT),
                                 ACT.Sigmoid).then_inc(gates_ready, 1)

            def cmp_tanh(which):
                eng.wait_ge(gelu_cubic, which + 1)
                nc.scalar.activation(gelu_y, gelu_y, ACT.Tanh, scale=math.sqrt(2 / math.pi)).then_inc(gelu_tanh, 1)

            for k in range(JOBS0, JOBS):
                if k == KCMP_STEP + 4:
                    for i in range(TT):
                        n = cmp_keys(i)
                        eng.wait_ge(cs_ready, i + 1)
                        nc.scalar.activation(ce[:, i, :, 0:n], cs[:, i, :, 0:n], ACT.Exp, scale=-1.0)\
                          .then_inc(ce_exp, 1)
                for c, half in FILL1.get(k, []):
                    if half == 0:
                        split(c + LEAD)
                exps(k)
                if k in (KCMP_STEP + 1, VCMP_STEP + 1):
                    cmp_tanh(int(k != KCMP_STEP + 1))
                if k > JOBS0:
                    probs_out(k - 1)
                for c, half in FILL1.get(k, []):
                    if c < CMPK:
                        evacuate(c, half)
                    elif half == 1 and c in (CMPK + 3, CMPV + 3):
                        which = (c - CMPK) // 4
                        eng.wait_ge(half_done, 2 * c + 2)
                        nc.scalar.activation(hidden[0:2 * GROUPS * NC, which, :],
                                             wk[which][0:2 * GROUPS * NC, 0:CMP_HIDDEN], ACT.Copy)\
                          .then_inc(cmp_product, 1)
            probs_out(JOBS - 1)
            eng.wait_ge(kv_done, 2)
            for j in range(PER_GROUP):
                rows = slice(j * NPAD, (j + 1) * NPAD)
                nc.scalar.activation(vcmp[rows, :, j * P:(j + 1) * P],
                                     wk[1][rows, T:2 * T].rearrange("p (g d) -> p g d", g=GROUPS), ACT.Copy)\
                  .then_inc(kv_ready, 1)
            load_sqrt()
            o_parts(2, [(i, half, 2 * i + half) for i in range(TT) for half in range(2)])
            for c in range(OUT1, MLP1):
                split(c + LEAD)
            boundary(3)
            mlp(MLP1, UNIT_MLP1)
            for i in range(TT):
                post(4, i)

        @block.vector
        def _(eng):
            steps = [0]

            def link(ins):
                steps[0] += 1
                ins.then_inc(dve_step, 1)
                eng.wait_ge(dve_step, steps[0])

            def lo(c, n):
                eng.wait_ge(hi_ready, n + 1)
                nc.vector.tensor_tensor(w_lo[:, c, :], raw[:, c, :], w_hi[:, c, :].bitcast(F32),
                                        ALU.subtract).then_inc(lo_ready, 1)

            def split(n):
                if n < CHUNKS:
                    lo(n % RING, n)

            def scaled(b, i):
                k = TT * (b - 1) + i
                if i == 0:
                    eng.wait_ge(gain_landed[0], 16 * b)
                for half in range(2):
                    cols = slice(half * 512, (half + 1) * 512)
                    eng.wait_ge(post_sq, 2 * k + half + 1)
                    o = nc.vector.tensor_tensor(tok[:, i, cols], acc[:, 2 * i + half, :], gain[:, 0, cols], ALU.mult)
                link(o)

            def post(b, i):
                std = stat[:, 0, 3, TT * (b - 1) + i:TT * (b - 1) + i + 1]
                eng.wait_ge(post_std, TT * (b - 1) + i + 1)
                link(nc.vector.reciprocal(std, std))
                for half in range(2):
                    cols = slice(half * 512, (half + 1) * 512)
                    nc.vector.scalar_tensor_tensor(out=x[:, i, cols], in0=tok[:, i, cols], scalar=std,
                                                   in1=x[:, i, cols], op0=ALU.mult, op1=ALU.add).then_inc(x_ready, 1)

            def pre(b, i):
                k = TT * b + i
                std = stat[:, 1, 3, k:k + 1]
                if b == 0:
                    eng.wait_ge(x_landed[i], 16)
                else:
                    eng.wait_ge(x_ready, 2 * (TT * (b - 1) + i + 1))
                if i == 0:
                    eng.wait_ge(gain_landed[1], 16 * (b + 1))
                link(nc.vector.tensor_tensor(tok[:, i, :], x[:, i, :], gain[:, 1, :], ALU.mult))
                eng.wait_ge(pre_std, k + 1)
                link(nc.vector.reciprocal(std, std))
                nc.vector.tensor_scalar(diag[:, i, :], ident[:, :], std, None, ALU.mult).then_inc(xn_ready, 1)

            def turned(b, i):
                for half in range(2):
                    eng.wait_ge(tT_hi, 2 * (TT * b + i) + half + 1)
                    dst = slice(4 * half, 4 * half + 4), slice(i * P, (i + 1) * P)
                    nc.vector.tensor_tensor(t_lo[:, dst[0], dst[1]],
                                            turned_bank(b, i, half)[:, :].rearrange("p (k t) -> p k t", k=4),
                                            t_hi[:, dst[0], dst[1]].bitcast(F32), ALU.subtract)\
                      .then_inc(tT_ready, 1)

            def boundary(b):
                scaled(b, 0)
                post(b, 0)
                pre(b, 0)
                scaled(b, 1)
                if b in OPENS:
                    turned(b, 0)
                post(b, 1)
                pre(b, 1)
                if b not in OPENS:
                    turned(b, 0)
                turned(b, 1)

            def scores(k, i):
                head = job(k)[0]
                if i == 0:
                    eng.wait_ge(scores_done, k + 1)
                    if k >= 2:
                        eng.wait_ge(exp_done, k - 1)
                a, n = ((0, P), (P, 2 * P))[i]
                s = nc.vector.tensor_tensor_reduce(
                    out=sneg[:, k % 2, a:a + n], in0=wk[2 + k % 2][:, a:a + n],
                    in1=toep[:, head, a:a + n], scale=1.0, scalar=3.0e38, op0=ALU.add, op1=ALU.min,
                    accum_out=mneg[:, 2 * k + i:2 * k + i + 1])
                if i == 1:
                    s.then_inc(sneg_ready, 1)

            def probs_out(k):
                eng.wait_ge(pT_done, k + 1)
                if k >= 2:
                    eng.wait_ge(pv_done, k - 1)
                nc.vector.tensor_copy(pT[:, k % 2, :], acc[:, k % 2, 0:3 * P]).then_inc(pT_ready, 1)

            def coefs(k, part):
                head = job(k)[0]
                c2 = coef[:, 2 * k:2 * k + 2]
                if part == 0:
                    eng.wait_ge(exp_done, k + 1)
                    c = nc.vector.tensor_scalar(c2, sums[:, 2 * k:2 * k + 2], 1e-30, None, ALU.max)
                elif part == 1:
                    eng.wait_ge(coef_part, len(parts))
                    c = nc.vector.reciprocal(c2, c2)
                elif k >= JOBS0:
                    eng.wait_ge(coef_part, len(parts))
                    eng.wait_ge(gates_ready, 1)
                    c = nc.vector.tensor_tensor(c2, c2, gates[:, :, 3 * head + 1 + (k - JOBS0) // HEADS], ALU.mult)
                else:
                    return
                c.then_inc(coef_part, 1)
                parts.append(1)

            def head_out(k):
                head, d = job(k)[0:2]
                eng.wait_ge(coef_part, len(parts))
                eng.wait_ge(pv_done, k + 1)
                for i in range(TT):
                    dst = tok[:, i, head * d:(head + 1) * d]
                    src = acc[:, 2 + k % 2, i * T:i * T + d]
                    if k < 2 * HEADS:
                        o = nc.vector.tensor_scalar(dst, src, coef[:, 2 * k + i:2 * k + i + 1], None, ALU.mult)
                    else:
                        if i == 0:
                            eng.wait_ge(o_ready, k - HEADS + 1)
                        o = nc.vector.scalar_tensor_tensor(out=dst, in0=src, scalar=coef[:, 2 * k + i:2 * k + i + 1],
                                                           in1=dst, op0=ALU.mult, op1=ALU.add)
                o.then_inc(o_ready, 1)

            parts = []

            def pipeline(first, last, fill, extra):
                for s in range(first, last + 2):
                    for part in range(3):
                        if first <= s - 2 < last:
                            coefs(s - 2, part)
                        if s < last and part < 2:
                            scores(s, part)
                    if first <= s - 1 < min(last, PROBS_TO_ACT):
                        probs_out(s - 1)
                    if first <= s - 2 < last:
                        head_out(s - 2)
                    for c, half in fill.get(s, []):
                        if half == 0:
                            split(c + LEAD)
                    extra(s)

            def squares(slot, s, read, sq):
                eng.wait_ge(unit_read, read)
                if not isinstance(sq, int) or sq >= 2:
                    eng.wait_ge(h_ready, sq - 1)
                nc.vector.tensor_tensor(h_hi[:, slot, :], relu[:, s, :], relu[:, s, :], ALU.mult)
                nc.vector.tensor_tensor(square[:, s, :], relu[:, s, :], relu[:, s, :], ALU.mult)\
                  .then_inc(squared, 1)
                eng.wait_ge(squared, sq + 1)
                nc.vector.tensor_tensor(h_lo[:, slot, :], square[:, s, :], h_hi[:, slot, :].bitcast(F32),
                                        ALU.subtract).then_inc(h_ready, 1)

            def mlp(first, unit0):
                split(first + LEAD)
                for s in range(2):
                    squares(s, s, unit0 + s + 1, sq_of(unit0 + s))
                with eng.Fori(0, 7) as j:
                    for c in range(4):
                        n = first + 1 + c + LEAD
                        lo(n % RING, j * 4 + n)
                        if c % 2 == 0:
                            for s in range(2):
                                u = unit0 + 2 + c + s
                                squares((2 + c + s) % 4, s, j * 4 + (u + 1), j * 4 + sq_of(u))
                split(first + 29 + LEAD)
                for s in range(2):
                    u = unit0 + 30 + s
                    squares(2 + s, s, u + 1, sq_of(u))
                split(first + 30 + LEAD)
                split(first + 31 + LEAD)

            def o_parts(before, groups):
                for n, (i, half, bank) in enumerate(groups, before):
                    eng.wait_ge(oT_hi, n + 1)
                    dst = slice(4 * half, 4 * half + 4), slice(i * P, (i + 1) * P)
                    nc.vector.tensor_tensor(t_lo[:, dst[0], dst[1]],
                                            wk[bank][:, :].rearrange("p (k t) -> p k t", k=4),
                                            t_hi[:, dst[0], dst[1]].bitcast(F32), ALU.subtract)\
                      .then_inc(oT_ready, 1)

            nc.vector.memset(pT[:, 0, 0:P], 0.0).then_inc(zeros, 1)
            eng.wait_ge(small_landed, 16)
            def split_halves(c):
                for half, ready in ((slice(0, CHUNK // 2), first_hi), (slice(CHUNK // 2, CHUNK), hi_ready)):
                    eng.wait_ge(ready, c + 1)
                    o = nc.vector.tensor_tensor(w_lo[:, c, half], raw[:, c, half], w_hi[:, c, half].bitcast(F32),
                                                ALU.subtract)
                o.then_inc(lo_ready, 1)

            pre(0, 0)
            split_halves(0)
            turned(0, 0)
            pre(0, 1)
            split_halves(1)
            turned(0, 1)
            for c in range(V0, QB):
                for n in split_at(c):
                    split(n)
                if c == V0:
                    lam = lvec[:, :, 7]
                    eng.wait_ge(lru_landed, 32)
                    nc.vector.scalar_tensor_tensor(out=sp[:, 0, :], in0=lam, scalar=-1.0, in1=lam, op0=ALU.mult,
                                                   op1=ALU.min).then_inc(sp_ready, 1)
                if c == V0 + 1:
                    eng.wait_ge(ext_done, 1)
                    nc.vector.tensor_copy(ext, acc[0:HEADS, 3, 0:3 * P - 1]).then_inc(ext_read, 1)
                if c == XR:
                    eng.wait_ge(sp_ready, 2)
                    link(nc.vector.tensor_scalar(sp[:, 2, :], sp[:, 1, :], 2.0, None, ALU.add))
                    link(nc.vector.reciprocal(sp[:, 2, :], sp[:, 2, :]))
                    link(nc.vector.tensor_tensor(sp[:, 1, :], sp[:, 1, :], sp[:, 2, :], ALU.mult))
                    link(nc.vector.tensor_tensor(sp[:, 2, :], sp[:, 1, :], sp[:, 1, :], ALU.mult))
                    link(nc.vector.memset(sp[:, 3, :], 1.0 / 17))
                    for odd in range(15, 0, -2):
                        link(nc.vector.tensor_tensor(sp[:, 3, :], sp[:, 3, :], sp[:, 2, :], ALU.mult))
                        link(nc.vector.tensor_scalar(sp[:, 3, :], sp[:, 3, :], 1.0 / odd, None, ALU.add))
                    link(nc.vector.tensor_tensor(sp[:, 3, :], sp[:, 3, :], sp[:, 1, :], ALU.mult))
                    link(nc.vector.tensor_scalar(sp[:, 3, :], sp[:, 3, :], 2.0 * LRU_C, None, ALU.mult))
                    link(nc.vector.tensor_scalar(sp[:, 2, :], lam, -LRU_C, 0.0, ALU.mult, ALU.max))
                    link(nc.vector.tensor_tensor(sp[:, 3, :], sp[:, 3, :], sp[:, 2, :], ALU.add))
                    nc.vector.tensor_scalar(sp[:, 4, :], sp[:, 3, :], -1.0, None, ALU.mult)
                    nc.vector.tensor_scalar(sp[:, 5, :], sp[:, 3, :], -2.0, None, ALU.mult).then_inc(sp_ready, 1)
                if c == QA:
                    eng.wait_ge(unit_read, unit_of(XR + 1, 1) + 1)
                    for tap in range(TAPS):
                        for t in range(CT):
                            if tap == 0:
                                o = nc.vector.tensor_scalar(xc_tile(t), xr[:, t, 0:T], lvec[:, t, 0:1],
                                                            lvec[:, t, 4:5], ALU.mult, ALU.add)
                            else:
                                o = nc.vector.scalar_tensor_tensor(out=xc_tile(t), in0=xr[:, t, tap:tap + T],
                                                                   scalar=lvec[:, t, tap:tap + 1], in1=xc_tile(t),
                                                                   op0=ALU.mult, op1=ALU.add)
                        if tap < TAPS - 1:
                            link(o)
                    o.then_inc(xc_ready, 1)

            def recurrence(s):
                if s == 1:
                    eng.wait_ge(lru_gates, 8)
                    link(nc.vector.tensor_tensor(pairs(ig), pairs(ig), xc, ALU.mult))
                elif s == 3:
                    eng.wait_ge(decays, 3 * CT)
                    nc.vector.scalar_tensor_tensor(out=mixb[:, :, :], in0=mixb[:, :, :], scalar=1.0,
                                                   in1=rg[:, :, :], op0=ALU.add, op1=ALU.mult)\
                      .then_inc(beta2_ready, 1)
                elif s == 4:
                    eng.wait_ge(beta_ready, 1)
                    link(nc.vector.tensor_tensor(ig[:, :, :], ig[:, :, :], mixb[:, :, :], ALU.mult))
                elif 5 <= s < 5 + CT // 2:
                    for t in (2 * (s - 5), 2 * (s - 5) + 1):
                        o = nc.vector.tensor_tensor_scan(xc_tile(t), decay[:, t, :], ig[:, t, :], 0.0,
                                                         ALU.mult, ALU.add)
                    link(o)

            eng.wait_ge(toep_landed, 32)
            pipeline(0, JOBS0, FILL0, recurrence)
            for a in range(2):
                tiles, feats = slice(2 * a, 2 * a + 2), slice(CT + 2 * a, CT + 2 * a + 2)
                eng.wait_ge(gelu_ready, a + 1)
                link(nc.vector.tensor_tensor(rg[:, tiles, :], xc[:, a, :].rearrange("p (b t) -> p b t", b=2),
                                             xr[:, tiles, 0:T], ALU.mult))
                link(nc.vector.tensor_copy(t_hi[:, feats, :], rg[:, tiles, :]))
                nc.vector.tensor_tensor(t_lo[:, feats, :], rg[:, tiles, :], t_hi[:, feats, :].bitcast(F32),
                                        ALU.subtract).then_inc(ob_ready, 1)
            o_parts(0, ((0, 0, 2), (1, 0, 3)))
            for c in range(OUT0, MLP0):
                split(c + LEAD)
            boundary(1)
            mlp(MLP0, UNIT_MLP0)
            boundary(2)
            eng.wait_ge(nsa_landed, 48)
            n = 3 * HEADS
            nc.vector.tensor_tensor(gates_sum, ident[0:2 * n, 0:n], ident[0:2 * n, n:2 * n], ALU.add)
            link(nc.vector.tensor_copy(gw_parts[:, :, 0, :], gw))
            nc.vector.tensor_tensor(gw_parts[:, :, 1, :], gw, gw_parts[:, :, 0, :].bitcast(F32), ALU.subtract)\
              .then_inc(gw_ready, 1)
            for c in range(Q1, QS_B):
                for n in split_at(c):
                    split(n)

            def flatten(which):
                src = cmp_in[:, 2 * which:2 * which + 2, :]
                blocks_f32 = ig[:, :, :].rearrange("p a t -> p (a t)")[:, 0:CMP_LEN * GROUPS * NC]\
                    .rearrange("p (l g n) -> p l g n", l=CMP_LEN, g=GROUPS)
                eng.wait_ge(unit_read, unit_of((KC, VC)[which], 1) + 1)
                if which == 1:
                    eng.wait_ge(flat_ready, 1)
                for g in range(GROUPS):
                    s = src[:, g, :]
                    blocks = bass.AP(s.tensor, s.offset, [list(s.ap[0]), [1, CMP_LEN], [CMP_STRIDE, NC]])
                    p = pos[:, which, :]
                    emb = bass.AP(p.tensor, p.offset, [list(p.ap[0]), [1, CMP_LEN], [0, NC]])
                    o = nc.vector.tensor_tensor(blocks_f32[:, :, g, :], blocks, emb, ALU.add)
                link(o)
                flat1 = blocks_f32.rearrange("p l g n -> p l (g n)")
                link(nc.vector.tensor_copy(flat[:, which, :, 0, :], flat1))
                nc.vector.tensor_tensor(flat[:, which, :, 1, :], flat1, flat[:, which, :, 0, :].bitcast(F32),
                                        ALU.subtract).then_inc(flat_ready, 1)

            def cmp_scores(i):
                n = cmp_keys(i)
                s_i = cs[:, i, :, 0:n]
                if i == 0:
                    eng.wait_ge(cs_done, 1)
                link(nc.vector.tensor_tensor(s_i, cmp_scored[:, i, :, 0:n], cmp_bias[i], ALU.add))
                link(nc.vector.tensor_reduce(cst[:, i, 0, :], s_i, AX.X, ALU.min))
                m = cst[:, i, 0, :]
                nc.vector.tensor_tensor(s_i, s_i, bass.AP(m.tensor, m.offset, [list(m.ap[0]), [1, HEADS], [0, n]]),
                                        ALU.subtract).then_inc(cs_ready, 1)

            def cmp_probs():
                def both(f):
                    for i in range(TT):
                        o = f(i, ce[:, i, :, 0:cmp_keys(i)], cst[:, i, 1, :])
                    return o

                eng.wait_ge(ce_exp, TT)
                link(both(lambda i, e, c: nc.vector.scalar_tensor_tensor(
                    out=e, in0=cmp_bias[i], scalar=MASKED / 10, in1=e, op0=ALU.is_lt, op1=ALU.mult)))
                link(both(lambda i, e, c: nc.vector.tensor_reduce(c, e, AX.X, ALU.add)))
                link(both(lambda i, e, c: nc.vector.tensor_scalar(c, c, 1e-30, None, ALU.max)))
                link(both(lambda i, e, c: nc.vector.reciprocal(c, c)))
                link(both(lambda i, e, c: nc.vector.tensor_tensor(c, c, gates[:, i, 0::3], ALU.mult)))
                both(lambda i, e, c: nc.vector.tensor_tensor(
                    e, e, bass.AP(c.tensor, c.offset, [list(c.ap[0]), [1, HEADS], [0, cmp_keys(i)]]), ALU.mult))\
                    .then_inc(ce_ready, 1)

            def cmp_out(i):
                eng.wait_ge(o_ready, JOBS)
                for g in range(GROUPS):
                    eng.wait_ge(cpv_done, GROUPS * i + g + 1)
                    dst = tok[:, i, g * 512:(g + 1) * 512]
                    nc.vector.tensor_tensor(dst, wk[2 * i + g][:, :], dst, ALU.add).then_inc(oc_ready, 1)

            def gelu_in(which):
                eng.wait_ge(hT_done, which + 1)
                link(nc.vector.tensor_copy(gelu_x, wk[which][:, 0:2 * NPAD].rearrange("p (t n) -> p t n", t=2)
                                           [:, :, 0:GROUPS * NC]))
                link(nc.vector.tensor_tensor(gelu_y, gelu_x, gelu_x, ALU.mult))
                link(nc.vector.tensor_scalar(gelu_y, gelu_y, 0.044715, 1.0, ALU.mult, ALU.add))
                nc.vector.tensor_tensor(gelu_y, gelu_y, gelu_x, ALU.mult).then_inc(gelu_cubic, 1)

            def gelu_out(which):
                eng.wait_ge(gelu_tanh, which + 1)
                link(nc.vector.tensor_scalar(gelu_y, gelu_y, 1.0, 0.5, ALU.add, ALU.mult))
                for t in range(2):
                    a, b = gelu_x[:, t, :], gelu_y[:, t, :]
                    if which == 0:
                        o = nc.vector.tensor_tensor(hkT[:, t, :], a, b, ALU.mult)
                    else:
                        a, b = (bass.AP(f.tensor, f.offset, [list(f.ap[0]), [NC, GROUPS], [0, PER_GROUP], [1, NC]])
                                for f in (a, b))
                        o = nc.vector.tensor_tensor(hvT[:, t, :, :, 0:NC], a, b, ALU.mult)
                o.then_inc(hT_ready, 1)

            cmp_scored = wk[0][:, 0:T].rearrange("p (i h n) -> p i h n", i=TT, h=HEADS)
            cmp_bias = [toep[:, :, CMP_LEN - 1:P:CMP_STRIDE], toep[:, :, P + CMP_LEN - 1::CMP_STRIDE]]
            flattened = next(s for s, units in FILL1.items() if (VC, 1) in units)

            def extra(s):
                units = FILL1.get(s, [])
                for which in range(2):
                    if ((KC, VC)[which], 1) in units:
                        flatten(which)
                if s == flattened + 1:
                    n = GROUPS * NC
                    nc.vector.tensor_tensor(halves_sum, ident[0:2 * n, 0:n], ident[0:2 * n, n:2 * n], ALU.add)
                    link(nc.vector.memset(ig[:, :, :], 0.0))
                if s == KCMP_STEP:
                    gelu_in(0)
                if s == KCMP_STEP + 1:
                    gelu_out(0)
                if s == KCMP_STEP + 2:
                    eng.wait_ge(kv_done, 1)
                    nc.vector.tensor_copy(kcmp[:, :], wk[0][:, P:P + GROUPS * NC]).then_inc(kv_ready, 1)
                if s == KCMP_STEP + 3:
                    for i in range(TT):
                        cmp_scores(i)
                if s == VCMP_STEP:
                    gelu_in(1)
                if s == VCMP_STEP + 1:
                    gelu_out(1)
                if s == KCMP_STEP + 5:
                    cmp_probs()
                if s == JOBS:
                    eng.wait_ge(cpT_done, 1)
                    nc.vector.tensor_copy(cpT, wk[0][:, :].rearrange("p (i g t) -> p i g t", i=TT, g=GROUPS))\
                      .then_inc(cpT_ready, 1)

            link(nc.vector.memset(mixb[:, :, :], 0.0))
            pipeline(JOBS0, JOBS, FILL1, extra)
            for i in range(TT):
                cmp_out(i)
            o_parts(2, [(i, half, 2 * i + half) for i in range(TT) for half in range(2)])
            for c in range(OUT1, MLP1):
                split(c + LEAD)
            boundary(3)
            mlp(MLP1, UNIT_MLP1)
            for i in range(TT):
                scaled(4, i)
                post(4, i)

        @block.tensor
        def _(eng):
            PASSES = ((0, 0), (1, 0), (0, 1))
            t_part, w_part, h_part = (t_hi, t_lo), (w_hi, w_lo), (h_hi, h_lo)

            def group(psum, lhsT, rhs, n, before=lambda k: None):
                for k in range(n):
                    before(k)
                    for a, w in PASSES:
                        m = nc.tensor.matmul(psum, lhsT(k, a, w), rhs(k, a, w), start=k == 0 and (a, w) == (0, 0),
                                             stop=k == n - 1 and (a, w) == PASSES[-1])
                return m

            def weights(c, part):
                return w_part[part][:, c, :].rearrange("p (k n) -> p k n", k=KT)

            def up_unit(slot, half, bank, before=lambda k: None):
                return group(wk[bank][:, 0:T],
                             lambda k, a, w: weights(slot, w)[:, k, half * P:(half + 1) * P],
                             lambda k, a, w: t_part[a][:, k, :], KT, before)

            def unit(c, half):
                u = unit_of(c, half)
                if half == 0:
                    eng.wait_ge(lo_ready, c + 1)
                if u >= 2:
                    eng.wait_ge(unit_read, u - 1)
                up_unit(c % RING, half, half).then_inc(half_done, 1)

            def chunk(c):
                for half in range(2):
                    unit(c, half)

            def product(i, half, slot, r0, part, first=False, last=False):
                for r in range(2):
                    for a, w in PASSES:
                        m = nc.tensor.matmul(
                            acc[:, 2 * i + half, :],
                            part[a][:, r0 + r, i * P:(i + 1) * P],
                            w_part[w][:, slot, r * D + half * 512:r * D + half * 512 + 512],
                            start=first and r == 0 and (a, w) == (0, 0),
                            stop=last and r == 1 and (a, w) == PASSES[-1])
                return m

            def products(i, slot, r0, part, first):
                product(i, 0, slot, r0, part, first)
                return product(i, 1, slot, r0, part, first)

            def down(slot, r0, part, first):
                for i in range(TT):
                    products(i, slot, r0, part, first).then_inc(half_done, 1)

            def closing(c, r0, part, ready=lambda n: None):
                for i in range(TT):
                    for half in range(2):
                        for n in range(2):
                            if (i, half) == (0, 0):
                                eng.wait_ge(lo_ready, c + n + 1)
                                ready(n)
                            m = product(i, half, (c + n) % RING, r0[n], part, last=n == 1)
                        if (i, half) != (1, 1):
                            m.then_inc(sums_done, 1)
                m.then_inc(half_done, 4)

            def out_chunk(c, r0, first):
                eng.wait_ge(lo_ready, c + 1)
                down(c % RING, r0, t_part, first)

            def keep_clock(n, operand, bank):
                for _ in range(n):
                    nc.tensor.matmul(bank[:, 0:P], operand, operand, start=True, stop=True)

            def turned(b, i):
                eng.wait_ge(xn_ready, TT * b + i + 1)
                for half in range(2):
                    if i == 1 and b in OPENS:
                        eng.wait_ge(tT_ready, 2 * TT * b + half + 1)
                    for q in range(4):
                        k = 4 * half + q
                        m = nc.tensor.matmul(turned_bank(b, i, half)[:, q * P:(q + 1) * P], tok[:, i, k * P:(k + 1) * P],
                                             diag[:, i, :], start=True, stop=True)
                    m.then_inc(xT_done, 1)

            def tile_in(b, i):
                def before(k):
                    if k % 4 == 0:
                        eng.wait_ge(tT_ready, 2 * (TT * b + i) + k // 4 + 1)
                return before

            def opening(b):
                c0 = OPENS[b]
                turned(b, 0)
                for i in range(TT):
                    for c in (c0, c0 + 1):
                        if (c, i) == (c0 + 1, 0) and b == 0:
                            turned(b, 1)
                        eng.wait_ge(lo_ready, c + 1)

                        def before(k):
                            tile_in(b, i)(k)
                            if b > 0 and (c, i, k) == (c0 + 1, 0, KT // 2):
                                turned(b, 1)

                        m = group(unit_bank(c, i)[:, 0:T],
                                  lambda k, a, w: t_part[a][:, k, i * P:(i + 1) * P],
                                  lambda k, a, w: weights(c % RING, w)[:, k, :], KT, before)
                        if (c, i) != (c0 + 1, 0):
                            m.then_inc(half_done, 1 if (c, i) != (c0 + 1, 1) else 2)

            def transposed_o(groups, ready):
                for i, half, bank in groups:
                    ready(i, half)
                    for q in range(4):
                        k = 4 * half + q
                        m = nc.tensor.transpose(wk[bank][:, q * P:(q + 1) * P], tok[:, i, k * P:(k + 1) * P],
                                                ident[:, :])
                    m.then_inc(oT_done, 1)

            def scores(k):
                head, d, p0, qs, ks, v0 = job(k)
                eng.wait_ge(unit_read, unit_of(last_chunk(k), 1) + 1)
                if k >= 2:
                    eng.wait_ge(sneg_ready, k - 1)
                bank = wk[2 + k % 2]
                q, kk = qT[p0:p0 + d, qs, :], kT[p0:p0 + d, ks, :]
                nc.tensor.matmul(bank[:, 0:P], q[:, 0:P], kk[:, 0:P], start=True, stop=True)
                nc.tensor.matmul(bank[:, P:3 * P], q[:, P:T], kk, start=True, stop=True).then_inc(scores_done, 1)

            def turn(k):
                eng.wait_ge(exp_done, k + 1)
                if k >= 2:
                    eng.wait_ge(pT_ready, k - 1)
                for n in range(3):
                    m = nc.tensor.transpose(acc[:, k % 2, n * P:(n + 1) * P], prob[:, k % 2, n * P:(n + 1) * P],
                                            ident[:, :])
                m.then_inc(pT_done, 1)

            def values(k):
                head, d, p0, qs, ks, v0 = job(k)
                eng.wait_ge(pT_ready, k + 1)
                if k >= 2:
                    eng.wait_ge(o_ready, k - 1)
                bank = acc[:, 2 + k % 2, :]
                pt = pT[:, k % 2, :]
                nc.tensor.matmul(bank[:, 0:d], pt[:, 0:P], v[:, 0, v0:v0 + d], start=True, stop=True)
                nc.tensor.matmul(bank[:, T:T + d], pt[:, P:2 * P], v[:, 0, v0:v0 + d], start=True, stop=False)
                nc.tensor.matmul(bank[:, T:T + d], pt[:, 2 * P:3 * P], v[:, 1, v0:v0 + d], start=False, stop=True)\
                  .then_inc(pv_done, 1)

            def pipeline(first, last, fill, filler, extra):
                for s in range(first, last + 2):
                    if s < last:
                        scores(s)
                    if first <= s - 1 < last:
                        turn(s - 1)
                    if first <= s - 2 < last:
                        values(s - 2)
                    for c, half in fill.get(s, []):
                        filler(c, half)
                    extra(s)

            def cmp_unit(c, half):
                if c < CMPK:
                    return unit(c, half)
                which, at = divmod(c - CMPK, 4)
                if half == 0:
                    eng.wait_ge(lo_ready, c + 1)
                if at == 0 and half == 0:
                    eng.wait_ge(flat_ready, which + 1)
                    eng.wait_ge(unit_read, unit_of(KW, 1) + 1)
                for q in range(4):
                    place = 8 * at + 4 * half + q
                    for w in range(2):
                        m = nc.tensor.matmul(wk[which][0:2 * GROUPS * NC, 0:CMP_HIDDEN],
                                             flat[:, which, place, :, :].rearrange("p a n -> p (a n)"),
                                             weights(c % RING, w)[:, 4 * half + q, :],
                                             start=(place, w) == (0, 0), stop=(place, w) == (CMP_LEN - 1, 1))
                m.then_inc(half_done, 1)

            def hidden_turned(which):
                eng.wait_ge(cmp_product, which + 1)
                for t in range(2):
                    m = nc.tensor.matmul(wk[which][:, t * NPAD:t * NPAD + GROUPS * NC],
                                         hidden[0:2 * GROUPS * NC, which, t * P:(t + 1) * P], halves_sum,
                                         start=True, stop=True)
                m.then_inc(hT_done, 1)

            def compressed(which):
                eng.wait_ge(hT_ready, which + 1)
                if which == 0:
                    for t in range(2):
                        m = nc.tensor.matmul(wk[0][:, P:P + GROUPS * NC], w2[:, 0, t, :], hkT[:, t, :],
                                             start=t == 0, stop=t == 1)
                else:
                    for g in range(GROUPS):
                        for t in range(2):
                            m = nc.tensor.matmul(wk[1][:, T + g * P:T + (g + 1) * P],
                                                 hvT[:, t, g, :, :].rearrange("p j n -> p (j n)"),
                                                 w2[:, 1, t, :], start=t == 0, stop=t == 1)
                m.then_inc(kv_done, 1)

            def mlp(b, first, unit0):
                def up(c, u, slot, before=lambda k: None):
                    eng.wait_ge(lo_ready, c + 1)
                    for s in range(2):
                        eng.wait_ge(unit_read, u + (s - 1))
                        up_unit(slot, s, s, before).then_inc(half_done, 1)

                def dn(c, slot, h0, ready, first_sum):
                    eng.wait_ge(lo_ready, c + 1)
                    eng.wait_ge(h_ready, ready)
                    down(slot, h0, h_part, first_sum)

                def body(j4, first_sum):
                    for c in range(0, 4, 2):
                        n = first + 1 + c
                        up(j4 + n, j4 + (unit0 + 2 + c), n % RING)
                        dn(j4 + (n + 1), (n + 1) % RING, c, j4 + (sq_of(unit0) + c + 2), first_sum and c == 0)

                up(first, unit0, first % RING, tile_in(b, 1))
                body(0, True)
                with eng.Fori(1, 7) as j:
                    body(j * 4, False)
                up(first + 29, unit0 + 30, (first + 29) % RING)
                closing(first + 30, (0, 2), h_part, lambda n: eng.wait_ge(h_ready, sq_of(unit0) + 30 + 2 * n))

            eng.wait_ge(zeros, 1)
            keep_clock(18, pT[:, 0, 0:P], acc[:, 0, :])
            eng.wait_ge(small_landed, 16)
            opening(0)
            eng.wait_ge(table_landed, 32)
            nc.tensor.matmul(acc[0:HEADS, 3, 0:3 * P - 1], table[:, :], select, start=True, stop=True)\
              .then_inc(ext_done, 1)
            for c in range(XR, QB):
                chunk(c)
            eng.wait_ge(xc_ready, 1)
            eng.wait_ge(lru_landed, 32)
            for t in range(CT):
                for w in range(2):
                    m = nc.tensor.matmul(acc[:, t, w * T:(w + 1) * T], lgate[:, w, t, :], xc_tile(t),
                                         start=True, stop=True)
            m.then_inc(lru_gates_done, 1)

            def extra0(s):
                if s == 0:
                    eng.wait_ge(lru_gates, 8)
                if s >= JOBS0:
                    eng.wait_ge(unit_read, unit_of(GR + 1, 1) + 1)
                    keep_clock(3, ident[:, :], wk[0])

            pipeline(0, JOBS0, FILL0, unit, extra0)
            transposed_o(((0, 0, 2), (1, 0, 3)), lambda i, half: eng.wait_ge(o_ready, JOBS0))
            keep_clock(4, ident[:, :], wk[0])
            eng.wait_ge(ob_ready, 1)
            out_chunk(OUT0, CT, True)
            eng.wait_ge(ob_ready, 2)
            out_chunk(OUT0 + 1, CT + 2, False)
            eng.wait_ge(oT_ready, 2)
            closing(OUT0 + 2, (0, 2), t_part)
            turned(1, 0)
            keep_clock(12, ident[:, :], acc[:, 0, :])
            turned(1, 1)
            mlp(1, MLP0, UNIT_MLP0)
            opening(2)
            chunk(QS_A)
            eng.wait_ge(gw_ready, 1)
            for k in range(KT):
                for a in range(2):
                    m = nc.tensor.matmul(acc[0:6 * HEADS, 3, 0:T], gw_parts[:, k, :, :].rearrange("p a n -> p (a n)"),
                                         t_part[a][:, k, :], start=(k, a) == (0, 0), stop=(k, a) == (KT - 1, 1))
            m.then_inc(gates_done, 1)
            chunk(KS)
            eng.wait_ge(gates_read, 1)
            for i in range(TT):
                m = nc.tensor.matmul(acc[:, 3, i * 3 * HEADS:(i + 1) * 3 * HEADS], gates_T[:, i * P:(i + 1) * P],
                                     gates_sum, start=True, stop=True)
            m.then_inc(gates_done, 1)

            def extra(s):
                if s == JOBS0:
                    eng.wait_ge(gates_ready, 1)
                if s == KCMP_STEP:
                    hidden_turned(0)
                if s == KCMP_STEP + 2:
                    compressed(0)
                if s == KCMP_STEP + 3:
                    eng.wait_ge(kv_ready, 1)
                    for i in range(TT):
                        for h in range(HEADS):
                            g, at = h // PER_GROUP, (i * HEADS + h) * 16
                            m = nc.tensor.matmul(wk[0][:, at:at + NC], qT[:, h, i * P:(i + 1) * P],
                                                 kcmp[:, g * NC:(g + 1) * NC], start=True, stop=True)
                    m.then_inc(cs_done, 1)
                if s == VCMP_STEP:
                    hidden_turned(1)
                if s == JOBS:
                    compressed(1)
                    eng.wait_ge(ce_ready, 1)
                    for i in range(TT):
                        for g in range(GROUPS):
                            at = (i * GROUPS + g) * P
                            m = nc.tensor.transpose(wk[0][:, at:at + P], ce[:, i, g * PER_GROUP:(g + 1) * PER_GROUP, :]
                                                    .rearrange("p h n -> p (h n)"), ident[:, :])
                    m.then_inc(cpT_done, 1)

            pipeline(JOBS0, JOBS, FILL1, cmp_unit, extra)
            eng.wait_ge(kv_ready, 1 + PER_GROUP)
            eng.wait_ge(cpT_ready, 1)
            eng.wait_ge(sneg_ready, JOBS)
            for i in range(TT):
                for g in range(GROUPS):
                    nc.tensor.matmul(wk[2 * i + g][:, :], cpT[:, i, g, :], vcmp[:, g, :], start=True, stop=True)\
                      .then_inc(cpv_done, 1)
            transposed_o([(i, half, 2 * i + half) for i in range(TT) for half in range(2)],
                         lambda i, half: eng.wait_ge(oc_ready, GROUPS * i + half + 1))
            eng.wait_ge(oT_ready, 4)
            eng.wait_ge(lo_ready, OUT1 + 1)
            products(0, OUT1 % RING, 0, t_part, True).then_inc(half_done, 1)
            eng.wait_ge(oT_ready, 6)
            products(1, OUT1 % RING, 0, t_part, True).then_inc(half_done, 1)
            out_chunk(OUT1 + 1, 2, False)
            closing(OUT1 + 2, (4, 6), t_part)
            turned(3, 0)
            keep_clock(12, ident[:, :], acc[:, 0, :])
            turned(3, 1)
            mlp(3, MLP1, UNIT_MLP1)


def bucket_rows():
    exact = BUCKETS // 2
    rows = np.zeros((BUCKETS + 1, 3 * P - 1), np.float32)
    for j in range(3 * P - 1):
        n = T - 1 - j
        if n < 0:
            rows[BUCKETS, j] = MASKED
        elif n < exact:
            rows[n, j] = -1.0
        else:
            large = exact + int(math.log(n / exact) / math.log(128 / exact) * (BUCKETS - exact))
            rows[min(large, BUCKETS - 1), j] = -1.0
    return rows


def columns(w):
    k, n = w.shape
    return w.reshape(k // P, P, n // 256, 256).transpose(2, 1, 0, 3).reshape(n // 256, P, -1)


def rows(w):
    return w.reshape(-1, 2, P, D).transpose(0, 2, 1, 3).reshape(-1, P, 2 * D)


def places(w):
    return w.reshape(-1, 8, P, CMP_HIDDEN).transpose(0, 2, 1, 3).reshape(-1, P, CHUNK)


def kernel(**inputs):
    import concourse.bacc as bacc
    from concourse.bass_utils import run_bass_kernel_spmd

    a = {k: np.asarray(v) for k, v in inputs.items()}
    dq = HEADS * DH_A
    w_in, c_in, w_o = a["ab_w_in"][0], a["c_w_in"][0], a["ab_w_out"][0]
    part = lambda lo, n: columns(w_in[:, lo:lo + n])

    def mlp_stream(layer):
        up, down = columns(a["w_up"][layer]), rows(a["w_down"][layer])
        order = [up[0]]
        for c in range(15):
            order += [up[c + 1], down[c]]
        return np.stack(order + [down[15]])

    def q_part(j):
        return columns(c_in[:, j * GROUPS * DH_C:(j + 1) * GROUPS * DH_C])

    def c_part(j):
        lo = HEADS * DH_C + j * GROUPS * DH_C
        return columns(c_in[:, lo:lo + GROUPS * DH_C])

    stream = np.concatenate([
        part(2 * dq, dq), part(3 * dq, W), part(0, T), part(dq, T), part(T, T), part(dq + T, T), part(3 * dq + W, W),
        rows(w_o[dq:]), rows(w_o[:dq]), mlp_stream(0),
        c_part(3), c_part(5), q_part(0), c_part(2), q_part(1), c_part(0), q_part(2), c_part(1), q_part(3), c_part(4),
        places(a["c_cmp_k_w1"][0]), places(a["c_cmp_v_w1"][0]), rows(a["c_w_out"][0]), mlp_stream(1)])
    assert stream.shape == (CHUNKS, P, CHUNK)
    gains = np.stack([a[n][layer] for layer in range(2)
                      for n in ("norm_mix_pre", "norm_mix_post", "norm_mlp_pre", "norm_mlp_post")])
    lru_vec = np.stack([*a["ab_conv_w"][0], a["ab_conv_b"][0], a["ab_b_rg"][0], a["ab_b_ig"][0],
                        a["ab_lru_lambda"][0]], axis=1).reshape(CT, P, 8).transpose(1, 0, 2)
    lru_gate = np.zeros((P, 2, CT, P), np.float32)
    for w, name in enumerate(("ab_w_rg", "ab_w_ig")):
        for b in range(8):
            r = (b % 2) * 64
            lru_gate[r:r + 64, w, b // 2, r:r + 64] = a[name][0, b]
    fed = {
        "x_in": a["x"][0], "w_stream": stream, "gains": gains, "lru_vec": lru_vec, "lru_gate": lru_gate,
        "rel_bias": a["rel_bias"], "bias_select": bucket_rows(), "ident_in": np.eye(P, dtype=np.float32),
        "gate_w": c_in[:, -3 * HEADS:].reshape(KT, P, 3 * HEADS).transpose(1, 0, 2),
        "cmp_pos": np.stack([a["c_cmp_pos_k"][0].T, a["c_cmp_pos_v"][0].T], axis=1),
        "cmp_w2": np.stack([a[n][0].reshape(2, P, P).transpose(1, 0, 2) for n in ("c_cmp_k_w2", "c_cmp_v_w2")],
                           axis=1),
    }
    nc = bacc.Bacc("TRN2", target_bir_lowering=False, num_devices=1)
    arrays, args = {}, []
    for name, value in fed.items():
        value = np.ascontiguousarray(value)
        arrays[name] = value
        args.append(nc.dram_tensor(name, value.shape, mybir.dt.from_np(value.dtype), kind="ExternalInput").ap())
    out = nc.dram_tensor("out", [T, D], F32, kind="ExternalOutput").ap()
    trunk(nc, *args, out)
    r = run_bass_kernel_spmd(nc, [arrays], core_ids=[0])
    return r.results[0]["out"].reshape(1, T, D)
```
